# Optimizing a Trainium2 kernel written in Bass

```python
import jax, jax.numpy as jnp
from jax import lax
import numpy as np
import math

D_MODEL = 1024
BATCH = 1
SEQ = 512
DEPTH = 2

N_MIXERS = 2
NORM_EPS = 1e-6

GDN_K_HEADS = 8
GDN_V_HEADS = 16
GDN_HEAD_K = 128
GDN_HEAD_V = 128
GDN_CONV = 4
GDN_CHUNK = 64
GDN_QK = GDN_K_HEADS * GDN_HEAD_K
GDN_V = GDN_V_HEADS * GDN_HEAD_V
GDN_CONV_DIM = 2 * GDN_QK + GDN_V
GDN_PROJ = GDN_CONV_DIM + GDN_V + 2 * GDN_V_HEADS

SC_WIDTH = 2 * D_MODEL
SC_CONV = 3
SC_PROJ = 4 * SC_WIDTH

N_GDN_LAYERS = (DEPTH + 1) // 2
N_SC_LAYERS = DEPTH // 2


def rms_norm(x, w):
    xf = x.astype(jnp.float32)
    y = xf * lax.rsqrt(jnp.mean(xf * xf, axis=-1, keepdims=True) + NORM_EPS)
    return y * w.astype(jnp.float32)

def l2_normalize(x):
    xf = x.astype(jnp.float32)
    return xf * lax.rsqrt(jnp.sum(xf * xf, axis=-1, keepdims=True) + NORM_EPS)

def causal_depthwise_conv(x, w):
    width = w.shape[0]
    t = x.shape[1]
    xp = jnp.pad(x, ((0, 0), (width - 1, 0), (0, 0)))
    return sum(w[j] * xp[:, j:j + t] for j in range(width))

def chunked_gated_delta_rule(q, k, v, g, beta):
    b, h, t, dk = q.shape
    dv = v.shape[-1]
    c = GDN_CHUNK
    n = t // c
    q = q * (dk ** -0.5)
    kb = k * beta[..., None]
    vb = v * beta[..., None]
    q, k, kb = [a.reshape(b, h, n, c, dk) for a in (q, k, kb)]
    vb = vb.reshape(b, h, n, c, dv)
    g = jnp.cumsum(g.reshape(b, h, n, c), axis=-1)
    incl = jnp.tril(jnp.ones((c, c), dtype=bool))
    strict = jnp.tril(jnp.ones((c, c), dtype=bool), k=-1)
    diff = g[..., :, None] - g[..., None, :]
    decay = jnp.where(incl, jnp.exp(jnp.where(incl, diff, 0.0)), 0.0)
    a_mat = jnp.where(strict, jnp.einsum('bhnid,bhnjd->bhnij', kb, k) * decay, 0.0)
    ia = a_mat + jnp.eye(c, dtype=a_mat.dtype)
    u = lax.linalg.triangular_solve(ia, vb, left_side=True, lower=True, unit_diagonal=True)
    w = lax.linalg.triangular_solve(ia, kb * jnp.exp(g)[..., None], left_side=True, lower=True,
                                    unit_diagonal=True)
    qk = jnp.where(incl, jnp.einsum('bhnid,bhnjd->bhnij', q, k) * decay, 0.0)
    q_dec = q * jnp.exp(g)[..., None]
    g_last = g[..., -1]
    k_dec = k * jnp.exp(g_last[..., None] - g)[..., None]
    state_decay = jnp.exp(g_last)

    def step(s, xs):
        q_c, k_c, u_c, w_c, qk_c, sd_c = xs
        v_new = u_c - jnp.einsum('bhck,bhkv->bhcv', w_c, s)
        o_c = jnp.einsum('bhck,bhkv->bhcv', q_c, s) + jnp.einsum('bhij,bhjv->bhiv', qk_c, v_new)
        s = s * sd_c[..., None, None] + jnp.einsum('bhck,bhcv->bhkv', k_c, v_new)
        return s, o_c

    xs = tuple(jnp.moveaxis(a, 2, 0) for a in (q_dec, k_dec, u, w, qk, state_decay))
    s0 = jnp.zeros((b, h, dk, dv), dtype=jnp.float32)
    _, o = lax.scan(step, s0, xs)
    return jnp.moveaxis(o, 0, 2).reshape(b, h, t, dv)

def gated_deltanet_mixer(h, w_in, conv_w, a_log, dt_bias, norm_w, w_out):
    bsz, t, _ = h.shape
    proj = h @ w_in
    qkv, z, b_logit, a_logit = jnp.split(
        proj, [GDN_CONV_DIM, GDN_CONV_DIM + GDN_V, GDN_CONV_DIM + GDN_V + GDN_V_HEADS], axis=-1)
    qkv = jax.nn.silu(causal_depthwise_conv(qkv, conv_w))
    q, k, v = jnp.split(qkv, [GDN_QK, 2 * GDN_QK], axis=-1)
    rep = GDN_V_HEADS // GDN_K_HEADS
    q = jnp.repeat(l2_normalize(q.reshape(bsz, t, GDN_K_HEADS, GDN_HEAD_K)), rep, axis=2)
    k = jnp.repeat(l2_normalize(k.reshape(bsz, t, GDN_K_HEADS, GDN_HEAD_K)), rep, axis=2)
    v = v.reshape(bsz, t, GDN_V_HEADS, GDN_HEAD_V).astype(jnp.float32)
    beta = jax.nn.sigmoid(b_logit.astype(jnp.float32))
    g = -jnp.exp(a_log.astype(jnp.float32)) * jax.nn.softplus(
        a_logit.astype(jnp.float32) + dt_bias.astype(jnp.float32))
    to_bht = lambda a: jnp.swapaxes(a, 1, 2)
    o = chunked_gated_delta_rule(to_bht(q), to_bht(k), to_bht(v), to_bht(g), to_bht(beta))
    o = jnp.swapaxes(o, 1, 2)
    gate = jax.nn.silu(z.reshape(bsz, t, GDN_V_HEADS, GDN_HEAD_V).astype(jnp.float32))
    o = rms_norm(o, norm_w) * gate
    return o.reshape(bsz, t, GDN_V).astype(h.dtype) @ w_out

def short_conv_mixer(h, w_in, conv_w, w_out):
    u, b_gate, c_gate, z = jnp.split(h @ w_in, 4, axis=-1)
    y = b_gate * causal_depthwise_conv(c_gate * u, conv_w)
    return (y * jax.nn.silu(z)) @ w_out

def first_inputs(seed: int = 0) -> dict:
    key = jax.random.key(seed)
    ks = jax.random.split(key, 12)
    f32 = jnp.float32
    x = jax.random.normal(ks[0], (BATCH, SEQ, D_MODEL), f32)
    pre_norm_w = 1.0 + 0.05 * jax.random.normal(ks[1], (DEPTH, D_MODEL), f32)
    post_norm_w = 1.0 + 0.05 * jax.random.normal(ks[2], (DEPTH, D_MODEL), f32)
    gdn_w_in = jax.random.normal(ks[3], (N_GDN_LAYERS, D_MODEL, GDN_PROJ), f32) * D_MODEL ** -0.5
    gdn_conv_w = jax.random.normal(ks[4], (N_GDN_LAYERS, GDN_CONV, GDN_CONV_DIM), f32) * GDN_CONV ** -0.5
    gdn_A_log = jnp.log(jax.random.uniform(ks[5], (N_GDN_LAYERS, GDN_V_HEADS), f32, 1.0, 16.0))
    dt = jnp.exp(jax.random.uniform(ks[6], (N_GDN_LAYERS, GDN_V_HEADS), f32,
                                    float(np.log(1e-3)), float(np.log(1e-1))))
    gdn_dt_bias = dt + jnp.log(-jnp.expm1(-dt))
    gdn_norm_w = 1.0 + 0.05 * jax.random.normal(ks[7], (N_GDN_LAYERS, GDN_HEAD_V), f32)
    gdn_w_out = jax.random.normal(ks[8], (N_GDN_LAYERS, GDN_V, D_MODEL), f32) * GDN_V ** -0.5
    sc_w_in = jax.random.normal(ks[9], (N_SC_LAYERS, D_MODEL, SC_PROJ), f32) * D_MODEL ** -0.5
    sc_conv_w = jax.random.normal(ks[10], (N_SC_LAYERS, SC_CONV, SC_WIDTH), f32) * SC_CONV ** -0.5
    sc_w_out = jax.random.normal(ks[11], (N_SC_LAYERS, SC_WIDTH, D_MODEL), f32) * SC_WIDTH ** -0.5
    return {"x": x, "pre_norm_w": pre_norm_w, "post_norm_w": post_norm_w,
            "gdn_w_in": gdn_w_in, "gdn_conv_w": gdn_conv_w, "gdn_A_log": gdn_A_log,
            "gdn_dt_bias": gdn_dt_bias, "gdn_norm_w": gdn_norm_w, "gdn_w_out": gdn_w_out,
            "sc_w_in": sc_w_in, "sc_conv_w": sc_conv_w, "sc_w_out": sc_w_out}

def first_block(x, pre_norm_w, post_norm_w, gdn_w_in, gdn_conv_w, gdn_A_log, gdn_dt_bias, gdn_norm_w,
              gdn_w_out, sc_w_in, sc_conv_w, sc_w_out):
    for i in range(DEPTH):
        h = rms_norm(x, pre_norm_w[i]).astype(x.dtype)
        j = i // N_MIXERS
        if i % N_MIXERS == 0:
            y = gated_deltanet_mixer(h, gdn_w_in[j], gdn_conv_w[j], gdn_A_log[j], gdn_dt_bias[j],
                                     gdn_norm_w[j], gdn_w_out[j])
        else:
            y = short_conv_mixer(h, sc_w_in[j], sc_conv_w[j], sc_w_out[j])
        x = x + rms_norm(y, post_norm_w[i]).astype(x.dtype)
    return x


DEPTH_2 = 1

NSA_WIDTH = D_MODEL // 2
POOL_WIDTH = D_MODEL // 4
SGU_WIDTH = D_MODEL // 4
MIX_WIDTH = NSA_WIDTH + POOL_WIDTH + SGU_WIDTH

NSA_HEADS = 8
NSA_KV_GROUPS = 2
HEADS_PER_GROUP = NSA_HEADS // NSA_KV_GROUPS
HEAD_DIM = NSA_WIDTH // NSA_HEADS
KV_WIDTH = NSA_KV_GROUPS * HEAD_DIM
GATE_WIDTH = NSA_HEADS * 3
CMP_STRIDE = 16
CMP_LEN = 2 * CMP_STRIDE
CMP_HIDDEN = 2 * HEAD_DIM
SEL_BLOCK = 64
SEL_TOPK = 16
N_LOCAL_SEL = 2
SEL_RATIO = SEL_BLOCK // CMP_STRIDE
SEL_AGG = (1.0, 2.0, 2.0, 2.0, 1.0)
FORCE_SCORE = 1e9
WINDOW = 512
Q_BLOCK = 128

REL_BUCKETS = 32
REL_MAX_DIST = 1024

POOL_WINDOWS = (2, 4, 8, 16)
POOL_GROUPS = len(POOL_WINDOWS)
POOL_CH = POOL_WIDTH // POOL_GROUPS

SGU_GROUPS = 4
SGU_CH = SGU_WIDTH // SGU_GROUPS
SGU_CHUNK = 128

IN_WIDTHS = (NSA_WIDTH, KV_WIDTH, KV_WIDTH, KV_WIDTH, KV_WIDTH, KV_WIDTH, KV_WIDTH,
             GATE_WIDTH, POOL_WIDTH, SGU_WIDTH, SGU_WIDTH)
IN_WIDTH = sum(IN_WIDTHS)
IN_SPLITS = tuple(int(s) for s in np.cumsum(IN_WIDTHS)[:-1])

MEM_LEN = 256
MEM_HEADS = 4
MEM_HEAD_DIM = D_MODEL // MEM_HEADS

FFN_HIDDEN = ((11 * D_MODEL // 4) // 128) * 128
CONV_WIDTH = 3

EPS = 1e-6
F32 = jnp.float32


def rms_norm_2(x, g):
    xf = x.astype(F32)
    y = xf * lax.rsqrt(jnp.mean(xf * xf, axis=-1, keepdims=True) + EPS)
    return (y * g.astype(F32)).astype(x.dtype)

def layer_norm(x, g, b):
    xf = x.astype(F32)
    mu = jnp.mean(xf, axis=-1, keepdims=True)
    var = jnp.mean(jnp.square(xf - mu), axis=-1, keepdims=True)
    return ((xf - mu) * lax.rsqrt(var + EPS) * g.astype(F32) + b.astype(F32)).astype(x.dtype)

def t5_bucket(dist):
    n = jnp.maximum(dist, 0)
    max_exact = REL_BUCKETS // 2
    nf = jnp.maximum(n, 1).astype(F32)
    large = max_exact + (jnp.log(nf / max_exact) / math.log(REL_MAX_DIST / max_exact)
                         * (REL_BUCKETS - max_exact)).astype(jnp.int32)
    large = jnp.minimum(large, REL_BUCKETS - 1)
    return jnp.where(n < max_exact, n, large)

def masked_softmax(s, mask):
    s = jnp.where(mask, s.astype(F32), -jnp.inf)
    m = jnp.max(s, axis=-1, keepdims=True)
    m = jnp.where(jnp.isfinite(m), m, 0.0)
    e = jnp.where(mask, jnp.exp(s - m), 0.0)
    return e / jnp.maximum(jnp.sum(e, axis=-1, keepdims=True), 1.0)

def compress(kv, pos, w1, b1, w2, b2):
    B, S, G, dk = kv.shape
    r = kv.reshape(B, S // CMP_STRIDE, CMP_STRIDE, G, dk)
    blocks = jnp.concatenate([r[:, :-1], r[:, 1:]], axis=2) + pos[None, None, :, None, :]
    h = jax.nn.gelu(jnp.einsum('bclgd,ldh->bcgh', blocks, w1) + b1)
    return jnp.einsum('bcgh,hd->bcgd', h, w2) + b2

def nsa_mixer(q, k_cmp, v_cmp, k_sel, v_sel, k_win, v_win, gates, rel_bias,
              cmp_pos, cmp_w1, cmp_b1, cmp_w2, cmp_b2):
    B, S, G, Hg, dk = q.shape
    scale = dk ** -0.5
    kc = compress(k_cmp, cmp_pos[0], cmp_w1[0], cmp_b1[0], cmp_w2[0], cmp_b2[0])
    vc = compress(v_cmp, cmp_pos[1], cmp_w1[1], cmp_b1[1], cmp_w2[1], cmp_b2[1])
    NC = kc.shape[1]
    NS = S // SEL_BLOCK
    topk = min(SEL_TOPK, NS)
    ksb = jnp.transpose(k_sel.reshape(B, NS, SEL_BLOCK, G, dk), (0, 3, 1, 2, 4))
    vsb = jnp.transpose(v_sel.reshape(B, NS, SEL_BLOCK, G, dk), (0, 3, 1, 2, 4))
    kwp = jnp.pad(k_win, ((0, 0), (WINDOW, 0), (0, 0), (0, 0)))
    vwp = jnp.pad(v_win, ((0, 0), (WINDOW, 0), (0, 0), (0, 0)))
    cmp_end = jnp.arange(NC) * CMP_STRIDE + CMP_LEN - 1
    sel_start = jnp.arange(NS) * SEL_BLOCK
    jj = jnp.arange(NS)
    bias_g = jnp.transpose(rel_bias.reshape(REL_BUCKETS, G, Hg), (1, 0, 2))
    gidx = jnp.arange(G)
    bidx = jnp.arange(B)
    ti = jnp.arange(Q_BLOCK)
    wj = jnp.arange(Q_BLOCK + WINDOW)
    wdist = ti[:, None] + WINDOW - wj[None, :]
    win_band = (wdist >= 0) & (wdist < WINDOW)
    win_bias = jnp.transpose(rel_bias[t5_bucket(wdist)].reshape(Q_BLOCK, Q_BLOCK + WINDOW, G, Hg), (2, 3, 0, 1))
    nblk = S // Q_BLOCK
    qb = jnp.moveaxis(q.reshape(B, nblk, Q_BLOCK, G, Hg, dk), 1, 0)
    gb = jnp.moveaxis(gates.reshape(B, nblk, Q_BLOCK, G, Hg, 3), 1, 0)

    def block(args):
        qi, gi, i = args
        s0 = i * Q_BLOCK
        t = s0 + ti
        qs = qi * scale
        sc = jnp.einsum('btghd,bcgd->bghtc', qs, kc)
        cdist = t[:, None] - cmp_end[None, :]
        cbias = jnp.transpose(rel_bias[t5_bucket(cdist)].reshape(Q_BLOCK, NC, G, Hg), (2, 3, 0, 1))
        pc = masked_softmax(sc + cbias, cdist >= 0)
        o_cmp = jnp.einsum('bghtc,bcgd->btghd', pc.astype(vc.dtype), vc)
        imp = jnp.pad(jnp.sum(pc, axis=2), ((0, 0), (0, 0), (0, 0), (1, 1)))
        p_sel = sum(w * imp[..., m:m + SEL_RATIO * NS:SEL_RATIO] for m, w in enumerate(SEL_AGG))
        blk_q = t // SEL_BLOCK
        rel_blk = blk_q[:, None] - jj[None, :]
        svalid = sel_start[None, :] <= t[:, None]
        forced = (jj[None, :] == 0) | ((rel_blk >= 0) & (rel_blk < N_LOCAL_SEL))
        score = jnp.where(forced, FORCE_SCORE, jnp.where(svalid, p_sel, -1.0))
        _, sidx = lax.top_k(score, topk)
        ks = ksb[bidx[:, None, None, None], gidx[None, :, None, None], sidx]
        vs = vsb[bidx[:, None, None, None], gidx[None, :, None, None], sidx]
        spos = sidx[..., None] * SEL_BLOCK + jnp.arange(SEL_BLOCK)
        sdist = t[None, None, :, None, None] - spos
        sbias = bias_g[gidx[None, :, None, None, None], t5_bucket(sdist)]
        ss = jnp.einsum('btghd,bgtkld->bghtkl', qs, ks) + jnp.transpose(sbias, (0, 1, 5, 2, 3, 4))
        nsel = topk * SEL_BLOCK
        ps = masked_softmax(ss.reshape(B, G, Hg, Q_BLOCK, nsel), (sdist >= 0).reshape(B, G, 1, Q_BLOCK, nsel))
        o_sel = jnp.einsum('bghtn,bgtnd->btghd', ps.astype(vs.dtype), vs.reshape(B, G, Q_BLOCK, nsel, dk))
        kw = lax.dynamic_slice_in_dim(kwp, s0, Q_BLOCK + WINDOW, axis=1)
        vw = lax.dynamic_slice_in_dim(vwp, s0, Q_BLOCK + WINDOW, axis=1)
        wpos = s0 - WINDOW + wj
        sw = jnp.einsum('btghd,bsgd->bghts', qs, kw) + win_bias
        pw = masked_softmax(sw, win_band & (wpos >= 0)[None, :])
        o_win = jnp.einsum('bghts,bsgd->btghd', pw.astype(vw.dtype), vw)
        return gi[..., 0:1] * o_cmp + gi[..., 1:2] * o_sel + gi[..., 2:3] * o_win

    out = lax.map(block, (qb, gb, jnp.arange(nblk)))
    return jnp.moveaxis(out, 0, 1).reshape(B, S, G * Hg * dk)

def pool_mixer(p, w, scale):
    B, S, C = p.shape
    pf = p.astype(F32)
    cs = jnp.pad(jnp.cumsum(pf, axis=1), ((0, 0), (1, 0), (0, 0)))
    t = jnp.arange(S)
    outs = []
    for gi, win in enumerate(POOL_WINDOWS):
        seg = cs[:, :, gi * POOL_CH:(gi + 1) * POOL_CH]
        lo = jnp.maximum(t + 1 - win, 0)
        cnt = jnp.minimum(t + 1, win).astype(F32)
        outs.append((seg[:, 1:] - seg[:, lo]) / cnt[None, :, None] - pf[:, :, gi * POOL_CH:(gi + 1) * POOL_CH])
    d = jnp.stack(outs, axis=2).astype(p.dtype)
    return jnp.einsum('bsgc,gcd->bsgd', d, w).reshape(B, S, C) * scale

def sgu_mixer(u, v, norm_g, norm_b, w_s, b_s):
    B, S, C = u.shape
    u = jax.nn.gelu(u)
    v = layer_norm(jax.nn.gelu(v), norm_g, norm_b)
    vc = v.reshape(B, S // SGU_CHUNK, SGU_CHUNK, SGU_GROUPS, SGU_CH)
    causal = jnp.tril(jnp.ones((SGU_CHUNK, SGU_CHUNK), dtype=bool))
    ws = jnp.where(causal, w_s, 0.0)
    mixed = jnp.einsum('hts,bnshc->bnthc', ws, vc) + jnp.transpose(b_s)[:, :, None]
    return u * mixed.reshape(B, S, C)

def memory_attention(h, mem_n, wq, wk, wv, wo):
    B, S, D = h.shape
    M = mem_n.shape[1]
    q = (h @ wq).reshape(B, S, MEM_HEADS, MEM_HEAD_DIM)
    k = (mem_n @ wk).reshape(B, M, MEM_HEADS, MEM_HEAD_DIM)
    v = (mem_n @ wv).reshape(B, M, MEM_HEADS, MEM_HEAD_DIM)
    s = jnp.einsum('bshd,bmhd->bhsm', q, k).astype(F32) * (MEM_HEAD_DIM ** -0.5)
    p = jax.nn.softmax(s, axis=-1).astype(v.dtype)
    return jnp.einsum('bhsm,bmhd->bshd', p, v).reshape(B, S, D) @ wo

def conv_ffn(h, w_up, conv_w, conv_b, w_down):
    a = h @ w_up
    a = lax.conv_general_dilated(a, conv_w[:, None, :], window_strides=(1,),
                                 padding=[(CONV_WIDTH - 1, 0)],
                                 dimension_numbers=('NWC', 'WIO', 'NWC'),
                                 feature_group_count=a.shape[-1]) + conv_b
    gate, val = jnp.split(a, 2, axis=-1)
    return (jax.nn.gelu(gate) * val) @ w_down

def second_inputs(seed: int = 0) -> dict:
    key = jax.random.key(seed)
    ks = iter(jax.random.split(key, 40))

    def nrm(shape, scale):
        return jax.random.normal(next(ks), shape, F32) * scale

    def gain(shape):
        return 1.0 + 0.1 * jax.random.normal(next(ks), shape, F32)

    L, D, H2 = DEPTH_2, D_MODEL, 2 * FFN_HIDDEN
    return {
        'x': nrm((BATCH, SEQ, D), 1.0),
        'mem': nrm((BATCH, MEM_LEN, D), 1.0),
        'rel_bias': nrm((REL_BUCKETS, NSA_HEADS), 0.2),
        'mix_norm_pre': gain((L, D)),
        'mix_norm_post': gain((L, D)),
        'w_in': nrm((L, D, IN_WIDTH), D ** -0.5),
        'cmp_pos': nrm((L, 2, CMP_LEN, HEAD_DIM), 0.1),
        'cmp_w1': nrm((L, 2, CMP_LEN, HEAD_DIM, CMP_HIDDEN), (CMP_LEN * HEAD_DIM) ** -0.5),
        'cmp_b1': nrm((L, 2, CMP_HIDDEN), 0.01),
        'cmp_w2': nrm((L, 2, CMP_HIDDEN, HEAD_DIM), CMP_HIDDEN ** -0.5),
        'cmp_b2': nrm((L, 2, HEAD_DIM), 0.01),
        'pool_w': nrm((L, POOL_GROUPS, POOL_CH, POOL_CH), POOL_CH ** -0.5),
        'pool_scale': gain((L, POOL_WIDTH)),
        'sgu_norm_g': gain((L, SGU_WIDTH)),
        'sgu_norm_b': nrm((L, SGU_WIDTH), 0.01),
        'sgu_w': nrm((L, SGU_GROUPS, SGU_CHUNK, SGU_CHUNK), SGU_CHUNK ** -0.5),
        'sgu_b': gain((L, SGU_GROUPS, SGU_CHUNK)),
        'w_out': nrm((L, MIX_WIDTH, D), MIX_WIDTH ** -0.5),
        'mem_norm_pre': gain((L, D)),
        'mem_norm_kv': gain((L, D)),
        'mem_norm_post': gain((L, D)),
        'w_mq': nrm((L, D, D), D ** -0.5),
        'w_mk': nrm((L, D, D), D ** -0.5),
        'w_mv': nrm((L, D, D), D ** -0.5),
        'w_mo': nrm((L, D, D), D ** -0.5),
        'ffn_norm_pre': gain((L, D)),
        'ffn_norm_post': gain((L, D)),
        'w_up': nrm((L, D, H2), D ** -0.5),
        'conv_w': nrm((L, CONV_WIDTH, H2), CONV_WIDTH ** -0.5),
        'conv_b': nrm((L, H2), 0.01),
        'w_down': nrm((L, FFN_HIDDEN, D), FFN_HIDDEN ** -0.5),
    }

def second_block(x, mem, rel_bias, mix_norm_pre, mix_norm_post, w_in, cmp_pos, cmp_w1, cmp_b1,
              cmp_w2, cmp_b2, pool_w, pool_scale, sgu_norm_g, sgu_norm_b, sgu_w, sgu_b, w_out,
              mem_norm_pre, mem_norm_kv, mem_norm_post, w_mq, w_mk, w_mv, w_mo,
              ffn_norm_pre, ffn_norm_post, w_up, conv_w, conv_b, w_down):
    B, S, D = x.shape
    G, Hg, dk = NSA_KV_GROUPS, HEADS_PER_GROUP, HEAD_DIM
    for l in range(DEPTH_2):
        h = rms_norm_2(x, mix_norm_pre[l])
        proj = h @ w_in[l]
        q, kc, vc, ksl, vsl, kw, vw, gt, pin, u, v = jnp.split(proj, IN_SPLITS, axis=-1)
        gates = jax.nn.sigmoid(gt.astype(F32)).astype(x.dtype).reshape(B, S, G, Hg, 3)
        kv = lambda a: a.reshape(B, S, G, dk)
        out_a = nsa_mixer(q.reshape(B, S, G, Hg, dk), kv(kc), kv(vc), kv(ksl), kv(vsl), kv(kw), kv(vw),
                          gates, rel_bias, cmp_pos[l], cmp_w1[l], cmp_b1[l], cmp_w2[l], cmp_b2[l])
        out_b = pool_mixer(pin, pool_w[l], pool_scale[l])
        out_c = sgu_mixer(u, v, sgu_norm_g[l], sgu_norm_b[l], sgu_w[l], sgu_b[l])
        mix = jnp.concatenate([out_a, out_b, out_c], axis=-1) @ w_out[l]
        x = x + rms_norm_2(mix, mix_norm_post[l])
        h = rms_norm_2(x, mem_norm_pre[l])
        m = rms_norm_2(mem, mem_norm_kv[l])
        x = x + rms_norm_2(memory_attention(h, m, w_mq[l], w_mk[l], w_mv[l], w_mo[l]), mem_norm_post[l])
        h = rms_norm_2(x, ffn_norm_pre[l])
        x = x + rms_norm_2(conv_ffn(h, w_up[l], conv_w[l], conv_b[l], w_down[l]), ffn_norm_post[l])
    return x


def setup_inputs(seed=0):
    out = dict(first_inputs(seed))
    for name, value in second_inputs(seed + 1).items():
        if name != "x":
            out[name + "_2"] = value
    return out


def reference(
    x, pre_norm_w, post_norm_w, gdn_w_in, gdn_conv_w, gdn_A_log, gdn_dt_bias, gdn_norm_w,
    gdn_w_out, sc_w_in, sc_conv_w, sc_w_out, mem_2, rel_bias_2, mix_norm_pre_2, mix_norm_post_2,
    w_in_2, cmp_pos_2, cmp_w1_2, cmp_b1_2, cmp_w2_2, cmp_b2_2, pool_w_2, pool_scale_2,
    sgu_norm_g_2, sgu_norm_b_2, sgu_w_2, sgu_b_2, w_out_2, mem_norm_pre_2, mem_norm_kv_2,
    mem_norm_post_2, w_mq_2, w_mk_2, w_mv_2, w_mo_2, ffn_norm_pre_2, ffn_norm_post_2, w_up_2,
    conv_w_2, conv_b_2, w_down_2,
):
    x = first_block(
        x, pre_norm_w, post_norm_w, gdn_w_in, gdn_conv_w, gdn_A_log, gdn_dt_bias, gdn_norm_w,
        gdn_w_out, sc_w_in, sc_conv_w, sc_w_out,
    )
    return second_block(
        x, mem_2, rel_bias_2, mix_norm_pre_2, mix_norm_post_2, w_in_2, cmp_pos_2, cmp_w1_2,
        cmp_b1_2, cmp_w2_2, cmp_b2_2, pool_w_2, pool_scale_2, sgu_norm_g_2, sgu_norm_b_2,
        sgu_w_2, sgu_b_2, w_out_2, mem_norm_pre_2, mem_norm_kv_2, mem_norm_post_2, w_mq_2,
        w_mk_2, w_mv_2, w_mo_2, ffn_norm_pre_2, ffn_norm_post_2, w_up_2, conv_w_2, conv_b_2,
        w_down_2,
    )


_drawn_inputs = setup_inputs


def setup_inputs(seed=0):
    import zlib

    import numpy as np

    out = dict(_drawn_inputs(seed))
    spreads = {}
    factors = {'rel_bias_2': 3.515,
     'cmp_pos_2': 3.424,
     'cmp_b1_2': 41.045,
     'cmp_b2_2': 24.021,
     'sgu_norm_g_2': 2.728,
     'sgu_norm_b_2': 44.515,
     'conv_b_2': 8.0}
    for name, (base, spread) in spreads.items():
        noise = np.random.default_rng([zlib.crc32(name.encode()), seed]).standard_normal(out[name].shape)
        drawn = base * np.exp(spread * noise) if base else spread * noise
        out[name] = __import__('jax').numpy.asarray(drawn.astype(out[name].dtype))
    for name, factor in factors.items():
        out[name] = (out[name] * factor).astype(out[name].dtype)
    return out
```

```python
import numpy as np
import concourse.bass as bass
from concourse import mybir
from contextlib import ExitStack

S = 512
D = 1024
P = 128
KD = D // P
NT = S // P
EPS = 1e-6
NEG = -1.0e30
KH, VH = 8, 16
QK_W, V_W = KH * P, VH * P
CONV_W = 2 * QK_W + V_W
TAPS = 4
CH = 64
GROUPS = 4
HG = VH // GROUPS
SC = 2048
ATT_H, DH = 8, 64
REL = 32
NC = S // 16 - 1
W2 = 2072
MEM, MH = 256, 4
FF = 2816
FK = FF // P
SLOT = 2048


def shape_constants():
    i = np.arange(P)
    row, col = i[:, None], i[None, :]
    same = row // CH == col // CH
    parts = [np.eye(P), same & (row <= col), np.where(same & (row <= col), 0.0, NEG)]
    for s in (1, 2, 4, 8, 16, 32):
        pair = (row // (2 * s) == col // (2 * s)) & (col // s % 2 == 1) & (row // s % 2 == 0)
        parts.append(-1.0 * pair)
    parts += [same, (row < CH) & (col >= 0), (row >= CH) & (col >= 0), np.ones((P, P)), row <= col]
    masks = np.concatenate([np.asarray(m, np.float32) for m in parts], 1)
    dist = np.arange(S)
    n = np.maximum(dist, 1).astype(np.float32)
    far = 16 + (np.log(n / np.float32(16)) / np.float32(np.log(64.0)) * np.float32(16)).astype(np.int32)
    bucket = np.where(dist < 16, dist, np.minimum(far, REL - 1))
    hot = np.zeros((REL + 1, 1023), np.float32)
    y = np.arange(1023)
    hot[np.where(y < 511, REL, bucket[np.maximum(y - 511, 0)]), y] = 1
    hot = np.concatenate([hot, np.zeros((REL + 1, 1), np.float32)], 1)
    hot[REL, 1023] = 1
    hot = np.concatenate([hot, hot[:, 1022::-1], hot[:, 1023:]], 1)
    inv = np.zeros((P, 2, 16), np.float32)
    for g, win in enumerate((2, 4, 8, 16)):
        inv[64 * (g % 2):64 * (g % 2) + 64, g // 2] = 1.0 / np.minimum(np.arange(16) + 1, win)
    return masks, hot, inv.reshape(P, 32)


class Tally:

    def __init__(self, eng, sem):
        self.eng, self.sem, self.base, self.n = eng, sem, 0, 0

    def did(self, ins):
        ins.then_inc(self.sem, 1)
        self.n += 1
        return self.now()

    def now(self):
        return self.base + self.n

    def settle(self):
        self.eng.wait_ge(self.sem, self.now())

    def enter(self, i, per):
        self.start, self.per = self.now(), per
        self.base, self.n = self.start + i * per, 0

    def leave(self, times):
        assert self.n == self.per, (self.sem, self.n)
        self.base, self.n = self.start + times * self.per, 0


def build(nc, x, pre_norm_w, post_norm_w, gdn_w_in, gdn_conv_w, gdn_A_log, gdn_dt_bias, gdn_norm_w, gdn_w_out,
          sc_w_in, sc_conv_w, sc_w_out, mem_2, rel_bias_2, mix_norm_pre_2, mix_norm_post_2, w_in_2, cmp_pos_2,
          cmp_w1_2, cmp_b1_2, cmp_w2_2, cmp_b2_2, pool_w_2, pool_scale_2, sgu_norm_g_2, sgu_norm_b_2, sgu_w_2,
          sgu_b_2, w_out_2, mem_norm_pre_2, mem_norm_kv_2, mem_norm_post_2, w_mq_2, w_mk_2, w_mv_2, w_mo_2,
          ffn_norm_pre_2, ffn_norm_post_2, w_up_2, conv_w_2, conv_b_2, w_down_2, masks_d, hot_d, inv_d, out):
    F32 = mybir.dt.float32
    ALU, ACT, AX = mybir.AluOpType, mybir.ActivationFunctionType, mybir.AxisListType
    ds = bass.ds
    ctx = ExitStack()
    with ctx:
        def sb(name, *shape):
            return ctx.enter_context(nc.sbuf_tensor(name, [shape[0], int(np.prod(shape[1:]))], F32))

        def sem(name):
            return ctx.enter_context(nc.semaphore(name))

        xT = sb("xT", P, KD, S)[:, :].rearrange("p (k s) -> p k s", k=KD)
        hT = sb("hT", P, KD, S)[:, :].rearrange("p (k s) -> p k s", k=KD)
        ring = sb("ring", P, 6, SLOT)[:, :].rearrange("p (r w) -> p r w", r=6)
        masks = sb("masks", P, 14, P)[:, :].rearrange("p (m c) -> p m c", m=14)
        cols = sb("cols", P, 5, P)[:, :].rearrange("p (m c) -> p m c", m=5)
        rs = sb("rs", P, S)
        sq = sb("sq", P, 2, S)[:, :].rearrange("p (r s) -> p r s", r=2)
        small = sb("small", P, 64)
        inv_count = sb("inv_count", P, 32)[:, :]
        eps = small[:, 0:1]
        ident, upper, negmask = masks[:, 0, :], masks[:, 1, :], masks[:, 2, :]
        neglevel = [masks[:, 3 + n, :] for n in range(6)]
        same, half0, half1, ones, causal = [masks[:, 9 + n, :] for n in range(5)]
        ARENA = 28600
        arena = sb("arena", P, ARENA)
        psum = [ctx.enter_context(nc.psum_tensor(f"bank{n}", [P, S], F32)) for n in range(8)]

        def cut(start, *shape):
            n = int(np.prod(shape))
            assert start + n <= ARENA, (start, shape)
            v = arena[:, start:start + n]
            if len(shape) == 2:
                v = v.rearrange("p (a b) -> p a b", a=shape[0])
            if len(shape) == 3:
                v = v.rearrange("p (a b c) -> p a b c", a=shape[0], b=shape[1])
            return v, start + n

        GCONV = lambda tap, c: cols[:, 0, tap * 32 + c:tap * 32 + c + 1] if isinstance(c, int) else cols[:, 0, ds(c + tap * 32, 1)]
        SCONV = lambda tap, c: cols[:, 1, ds(c + tap * 16, 1)]
        FCONV = lambda tap, c: (cols[:, 2 + tap // 2, ds(c + (tap % 2) * 44, 1)])
        FBIAS = lambda c: cols[:, 3, ds(c + 44, 1)]
        GNW = cols[:, 1, 50:51]
        PSC = lambda c: cols[:, 1, 48 + c:49 + c]
        PRE = [lambda k: cols[:, 4, k:k + 1], lambda k: cols[:, 4, 8 + k:9 + k],
               lambda k: cols[:, 4, 32 + k:33 + k], lambda k: cols[:, 4, 48 + k:49 + k], lambda k: cols[:, 4, 72 + k:73 + k]]
        POST = [lambda k: cols[:, 4, 16 + k:17 + k], lambda k: cols[:, 4, 24 + k:25 + k],
                lambda k: cols[:, 4, 40 + k:41 + k], lambda k: cols[:, 4, 64 + k:65 + k], lambda k: cols[:, 4, 80 + k:81 + k]]
        KVW = lambda k: cols[:, 4, 56 + k:57 + k]

        consts_in = sem("consts_in")
        rows_in = sem("rows_in")
        x_in = sem("x_in")
        slot_in = [sem(f"slot_in{n}") for n in range(6)]
        chunk_done = sem("chunk_done")
        chunk_out = sem("chunk_out")
        square_ready = sem("square_ready")
        square_used = sem("square_used")
        rms_ready = sem("rms_ready")
        h_ready = sem("h_ready")
        x_ready = sem("x_ready")
        act_step = sem("act_step")
        dve_step = sem("dve_step")
        pool_step = sem("pool_step")
        eps_set = sem("eps_set")
        turned = sem("turned")
        turned_used = sem("turned_used")
        inv_in = sem("inv_in")
        stored = sem("stored")

        gate_out, at = cut(0, VH, S)
        q_T, at = cut(at, 2, S)
        k_T, at = cut(at, 2, S)
        v_T, at = cut(at, HG, S)
        z_T, at = cut(at, HG, S)
        raw, at = cut(at, 3, S)
        k_rows, at = cut(at, 2, S)
        kk, at = cut(at, 2, S)
        kq, at = cut(at, 2, S)
        decay, at = cut(at, 2, S)
        A_T, at = cut(at, HG, S)
        Y_T, at = cut(at, HG, S)
        QK_T, at = cut(at, HG, S)
        state, at = cut(at, HG, P)
        resid, v_new, v_dec = [A_T[:, n, :].rearrange("p (h c) -> p h c", h=HG) for n in range(3)]
        tok, at = cut(at, 12, 64)
        grp, at = cut(at, 2, 16)
        ssq, at = cut(at, 2, 16)
        wba, at = cut(at, KD, 32)
        alog, at = cut(at, 2, 16)
        beta, g_log, G_cum, G_end, e_G, neg_G, neg_bG, e_rest, end0, end1, tmpA, tmpB = [tok[:, n, :] for n in range(12)]
        x_rows = arena[:, 0:NT * D].rearrange("p (t c) -> p t c", t=NT)
        par_rows = arena[:, NT * D:NT * D + 5 * P].rearrange("p (m c) -> p m c", m=5)
        y_T, _ = cut(VH * S, KD, S)
        R2 = lambda v: v.rearrange("p (t c) -> p t c", t=NT)
        R4 = lambda v: v.rearrange("p (t h) -> p t h", t=NT)

        wba_in = sem("wba_in")
        ba_done = sem("ba_done")
        tok_act, tok_dve, tok_exp = sem("tok_act"), sem("tok_dve"), sem("tok_exp")
        cum_done = sem("cum_done")
        tok_ready = sem("tok_ready")
        conv_done = sem("conv_done")
        silu_done = sem("silu_done")
        l2_sq = sem("l2_sq")
        l2_sum = sem("l2_sum")
        l2_rms = sem("l2_rms")
        qk_ready = sem("qk_ready")
        grp_ready = sem("grp_ready")
        kk_done, kk_ready = sem("kk_done"), sem("kk_ready")
        kr_done, kr_ready = sem("kr_done"), sem("kr_ready")
        vt_done, vb_ready = sem("vt_done"), sem("vb_ready")
        gb_done, decay_ready = sem("gb_done"), sem("decay_ready")
        decay_used = sem("decay_used")
        bb_done, y_start = sem("bb_done"), sem("y_start")
        level_ready, level_used = sem("level_ready"), sem("level_used")
        xt_done, xt_ready = sem("xt_done"), sem("xt_ready")
        p_done, p_ready = sem("p_done"), sem("p_ready")
        py_done, y_ready = sem("py_done"), sem("y_ready")
        ks_done, resid_ready = sem("ks_done"), sem("resid_ready")
        vn_done, vn_ready = sem("vn_done"), sem("vn_ready")
        su_done, state_ready = sem("su_done"), sem("state_ready")
        scan_done = sem("scan_done")
        ssq_ready, ot_done, gate_ready = sem("ssq_ready"), sem("ot_done"), sem("gate_ready")

        sc_out, _ = cut(0, SC // P, S)
        sc_in, at = cut(12288, 8, S)
        sc_conv, at = cut(at, 2, S)
        sc_used = sem("sc_used")
        mix_T, at = cut(0, KD, S)
        att_q, at = cut(at, 4, S)
        cmp_kv, at = cut(at, 2, S)
        att_k, at = cut(at, 2, S)
        pool_x, at = cut(at, 2, S)
        pool_a, at = cut(at, 2, S)
        pool_b, at = cut(at, 2, S)
        pool_d, at = cut(at, 2, S)
        sgu_u, at = cut(at, 2, S)
        att_v, at = cut(at, NT, 256)
        sgu_v, at = cut(at, NT, 256)
        w_gate, at = cut(at, KD, 24)
        gate_raw, at = cut(at, NT, 24)
        gate, at = cut(at, NT, 24)
        spatial_T, at = cut(at, 4, P)
        sgu_gb, at = cut(at, 2, 256)
        sgu_bias, at = cut(at, 2, P)
        w_pool, at = cut(at, 2, DH)
        w_c2, at = cut(at, 2, DH)
        b_c2, at = cut(at, 2, DH)
        assert at <= 17408, at
        bias_row, at = cut(17408, ATT_H, S)
        bias_cmp, at = cut(at, NT, ATT_H * NC)
        free = at
        hot, at = cut(free, 2, 1024)
        table, at = cut(at, 2, 1024)
        bias_cmp_T, _ = cut(free, ATT_H, S)
        prob, at = cut(free, 4, S)
        prob_T, at = cut(at, 2, S)
        att_o, at = cut(at, 3, S)
        sgu_t, _ = cut(free + 3072, NT, 256)
        blocks, at = cut(at, 32 * NC)
        hidden, at = cut(at, 4, NC)
        cmp_k, at = cut(at, NC)
        cmp_v, at = cut(at, P)
        pos_T, at = cut(at, 64)
        pos_rows, at = cut(at, P)
        spatial_rows = mix_T[:, 6, :].rearrange("p (h s) -> p h s", h=4)
        cmp_prob = blocks[:, 0:ATT_H * NC].rearrange("p (h c) -> p h c", h=ATT_H)
        rel = small[0:REL + 1, 1:9]
        neg_max = lambda n: small[:, 1 + n % 4:2 + n % 4]
        cmp_max = small[:, 5:13]
        sums = lambda qi, kind: small[:, 13 + 24 * (qi % 2) + 8 * kind:21 + 24 * (qi % 2) + 8 * kind]
        ROW_L, CMP_L = S + P, 2 * S - 32
        row_copies = nc.dram_tensor("row_copies", [ATT_H, P, ROW_L], F32, kind="Internal").ap()
        cmp_copies = nc.dram_tensor("cmp_copies", [ATT_H, NC, CMP_L], F32, kind="Internal").ap()
        hot_in, mixer_in = sem("hot_in"), sem("mixer_in")
        rel_in = sem("rel_in")
        table_done, table_out = sem("table_done"), sem("table_out")
        table_stored, bias_in = sem("table_stored"), sem("bias_in")
        turn_done, turn_out = sem("turn_done"), sem("turn_out")
        ct_done = sem("ct_done")
        mask_done = sem("mask_done")
        blocks_ready, hid_done, hid_ready = sem("blocks_ready"), sem("hid_done"), sem("hid_ready")
        c2_done, c2_ready = sem("c2_done"), sem("c2_ready")
        gate_exp, gates_ready = sem("gate_exp"), sem("gates_ready")
        var_ready, rstd_ready, sgu_norm = sem("var_ready"), sem("rstd_ready"), sem("sgu_norm")
        spatial_done, sgu_done = sem("spatial_done"), sem("sgu_done")
        pool_ready, pool_done, pool_out = sem("pool_ready"), sem("pool_done"), sem("pool_out")
        score_done, score_read, prob_ready = sem("score_done"), sem("score_read"), sem("prob_ready")
        probT_done, probT_out, pv_done = sem("probT_done"), sem("probT_out"), sem("pv_done")
        combined, attT_done, attT_out = sem("combined"), sem("attT_done"), sem("attT_out")
        units = [(qi, kind, h) for qi in range(NT) for kind, h in [(0, 0)] + [(k, h) for k in (1, 2) for h in range(ATT_H)]]
        is_cmp = lambda n: 0 <= n < len(units) and units[n][1] == 0
        MT, HD = MEM // P, D // MH
        mem_out, at = cut(0, KD, S)
        mem_q, at = cut(at, KD, S)
        mem_k, at = cut(12288, KD, MEM)
        mem_v, at = cut(at, MT, D)
        mem_rows, at = cut(at, MT, D)
        mem_T, at = cut(at, KD, MEM)
        mem_prob, at = cut(at, 4, MEM)
        mem_probT, at = cut(at, 4, S)
        mem_junk = mem_T.rearrange("p k m -> p (k m)")[:, 0:D]
        mem_sum = lambda n: small[:, 20 + n:21 + n]
        mem_max = lambda n: small[:, 36 + n:37 + n]
        mem_in = sem("mem_in")
        mem_rstd, mem_scaled = sem("mem_rstd"), sem("mem_scaled")
        mem_turned, mem_turned_out = sem("mem_turned"), sem("mem_turned_out")
        ms_done, ms_max, mp_exp, mp_ready = sem("ms_done"), sem("ms_max"), sem("mp_exp"), sem("mp_ready")
        mpT_done, mpT_out = sem("mpT_done"), sem("mpT_out")
        mem_units = [(h, qi) for h in range(MH) for qi in range(NT)]
        ff_hid, at = cut(0, FK, S)
        ff_y, at = cut(at, KD, S)
        ff_raw, at = cut(at, 4, S)
        ff_gate, at = cut(at, 2, S)
        ff_val, at = cut(at, 2, S)
        out_rows_sb, _ = cut(0, NT, D)
        ff_conv, ff_gelu, ff_ready = sem("ff_conv"), sem("ff_gelu"), sem("ff_ready")
        final_done, final_act, final_dve = sem("final_done"), sem("final_act"), sem("final_dve")
        FF0 = 196
        def passes(eng, n):
            with eng.Fori(0, n) as i:
                yield i

        def slab_rows(ring, pos, c, n):
            return lambda k: ring[:, pos, k * 256 + c:k * 256 + c + n]

        MIXER_IN = 16 * 17

        def halves(c):
            return slice(CH * (c % 2), CH * (c % 2) + CH), c // 2

        block = ctx.enter_context(nc.Block())

        @block.sync
        def _(sp):
            held = {}
            state_ = {"chunks": 0}

            def load(pos, src, view, chunks):
                if pos in held:
                    sp.wait_ge(chunk_done, held[pos])
                sp.dma_start(view(ring[:, pos, :]), src).then_inc(slot_in[pos], 16)
                state_["chunks"] += chunks
                held[pos] = state_["chunks"]

            wide = lambda n: (lambda r: r[:, 0:n * KD].rearrange("p (k c) -> p k c", k=KD))
            sp.dma_start(masks[:, :, :].rearrange("p m c -> p (m c)"), masks_d).then_inc(consts_in, 16)
            sp.dma_start(x_rows, x[0].rearrange("(t p) c -> p t c", p=P)).then_inc(x_in, 16)
            par = [
                (0, 0, gdn_conv_w[0].rearrange("t (c p) -> (t c) p", p=P), 128),
                (1, 0, sc_conv_w[0].rearrange("t (c p) -> (t c) p", p=P), 48),
                (1, 48, pool_scale_2[0].rearrange("(c p) -> c p", p=P), 2),
                (1, 50, gdn_norm_w, 1),
                (1, 51, cmp_b1_2[0], 2),
                (2, 0, conv_w_2[0, 0:2].rearrange("t (c p) -> (t c) p", p=P), 88),
                (3, 0, conv_w_2[0, 2:3].rearrange("t (c p) -> (t c) p", p=P), 44),
                (3, 44, conv_b_2[0].rearrange("(c p) -> c p", p=P), 44),
                (4, 0, pre_norm_w.rearrange("l (c p) -> (l c) p", p=P), 16),
                (4, 16, post_norm_w.rearrange("l (c p) -> (l c) p", p=P), 16)]
            for n, w in enumerate((mix_norm_pre_2, mix_norm_post_2, mem_norm_pre_2, mem_norm_kv_2, mem_norm_post_2,
                                   ffn_norm_pre_2, ffn_norm_post_2)):
                par.append((4, 32 + 8 * n, w[0].rearrange("(c p) -> c p", p=P), 8))
            sp.dma_start(par_rows[53:54, 1, 0:DH], cmp_b2_2[0, 0:1]).then_inc(rows_in, 16)
            sp.dma_start(par_rows[53:54, 1, DH:P], cmp_b2_2[0, 0:1]).then_inc(rows_in, 16)
            for m, row, src, n in par:
                sp.dma_start(par_rows[row:row + n, m, :], src).then_inc(rows_in, 16)
            w_k = gdn_w_in[0].rearrange("(k p) c -> p k c", p=P)
            sp.dma_start(wba, w_k[:, :, 6144:6176]).then_inc(wba_in, 16)
            sp.dma_start(alog[:, 0, :], gdn_A_log.to_broadcast([P, VH])).then_inc(wba_in, 16)
            sp.dma_start(alog[:, 1, :], gdn_dt_bias.to_broadcast([P, VH])).then_inc(wba_in, 16)
            for g in range(GROUPS):
                for pos, c0 in enumerate((256 * g, QK_W + 256 * g, 2 * QK_W + 512 * g, 2 * QK_W + 512 * g + 256,
                                          4096 + 512 * g, 4096 + 512 * g + 256)):
                    load(pos, w_k[:, :, c0:c0 + 256], wide(256), 2)
            tall = lambda r: r[:, :].rearrange("p (k c) -> p k c", c=P)
            for n in range(KD):
                load(n % 6, gdn_w_out[0].rearrange("(k p) c -> p k c", p=P)[:, :, P * n:P * n + P], tall, 1)
            w_sc = sc_w_in[0].rearrange("(k p) c -> p k c", p=P)
            c0 = state_["chunks"]
            for pos in range(4):
                sp.wait_ge(chunk_done, held[pos])
            for i in passes(sp, SC // 256):
                for pos in range(4):
                    sp.wait_ge(chunk_done, c0 + 8 * i - 6 + 2 * pos)
                    sp.dma_start(ring[:, pos, :].rearrange("p (k c) -> p k c", k=KD),
                                 w_sc[:, :, ds(256 * i + SC * pos, 256)]).then_inc(slot_in[pos], 16)
            state_["chunks"] += 64
            for pos in range(4):
                held[pos] = state_["chunks"]
            for n in range(KD):
                load(n % 6, sc_w_out[0].rearrange("(k p) c -> p k c", p=P)[:, :, P * n:P * n + P], tall, 1)
            m0 = state_["chunks"]
            sp.dma_start(small[0:REL, 1:9], rel_bias_2).then_inc(rel_in, 16)
            sp.dma_start(inv_count, inv_d).then_inc(inv_in, 16)
            w_in = w_in_2[0].rearrange("(k p) c -> p k c", p=P)
            sp.wait_ge(chunk_done, m0 - 8)
            sp.dma_start(hot[0:REL + 1, :, :], hot_d.rearrange("b (a y) -> b a y", a=2)).then_inc(hot_in, 16)
            for a in range(2):
                sp.wait_ge(chunk_done, held[a])
                for f in range(2):
                    for c in range(2):
                        sp.dma_start(ring[:, a, :].rearrange("p (k c f d) -> p k c f d", k=KD, c=2, f=2)[:, :, c, f, :],
                                     w_in[:, :, 256 * f + 128 * a + 64 * c:256 * f + 128 * a + 64 * c + 64])\
                            .then_inc(slot_in[a], 16)
                held[a] = m0 + 2 * a + 2
            state_["chunks"] = m0 + 4
            load(2, w_in[:, :, 512:768], wide(256), 2)
            load(3, w_in[:, :, 768:1024], wide(256), 1)
            load(4, w_in[:, :, 1024:1280], wide(256), 1)
            load(5, w_in[:, :, 1304:1560], wide(256), 2)
            load(0, w_in[:, :, 1560:1816], wide(256), 2)
            load(1, w_in[:, :, 1816:2072], wide(256), 8)
            sp.wait_ge(x_ready, 16)
            sp.dma_start(w_gate, w_in[:, :, 1280:1304]).then_inc(mixer_in, 16)
            sp.dma_start(spatial_rows, sgu_w_2[0].rearrange("h t s -> t h s")).then_inc(mixer_in, 16)
            for n, v in enumerate((sgu_norm_g_2, sgu_norm_b_2)):
                sp.dma_start(sgu_gb[:, n, :], v.to_broadcast([P, 256])).then_inc(mixer_in, 16)
            for h in range(4):
                f = slice(64 * (h % 2), 64 * (h % 2) + 64)
                sp.dma_start(sgu_bias[f, h // 2, :], sgu_b_2[0, h:h + 1, :].to_broadcast([64, P])).then_inc(mixer_in, 16)
                sp.dma_start(w_pool[f, h // 2, :], pool_w_2[0, h]).then_inc(mixer_in, 16)
            sp.dma_start(w_c2, cmp_w2_2[0].rearrange("k h d -> h k d")).then_inc(mixer_in, 16)
            for g in range(2):
                sp.dma_start(b_c2[0:NC, g, :], cmp_b2_2[0, 1:2, :].to_broadcast([NC, DH])).then_inc(mixer_in, 16)
                sp.dma_start(pos_rows[0:64, 64 * g:64 * g + 64], cmp_pos_2[0].rearrange("k l d -> (k l) d")).then_inc(mixer_in, 16)
            sp.wait_ge(table_out, 4)
            sp.dma_start(row_copies, table[0:ATT_H, 1:2, 0:ROW_L].to_broadcast([ATT_H, P, ROW_L])).then_inc(table_stored, 16)
            sp.dma_start(cmp_copies, table[0:ATT_H, 0:1, 0:CMP_L].to_broadcast([ATT_H, NC, CMP_L])).then_inc(table_stored, 16)
            sp.wait_ge(table_stored, 32)
            sp.dma_start(bias_row, bass.AP(tensor=row_copies.tensor, offset=P - 1, ap=[[ROW_L - 1, P], [P * ROW_L, ATT_H], [1, S]]))\
                .then_inc(bias_in, 16)
            sp.dma_start(bias_cmp_T[0:NC, :, :],
                         bass.AP(tensor=cmp_copies.tensor, offset=480, ap=[[CMP_L - 16, NC], [NC * CMP_L, ATT_H], [1, S]]))\
                .then_inc(bias_in, 16)
            sp.wait_ge(chunk_done, m0 + 16)
            for g in range(2):
                sp.dma_start(ring[64 * g:64 * g + 64, 2:6, :].rearrange("d r (x h) -> d (r x) h", h=P),
                             cmp_w1_2[0].rearrange("k l d h -> d (k l) h")).then_inc(slot_in[2], 16)
            sp.wait_ge(hid_done, 2)
            state_["chunks"] = m0 + 20
            for n in range(4):
                held[2 + n] = m0 + 20
                load(n if n < 2 else n, w_out_2[0].rearrange("(k p) c -> p k c", p=P)[:, :, 256 * n:256 * n + 256], wide(256), 2)
            sp.wait_ge(attT_out, NT)
            sp.dma_start(mem_rows, mem_2[0].rearrange("(t p) c -> p t c", p=P)).then_inc(mem_in, 16)
            pos = 4
            for w in (w_mk_2, w_mv_2, w_mq_2):
                for n in range(4):
                    load(pos % 6, w[0].rearrange("(k p) c -> p k c", p=P)[:, :, 256 * n:256 * n + 256], wide(256), 2)
                    pos += 1
            state_["chunks"] += KD
            for n in range(4):
                load(pos % 6, w_mo_2[0].rearrange("(k p) c -> p k c", p=P)[:, :, 256 * n:256 * n + 256], wide(256), 2)
                pos += 1
            assert state_["chunks"] == FF0, state_
            w_u = w_up_2[0].rearrange("(k p) c -> p k c", p=P)

            def pair_load(jj, side):
                for v in range(2):
                    sp.wait_ge(chunk_done, FF0 + 4 * jj - 6 + 2 * v)
                    sp.dma_start(ring[:, 2 + 2 * side + v, :].rearrange("p (k c) -> p k c", k=KD),
                                 w_u[:, :, ds(256 * jj + FF * v, 256)]).then_inc(slot_in[2 + 2 * side + v], 16)

            for i in passes(sp, FK // 4):
                for side in range(2):
                    pair_load(2 * i + side, side)
            pair_load(FK // 2 - 1, 0)
            for n, c in ((4, 38), (5, 40), (2, 42), (3, 44)):
                held[n] = FF0 + c
            state_["chunks"] += 44
            w_d = w_down_2[0].rearrange("(k p) c -> p k c", p=P)
            for c in range(KD):
                for a in range(2):
                    pos = (2 * c + a) % 6
                    load(pos, w_d[:, FK // 2 * a:FK // 2 * (a + 1), P * c:P * c + P],
                         lambda r: r[:, 0:FK // 2 * P].rearrange("p (k c) -> p k c", c=P), 1 if a == 0 else 0)
            for t in range(NT):
                sp.wait_ge(final_act, t + 1)
                sp.wait_ge(final_dve, t + 1)
                sp.dma_start(out[0, t * P:(t + 1) * P, :], out_rows_sb[:, t, :]).then_inc(stored, 16)
            sp.wait_ge(stored, 16 * NT)

        @block.tensor
        def _(pe):
            st = {"chunk": 0, "loads": [0] * 6, "norm": 0, "x": 0}

            def slot_wait(pos, dmas=1):
                st["loads"][pos] += 16 * dmas
                pe.wait_ge(slot_in[pos], st["loads"][pos])

            def chunk(weights, kt, rhs, n_rhs, first=True, last=True, at=None):
                count, b = at if at else (st["chunk"], st["chunk"] % 4)
                if first and st["chunk"] >= 4:
                    pe.wait_ge(chunk_out, count - 3)
                for k in range(kt):
                    mm = pe.matmul(psum[b][:, 0:n_rhs], weights(k), rhs(k), start=(first and k == 0), stop=(last and k == kt - 1))
                if last:
                    mm.then_inc(chunk_done, 1)
                    if at is None:
                        st["chunk"] += 1

            def norm_sum():
                base = 8 * st["norm"]
                for k in range(KD):
                    norm_sum_tile(k)
                st["norm"] += 1

            def norm_sum_tile(k):
                base = 8 * st["norm"]
                pe.wait_ge(square_ready, base + k + 1)
                pe.matmul(psum[7][:, :], ones, sq[:, k % 2, :], start=(k == 0), stop=(k == KD - 1)).then_inc(square_used, 1)

            def post_norm_layer(out_chunk):
                for c in range(KD):
                    out_chunk(c)
                    if c >= 1:
                        norm_sum_tile(c - 1)
                norm_sum_tile(KD - 1)
                st["norm"] += 1

            pe.wait_ge(consts_in, 16)
            pe.wait_ge(rows_in, 16 * 19)
            for m, n in enumerate((128, 54, 88, 88, 88)):
                mm = pe.transpose(psum[m % 4][:, 0:n], par_rows[0:n, m, :], ident[0:n, 0:n])
                mm.then_inc(turned, 1)
                if m == 3:
                    pe.wait_ge(turned_used, 1)
            pe.wait_ge(x_in, 16)
            for k in range(KD):
                pe.wait_ge(turned_used, k + 2)
                for t in range(NT):
                    mm = pe.transpose(psum[(k + 1) % 4][:, t * P:(t + 1) * P], x_rows[:, t, k * P:(k + 1) * P], ident)
                mm.then_inc(turned, 1)
            norm_sum()
            pe.wait_ge(h_ready, 8)
            pe.wait_ge(wba_in, 48)
            for t in range(NT):
                for k in range(KD):
                    mm = pe.matmul(psum[4][:, 32 * t:32 * t + 32], hT[:, k, t * P:(t + 1) * P], wba[:, k, :],
                                   start=(k == 0), stop=(k == KD - 1))
            mm.then_inc(ba_done, 1)

            def token_sums():
                pe.wait_ge(tok_dve, 1)
                for n, m in enumerate((upper, same, half0, half1)):
                    mm = pe.matmul(psum[5][:, 64 * n:64 * n + 64], m, g_log, start=True, stop=True)
                mm.then_inc(cum_done, 1)

            for g in range(GROUPS):
                for n in range(12):
                    pos, side = n // 2, n % 2
                    if side == 0:
                        slot_wait(pos)
                    chunk(lambda k: ring[:, pos, k * 256 + side * P:k * 256 + side * P + P], KD, lambda k: hT[:, k, :], S)
                    if g == 0 and n == 1:
                        token_sums()
                for n in range(4):
                    pe.wait_ge(l2_sq, 4 * g + n + 1)
                    pe.matmul(psum[4 + n][:, :], ones, raw[:, n % 3, :] if n < 3 else decay[:, 0, :], start=True, stop=True).then_inc(l2_sum, 1)
                pe.wait_ge(qk_ready, 4 * g + 4)
                for j in range(2):
                    for n in range(2):
                        rhs = (k_T, q_T)[n]
                        for t in range(NT):
                            mm = pe.matmul(psum[4 + 2 * j + n][:, t * P:(t + 1) * P], k_T[:, j, t * P:(t + 1) * P],
                                           rhs[:, j, t * P:(t + 1) * P], start=True, stop=True)
                        mm.then_inc(kk_done, 1)
                for j in range(2):
                    pe.wait_ge(kk_ready, 4 * g + 2 * j + 1)
                    for t in range(NT):
                        mm = pe.transpose(psum[4 + 2 * j][:, t * P:(t + 1) * P], k_T[:, j, t * P:(t + 1) * P], ident)
                    mm.then_inc(kr_done, 1)
                for h in range(HG):
                    if h % 2 == 0:
                        pe.wait_ge(kr_ready, 2 * g + h // 2 + 1)
                    else:
                        pe.wait_ge(kk_ready, 4 * g + h + 1)
                    pe.wait_ge(silu_done, 8 * g + 8)
                    for t in range(NT):
                        mm = pe.transpose(psum[4 + h][:, t * P:(t + 1) * P], v_T[:, h, t * P:(t + 1) * P], ident)
                    mm.then_inc(vt_done, 1)
                pe.wait_ge(grp_ready, g + 1)
                for h in range(HG):
                    pe.wait_ge(vb_ready, 4 * g + h + 1)
                    for t in range(NT):
                        o = psum[4 + h][:, t * P:(t + 1) * P]
                        pe.matmul(o, grp[:, 0, 4 * t + h:4 * t + h + 1].to_broadcast([P, P]), upper, start=True, stop=False)
                        mm = pe.matmul(o, ident, negmask, start=False, stop=True)
                    mm.then_inc(gb_done, 1)
                for h in range(HG):
                    pe.wait_ge(decay_ready, 4 * g + h + 1)
                    for t in range(NT):
                        mm = pe.matmul(psum[4 + h][:, t * P:(t + 1) * P],
                                       grp[:, 1, 4 * t + h:4 * t + h + 1].to_broadcast([P, P]), ident, start=True, stop=True)
                    mm.then_inc(bb_done, 1)
                for pair in range(2):
                    for lv in range(5):
                        n0 = 20 * g + 10 * pair + 2 * lv
                        for j in range(2):
                            h = 2 * pair + j
                            if lv == 0:
                                pe.wait_ge(y_start, 4 * g + h + 1)
                            else:
                                pe.wait_ge(y_ready, n0 + j - 1)
                            for t in range(NT):
                                mm = pe.transpose(psum[4 + h][:, t * P:(t + 1) * P], Y_T[:, h, t * P:(t + 1) * P], ident)
                            mm.then_inc(xt_done, 1)
                        for j in range(2):
                            h = 2 * pair + j
                            pe.wait_ge(xt_ready, n0 + j + 1)
                            pe.wait_ge(level_ready, n0 + j + 1)
                            for t in range(NT):
                                mm = pe.matmul(psum[4 + h][:, t * P:(t + 1) * P], decay[:, j, t * P:(t + 1) * P],
                                               kk[:, j, t * P:(t + 1) * P], start=True, stop=True)
                            mm.then_inc(p_done, 1)
                        for j in range(2):
                            h = 2 * pair + j
                            pe.wait_ge(p_ready, n0 + j + 1)
                            for t in range(NT):
                                mm = pe.matmul(psum[4 + h][:, t * P:(t + 1) * P], kq[:, j, t * P:(t + 1) * P],
                                               Y_T[:, h, t * P:(t + 1) * P], start=True, stop=True)
                            mm.then_inc(py_done, 1)
                pe.wait_ge(y_ready, 20 * g + 20)
                for c in range(8):
                    rows, t = halves(c)
                    i = slice(CH * c, CH * c + CH)
                    n0 = 32 * g + 4 * c
                    for h in range(HG):
                        pe.wait_ge(state_ready, 36 * g + 4 * c + h + 1)
                        if c >= 1:
                            pe.wait_ge(scan_done, n0 + h - 3)
                        pe.matmul(psum[4 + h][rows, 0:P], k_T[:, h // 2, i], state[:, h, :], start=True, stop=True)
                        pe.matmul(psum[4 + h][rows, P:2 * P], q_T[:, h // 2, i], state[:, h, :], start=True, stop=True)\
                            .then_inc(ks_done, 1)
                    for h in range(HG):
                        pe.wait_ge(resid_ready, n0 + h + 1)
                        pe.matmul(psum[4 + h][rows, 0:P], Y_T[rows, h, i], resid[rows, h, :], start=True, stop=True)\
                            .then_inc(vn_done, 1)
                    for h in range(HG):
                        pe.wait_ge(vn_ready, n0 + h + 1)
                        pe.matmul(psum[4 + h][:, P:2 * P], k_rows[rows, h // 2, t * P:(t + 1) * P], v_dec[rows, h, :],
                                  start=True, stop=True)
                        pe.matmul(psum[4 + h][rows, 2 * P:3 * P], QK_T[rows, h, i], v_new[rows, h, :],
                                  start=True, stop=True).then_inc(su_done, 1)
                for h in range(HG):
                    pe.wait_ge(ssq_ready, 4 * g + h + 1)
                    for tt in range(NT):
                        mm = pe.transpose(psum[4 + h][:, tt * P:(tt + 1) * P], v_T[:, h, tt * P:(tt + 1) * P], ident)
                    mm.then_inc(ot_done, 1)
            pe.wait_ge(gate_ready, 16)

            def gdn_out(c):
                slot_wait(c % 6)
                chunk(lambda k: ring[:, c % 6, k * P:(k + 1) * P], VH, lambda k: gate_out[:, k, :], S)

            post_norm_layer(gdn_out)
            norm_sum()
            pe.wait_ge(h_ready, 16)
            for i in passes(pe, SC // 256):
                for n in range(8):
                    pos, side = n // 2, n % 2
                    if side == 0:
                        pe.wait_ge(slot_in[pos], st["loads"][pos] + 16 + 16 * i)
                    chunk(lambda k: ring[:, pos, k * 256 + side * P:k * 256 + side * P + P], KD, lambda k: hT[:, k, :], S,
                          at=(st["chunk"] + 8 * i + n, n % 4))
            st["chunk"] += 64
            for pos in range(4):
                st["loads"][pos] += 16 * 8

            def sc_proj(c):
                if c == 0:
                    pe.wait_ge(sc_used, SC // P + 1)
                slot_wait(c % 6)
                chunk(lambda k: ring[:, c % 6, k * P:(k + 1) * P], SC // P, lambda k: sc_out[:, k, :], S)

            post_norm_layer(sc_proj)
            pe.wait_ge(hot_in, 16)
            pe.wait_ge(rel_in, 16)
            pe.wait_ge(chunk_out, st["chunk"])
            for n in range(4):
                pe.matmul(psum[3 + n][0:ATT_H, :], rel, hot[0:REL + 1, n // 2, 512 * (n % 2):512 * (n % 2) + 512],
                          start=True, stop=True).then_inc(table_done, 1)
            pe.wait_ge(table_out, 4)
            norm_sum()
            pe.wait_ge(h_ready, 24)
            slab = lambda pos, c: (lambda k: ring[:, pos, k * 256 + c:k * 256 + c + P])
            whole = lambda k: hT[:, k, :]
            for n, (pos, c, w) in enumerate(((0, 0, 64), (0, 128, 0), (1, 0, 64), (1, 128, 0), (2, 0, 16), (2, 128, 0), (3, 0, 16),
                                             (4, 0, 16), (5, 0, 16), (5, 128, 0), (0, 0, 16), (0, 128, 0))):
                if w:
                    slot_wait(pos, w // 16)
                chunk(slab(pos, c), KD, whole, S)
            pe.wait_ge(mixer_in, MIXER_IN)
            for t in range(NT):
                b, tok_t = st["chunk"] % 4, slice(t * P, (t + 1) * P)
                pe.wait_ge(chunk_out, st["chunk"] - 3)
                for o, w in ((0, slab_rows(ring, 3, 128, 128)), (128, slab_rows(ring, 4, 128, 128)), (256, lambda k: w_gate[:, k, :])):
                    for k in range(KD):
                        mm = pe.matmul(psum[b][:, o:o + (24 if o == 256 else P)], hT[:, k, tok_t], w(k), start=(k == 0), stop=(k == KD - 1))
                mm.then_inc(chunk_done, 1)
                st["chunk"] += 1
            slot_wait(1)
            for t in range(NT):
                b, tok_t = st["chunk"] % 4, slice(t * P, (t + 1) * P)
                pe.wait_ge(chunk_out, st["chunk"] - 3)
                for k in range(KD):
                    mm = pe.matmul(psum[b][:, 0:256], hT[:, k, tok_t], ring[:, 1, k * 256:k * 256 + 256], start=(k == 0), stop=(k == KD - 1))
                mm.then_inc(chunk_done, 1)
                st["chunk"] += 1
            pe.transpose(psum[4][:, 0:64], pos_rows[0:64, :], ident[0:64, 0:64]).then_inc(turn_done, 1)
            for h in range(4):
                mm = pe.transpose(psum[5][:, h * P:(h + 1) * P], spatial_rows[:, h, :], ident)
            mm.then_inc(turn_done, 1)
            pe.wait_ge(bias_in, 32)
            for qi in range(NT):
                pe.wait_ge(turn_out, 1)
                for h in range(ATT_H):
                    mm = pe.transpose(psum[(6, 7, 4, 6)[qi]][:, NC * h:NC * h + NC], bias_cmp_T[0:NC, h, qi * P:(qi + 1) * P], ident[0:NC, 0:NC])
                mm.then_inc(turn_done, 1)
                if qi == 2:
                    pe.wait_ge(turn_out, 2)
            slot_wait(2, 2)
            w_c1 = ring[:, 2:6, :].rearrange("p r (x h) -> p (r x) h", h=P)
            blk = blocks.rearrange("p (l c) -> p l c", c=NC)
            for kind in range(2):
                pe.wait_ge(blocks_ready, kind + 1)
                pe.wait_ge(turn_out, 4)
                pe.wait_ge(mask_done, 1)
                for g in range(2):
                    f = slice(64 * g, 64 * g + 64)
                    for l in range(32):
                        mm = pe.matmul(psum[4 + g][:, 32 * kind:32 * kind + NC], w_c1[f, 32 * kind + l, :], blk[f, l, :],
                                       start=(l == 0), stop=(l == 31))
                mm.then_inc(hid_done, 1)
            pe.wait_ge(hid_ready, 1)
            pe.wait_ge(turn_out, 5)
            for g in range(2):
                pe.matmul(psum[6][64 * g:64 * g + 64, 0:NC], w_c2[:, 0, :], hidden[:, g, :], start=True, stop=True)
            for g in range(2):
                mm = pe.matmul(psum[7][0:NC, 64 * g:64 * g + 64], hidden[:, 2 + g, :], w_c2[:, 1, :], start=True, stop=True)
            mm.then_inc(c2_done, 1)
            pe.wait_ge(sgu_norm, 1)
            for pair in range(2):
                for n in range(NT):
                    for f in range(2):
                        h = 2 * pair + f
                        mm = pe.matmul(psum[4 + pair][64 * f:64 * f + 64, n * P:(n + 1) * P], sgu_v[:, n, 64 * h:64 * h + 64],
                                       spatial_T[:, h, :], start=True, stop=True)
            mm.then_inc(spatial_done, 1)
            pe.wait_ge(pool_ready, 1)
            pe.wait_ge(c2_ready, 1)
            for c in range(2):
                if c:
                    pe.wait_ge(pool_out, 1)
                for f in range(2):
                    r = slice(64 * f, 64 * f + 64)
                    mm = pe.matmul(psum[6 + f][r, :], w_pool[r, c, :], pool_d[r, c, :], start=True, stop=True)
                mm.then_inc(pool_done, 1)
            pe.wait_ge(chunk_out, st["chunk"])
            pe.wait_ge(sgu_done, 2)
            pe.wait_ge(pool_out, 2)

            def scores(n):
                qi, kind, h = units[n]
                need = n if is_cmp(n) or is_cmp(n - 1) else n - 1
                if need > 0:
                    pe.wait_ge(score_read, need)
                tok_q = slice(qi * P, (qi + 1) * P)
                if kind == 0:
                    for hh in range(ATT_H):
                        f = slice(64 * (hh // 4), 64 * (hh // 4) + 64)
                        mm = pe.matmul(psum[hh // 4][:, 32 * (hh % 4):32 * (hh % 4) + NC], att_q[f, hh % 4, tok_q], cmp_k[f, :],
                                       start=True, stop=True)
                else:
                    f = slice(64 * (h // 4), 64 * (h // 4) + 64)
                    mm = pe.matmul(psum[n % 2][:, 0:P * (qi + 1)], att_q[f, h % 4, tok_q], att_k[f, kind - 1, 0:P * (qi + 1)],
                                   start=True, stop=True)
                mm.then_inc(score_done, 1)

            def turn_probs(n):
                qi, kind, h = units[n]
                pe.wait_ge(prob_ready, n + 1)
                need = n if is_cmp(n) or is_cmp(n - 1) else n - 1
                if need > 0:
                    pe.wait_ge(probT_out, need)
                if kind == 0:
                    for hh in range(ATT_H):
                        mm = pe.transpose(psum[2 + hh // 4][0:NC, P * (hh % 4):P * (hh % 4) + P], cmp_prob[:, hh, :], ident)
                else:
                    for j in range(qi + 1):
                        mm = pe.transpose(psum[2 + n % 2][:, P * j:P * j + P], prob[:, n % 4, P * j:P * j + P], ident)
                mm.then_inc(probT_done, 1)

            def values(n):
                qi, kind, h = units[n]
                pe.wait_ge(probT_out, n + 1)
                if qi and h == 0:
                    pe.wait_ge(combined, qi)
                if kind == 0:
                    pt = prob_T.rearrange("p a (h i) -> p (a h) i", i=P)
                    for hh in range(ATT_H):
                        mm = pe.matmul(psum[4][:, DH * hh:DH * hh + DH], pt[0:NC, hh, :], cmp_v[0:NC, 64 * (hh // 4):64 * (hh // 4) + 64],
                                       start=True, stop=True)
                else:
                    v0 = 128 * (kind - 1) + 64 * (h // 4)
                    for j in range(qi + 1):
                        mm = pe.matmul(psum[4 + kind][:, DH * h:DH * h + DH], prob_T[:, n % 2, P * j:P * j + P], att_v[:, j, v0:v0 + 64],
                                       start=(j == 0), stop=(j == qi))
                mm.then_inc(pv_done, 1)

            def turn_out_rows(qi):
                pe.wait_ge(combined, qi + 1)
                if qi:
                    pe.wait_ge(attT_out, qi)
                for c in range(4):
                    mm = pe.transpose(psum[7][:, c * P:(c + 1) * P], att_o[:, 0, c * P:(c + 1) * P], ident)
                mm.then_inc(attT_done, 1)

            for n in range(len(units) + 3):
                if n < len(units):
                    scores(n)
                if 0 <= n - 2 < len(units):
                    turn_probs(n - 2)
                if n >= 3:
                    values(n - 3)
                if n >= 22 and (n - 5) % 17 == 0:
                    turn_out_rows((n - 5) // 17 - 1)
            turn_out_rows(NT - 1)
            pe.wait_ge(attT_out, NT)

            def mix_proj(c):
                if c % 2 == 0:
                    slot_wait(c // 2)
                chunk(slab(c // 2, 128 * (c % 2)), KD, lambda k: mix_T[:, k, :], S)

            post_norm_layer(mix_proj)
            pe.wait_ge(mem_scaled, 1)
            for k in range(KD):
                if k >= 2:
                    pe.wait_ge(mem_turned_out, k - 1)
                for t in range(MT):
                    mm = pe.transpose(psum[4 + k % 2][:, t * P:(t + 1) * P], mem_rows[:, t, k * P:(k + 1) * P], ident)
                mm.then_inc(mem_turned, 1)
            pe.wait_ge(mem_turned_out, KD)
            pos = 4
            for n in range(4):
                slot_wait(pos % 6)
                for side in range(2):
                    chunk(slab(pos % 6, 128 * side), KD, lambda k: mem_T[:, k, :], MEM)
                pos += 1
            for n in range(4):
                slot_wait(pos % 6)
                for t in range(MT):
                    chunk(lambda k: mem_T[:, k, t * P:(t + 1) * P], KD, lambda k: ring[:, pos % 6, k * 256:k * 256 + 256], 256)
                pos += 1
            norm_sum()
            pe.wait_ge(h_ready, 32)
            for n in range(4):
                slot_wait(pos % 6)
                for side in range(2):
                    chunk(slab(pos % 6, 128 * side), KD, whole, S)
                pos += 1
            pe.wait_ge(chunk_out, st["chunk"])
            for n in range(len(mem_units) + 3):
                if n < len(mem_units):
                    h, qi = mem_units[n]
                    if n >= 2:
                        pe.wait_ge(mp_exp, n - 1)
                    for c in range(2):
                        mm = pe.matmul(psum[4 + n % 2][:, 0:MEM], mem_q[:, 2 * h + c, qi * P:(qi + 1) * P], mem_k[:, 2 * h + c, :],
                                       start=(c == 0), stop=(c == 1))
                    mm.then_inc(ms_done, 1)
                m = n - 2
                if 0 <= m < len(mem_units):
                    pe.wait_ge(mp_ready, m + 1)
                    if m >= 2:
                        pe.wait_ge(mpT_out, m - 1)
                    for t in range(MT):
                        mm = pe.transpose(psum[6 + m % 2][:, t * P:(t + 1) * P], mem_prob[:, m % 4, t * P:(t + 1) * P], ident)
                    mm.then_inc(mpT_done, 1)
                m = n - 3
                if m >= 0 and m % 4 == 3:
                    h = m // 4
                    pe.wait_ge(mpT_out, m + 1)
                    for c in range(2):
                        chunk(lambda t: mem_v[:, t, HD * h + P * c:HD * h + P * c + P], MT, lambda t: mem_probT[:, 2 * (h % 2) + t, :], S)
            pe.wait_ge(chunk_out, st["chunk"])

            def mem_proj(c):
                if c % 2 == 0:
                    slot_wait((pos + c // 2) % 6)
                chunk(slab((pos + c // 2) % 6, 128 * (c % 2)), KD, lambda k: mem_out[:, k, :], S)

            post_norm_layer(mem_proj)
            norm_sum()
            pe.wait_ge(h_ready, 40)
            assert st["chunk"] == FF0, st

            def pair_proj(jj, side, i):
                for v in range(2):
                    pos = 2 + 2 * side + v
                    pe.wait_ge(slot_in[pos], st["loads"][pos] + 16 + 16 * i)
                    for s in range(2):
                        chunk(slab(pos, 128 * s), KD, whole, S, at=(FF0 + 4 * jj + 2 * v + s, 2 * v + s))

            for i in passes(pe, FK // 4):
                for side in range(2):
                    pair_proj(2 * i + side, side, i)
            pair_proj(FK // 2 - 1, 0, FK // 4)
            for pos, n in ((2, 6), (3, 6), (4, 5), (5, 5)):
                st["loads"][pos] += 16 * n
            st["chunk"] += 2 * FK

            def down(c):
                for a in range(2):
                    pos = (2 * c + a) % 6
                    slot_wait(pos)
                    if c == 0:
                        pe.wait_ge(ff_ready, 12 if a == 0 else FK)
                    chunk(lambda k: ring[:, pos, k * P:(k + 1) * P], FK // 2, lambda k: ff_hid[:, FK // 2 * a + k, :], S,
                          first=(a == 0), last=(a == 1))

            post_norm_layer(down)
            pe.wait_ge(x_ready, 40)
            for t in range(NT):
                for a in range(2):
                    for k in range(4):
                        mm = pe.transpose(psum[2 * t + a][:, k * P:(k + 1) * P], xT[:, 4 * a + k, t * P:(t + 1) * P], ident)
                    mm.then_inc(final_done, 1)

        @block.scalar
        def _(act):
            own = Tally(act, act_step)
            st = {"chunk": 0, "norm": 0, "x": 8}

            def inverse_rms(bank, out_, scale, done, tmp=None):
                own.did(act.activation(out_, bank, ACT.Ln, bias=eps, scale=scale))
                own.settle()
                act.activation(out_, out_, ACT.Exp, scale=-0.5).then_inc(done, 1)

            def square_tile(k, src):
                n = 8 * st["norm"] + k
                if n >= 2:
                    act.wait_ge(square_used, n - 1)
                act.activation(sq[:, k % 2, :], src, ACT.Square).then_inc(square_ready, 1)

            def norm_rms():
                act.wait_ge(square_used, 8 * st["norm"] + 8)
                if st["norm"] >= 1:
                    pre, post = (st["norm"] + 1) // 2, st["norm"] // 2
                    act.wait_ge(h_ready, 8 * pre)
                    if post:
                        act.wait_ge(x_ready, 8 * post)
                inverse_rms(psum[7][:, :], rs[:, :], 1.0 / D, rms_ready)
                st["norm"] += 1

            def pre_norm():
                act.wait_ge(x_ready, 8 * (st["norm"] // 2))
                for k in range(KD):
                    square_tile(k, xT[:, k, :])
                norm_rms()

            def post_norm(y_T=y_T):
                for k in range(KD):
                    n = st["chunk"]
                    act.wait_ge(chunk_done, n + 1)
                    square_tile(k, psum[n % 4][:, :])
                    act.activation(y_T[:, k, :], psum[n % 4][:, :], ACT.Copy).then_inc(chunk_out, 1)
                    st["chunk"] += 1
                norm_rms()

            for m, n in enumerate((128, 54, 88, 88, 88)):
                act.wait_ge(turned, m + 1)
                act.activation(cols[:, m, 0:n], psum[m % 4][:, 0:n], ACT.Copy).then_inc(turned_used, 1)
            for k in range(KD):
                act.wait_ge(turned, 6 + k)
                act.activation(xT[:, k, :], psum[(k + 1) % 4][:, :], ACT.Copy).then_inc(turned_used, 1)
            act.wait_ge(turned_used, 13)
            act.wait_ge(eps_set, 2)
            for k in range(KD):
                square_tile(k, xT[:, k, :])
            norm_rms()
            act.wait_ge(tok_act, 1)
            own.did(act.activation(beta, tmpA, ACT.Exp, scale=-1.0))
            own.settle()
            own.did(act.activation(tmpA, tmpB, ACT.Exp, scale=-1.0))
            own.settle()
            own.did(act.activation(tmpA, tmpA, ACT.Ln, bias=1.0))
            act.activation(alog[:, 0, :], alog[:, 0, :], ACT.Exp).then_inc(tok_exp, 1)

            def token_exps():
                act.wait_ge(tok_act, 2)
                own.did(act.activation(e_G, G_cum, ACT.Exp))
                own.did(act.activation(e_rest, tmpB, ACT.Exp))
                own.did(act.activation(end0, end0, ACT.Exp))
                act.activation(end1, end1, ACT.Exp).then_inc(tok_exp, 1)
            for g in range(GROUPS):
                def silu(n, dst):
                    act.wait_ge(conv_done, 8 * g + n + 1)
                    act.activation(dst, dst, ACT.Silu).then_inc(silu_done, 1)
                dsts = [q_T[:, 0, :], q_T[:, 1, :], k_T[:, 0, :], k_T[:, 1, :]] + [v_T[:, h, :] for h in range(HG)]
                for n in range(12):
                    c = st["chunk"]
                    act.wait_ge(chunk_done, c + 1)
                    if n < 8:
                        if 8 * g + n >= 3:
                            act.wait_ge(conv_done, 8 * g + n - 2)
                        if n == 0 and g:
                            act.wait_ge(qk_ready, 4 * g)
                        act.activation(raw[:, n % 3, :], psum[c % 4][:, :], ACT.Copy).then_inc(chunk_out, 1)
                    else:
                        if g and n == 8:
                            act.wait_ge(gate_ready, 4 * g)
                        act.activation(z_T[:, n - 8, :], psum[c % 4][:, :], ACT.Silu).then_inc(chunk_out, 1)
                    if g == 0 and n == 3:
                        token_exps()
                    st["chunk"] += 1
                    if 1 <= n <= 8:
                        silu(n - 1, dsts[n - 1])
                for n in range(4):
                    act.wait_ge(l2_sum, 4 * g + n + 1)
                    inverse_rms(psum[4 + n][:, :], (raw[:, n, :] if n < 3 else decay[:, 0, :]), 1.0, l2_rms)
                for n in range(4):
                    act.wait_ge(kk_done, 4 * g + n + 1)
                    dst = (kk, kq)[n % 2][:, n // 2, :]
                    act.activation(dst, psum[4 + n][:, :], ACT.Copy).then_inc(kk_ready, 1)
                for j in range(2):
                    act.wait_ge(kr_done, 2 * g + j + 1)
                    act.activation(k_rows[:, j, :], psum[4 + 2 * j][:, :], ACT.Copy).then_inc(kr_ready, 1)
                for h in range(HG):
                    act.wait_ge(gb_done, 4 * g + h + 1)
                    act.wait_ge(grp_ready, g + 1)
                    if h >= 2:
                        act.wait_ge(decay_used, 4 * g + h - 1)
                    for t in range(NT):
                        col = neg_G[:, 16 * t + 4 * g + h:16 * t + 4 * g + h + 1]
                        ins = act.activation(decay[:, h % 2, t * P:(t + 1) * P], psum[4 + h][:, t * P:(t + 1) * P],
                                             ACT.Exp, bias=col)
                    ins.then_inc(decay_ready, 1)
                for pair in range(2):
                    for lv in range(5):
                        n0 = 20 * g + 10 * pair + 2 * lv
                        for j in range(2):
                            act.wait_ge(xt_done, n0 + j + 1)
                            if lv or pair:
                                act.wait_ge(p_done, n0 + j - 1)
                            act.activation(kk[:, j, :], psum[4 + 2 * pair + j][:, :], ACT.Copy).then_inc(xt_ready, 1)
                        for j in range(2):
                            act.wait_ge(p_done, n0 + j + 1)
                            act.wait_ge(py_done, n0 + j - 1) if (lv or pair) else None
                            act.activation(kq[:, j, :], psum[4 + 2 * pair + j][:, :], ACT.Copy).then_inc(p_ready, 1)
                for c in range(8):
                    rows, t = halves(c)
                    n0 = 32 * g + 4 * c
                    for h in range(HG):
                        col = 16 * t + 4 * g + h
                        act.wait_ge(vn_done, n0 + h + 1)
                        if c:
                            act.wait_ge(su_done, n0 + h - 3)
                        act.activation(v_new[rows, h, :], psum[4 + h][rows, 0:P], ACT.Copy)
                        act.activation(v_dec[rows, h, :], psum[4 + h][rows, 0:P], ACT.Copy,
                                       scale=e_rest[rows, col:col + 1]).then_inc(vn_ready, 1)
                for h in range(HG):
                    act.wait_ge(scan_done, 32 * g + 32)
                    act.wait_ge(vn_ready, 32 * g + 32)
                    for t in range(NT):
                        own.did(act.activation(A_T[:, h, t * P:(t + 1) * P], v_T[:, h, t * P:(t + 1) * P], ACT.Square,
                                               accum_out=ssq[:, 0, 4 * h + t:4 * h + t + 1]))
                own.settle()
                own.did(act.activation(ssq[:, 1, :], ssq[:, 0, :], ACT.Ln, bias=eps, scale=1.0 / P))
                own.settle()
                act.activation(ssq[:, 1, :], ssq[:, 1, :], ACT.Exp, scale=-0.5).then_inc(l2_rms, 1)
            post_norm()
            pre_norm()
            for i in passes(act, SC // 256):
                for n in range(8):
                    act.wait_ge(chunk_done, st["chunk"] + 8 * i + n + 1)
                    if n == 0:
                        act.wait_ge(sc_used, 2 * i + 1)
                    act.activation(sc_in[:, n, :], psum[n % 4][:, :], ACT.Silu if n >= 6 else ACT.Copy).then_inc(chunk_out, 1)
            st["chunk"] += 64
            post_norm()
            for n in range(4):
                act.wait_ge(table_done, n + 1)
                act.activation(table[0:ATT_H, n // 2, 512 * (n % 2):512 * (n % 2) + 512], psum[3 + n][0:ATT_H, :], ACT.Copy)\
                    .then_inc(table_out, 1)
            pre_norm()
            m0 = st["chunk"]
            act.wait_ge(x_ready, 16)
            dst = [att_q[:, n, :] for n in range(4)] + [cmp_kv[:, 0, :], cmp_kv[:, 1, :], att_k[:, 0, :], att_k[:, 1, :],
                                                        pool_x[:, 0, :], pool_x[:, 1, :], sgu_u[:, 0, :], sgu_u[:, 1, :]]
            for n in range(12):
                act.wait_ge(chunk_done, m0 + n + 1)
                act.activation(dst[n], psum[n % 4][:, :], ACT.Gelu_apprx_tanh if n >= 10 else ACT.Copy,
                               scale=DH ** -0.5 if n < 4 else 1.0).then_inc(chunk_out, 1)
            for t in range(NT):
                act.wait_ge(chunk_done, m0 + 13 + t)
                act.activation(att_v[:, t, :], psum[t % 4][:, 0:256], ACT.Copy)
                act.activation(gate_raw[:, t, :], psum[t % 4][:, 256:280], ACT.Copy).then_inc(chunk_out, 1)
            for t in range(NT):
                act.wait_ge(chunk_done, m0 + 17 + t)
                act.activation(sgu_v[:, t, :], psum[t % 4][:, 0:256], ACT.Gelu_apprx_tanh).then_inc(chunk_out, 1)
            st["chunk"] += 20
            act.wait_ge(chunk_out, m0 + 16)
            act.activation(gate, gate_raw, ACT.Exp, scale=-1.0).then_inc(gate_exp, 1)
            act.wait_ge(turn_done, 1)
            act.activation(pos_T, psum[4][:, 0:64], ACT.Copy).then_inc(turn_out, 1)
            for qi in range(NT):
                act.wait_ge(turn_done, 3 + qi)
                act.activation(bias_cmp[:, qi, :], psum[(6, 7, 4, 6)[qi]][:, 0:ATT_H * NC], ACT.Copy).then_inc(turn_out, 1)
            for kind in range(2):
                act.wait_ge(hid_done, kind + 1)
            for kind in range(2):
                for g in range(2):
                    ins = act.activation(hidden[:, 2 * kind + g, :], psum[4 + g][:, 32 * kind:32 * kind + NC], ACT.Gelu_apprx_tanh,
                                         bias=cols[:, 1, 51 + kind:52 + kind])
            ins.then_inc(hid_ready, 1)
            act.wait_ge(var_ready, 1)
            own.did(act.activation(small[:, 5:9], small[:, 5:9], ACT.Ln, bias=eps, scale=1.0 / 256))
            own.settle()
            act.activation(small[:, 5:9], small[:, 5:9], ACT.Exp, scale=-0.5).then_inc(rstd_ready, 1)
            for c in range(2):
                act.wait_ge(pool_done, c + 1)
                for f in range(2):
                    r = slice(64 * f, 64 * f + 64)
                    ins = act.activation(mix_T[r, 4 + c, :], psum[6 + f][r, :], ACT.Copy, scale=PSC(c)[r])
                ins.then_inc(pool_out, 1)

            def out_rows(qi):
                act.wait_ge(attT_done, qi + 1)
                act.activation(mix_T[:, 0:4, qi * P:(qi + 1) * P], psum[7][:, :].rearrange("p (c i) -> p c i", c=4), ACT.Copy)\
                    .then_inc(attT_out, 1)

            for n in range(len(units)):
                qi, kind, h = units[n]
                act.wait_ge(score_read, n + 1)
                if kind == 0:
                    act.activation(cmp_prob, cmp_prob, ACT.Exp).then_inc(prob_ready, 1)
                else:
                    if qi >= 2:
                        act.wait_ge(combined, qi - 1)
                    p = prob[:, n % 4, 0:P * (qi + 1)]
                    act.activation(p, p, ACT.Exp, bias=neg_max(n), accum_out=sums(qi, kind)[:, h:h + 1]).then_inc(prob_ready, 1)
                if n >= 22 and (n - 5) % 17 == 0:
                    out_rows((n - 5) // 17 - 1)
            out_rows(NT - 1)
            post_norm()
            act.wait_ge(mem_in, 16)
            for t in range(MT):
                own.did(act.activation(mem_junk, mem_rows[:, t, :], ACT.Square, accum_out=small[:, 1 + t:2 + t]))
                own.settle()
            own.did(act.activation(small[:, 1:3], small[:, 1:3], ACT.Ln, bias=eps, scale=1.0 / D))
            own.settle()
            act.activation(small[:, 1:3], small[:, 1:3], ACT.Exp, scale=-0.5).then_inc(mem_rstd, 1)
            for k in range(KD):
                act.wait_ge(mem_turned, k + 1)
                act.activation(mem_T[:, k, :], psum[4 + k % 2][:, 0:MEM], ACT.Copy, scale=KVW(k)).then_inc(mem_turned_out, 1)
            for c in range(KD):
                act.wait_ge(chunk_done, st["chunk"] + 1)
                act.activation(mem_k[:, c, :], psum[st["chunk"] % 4][:, 0:MEM], ACT.Copy).then_inc(chunk_out, 1)
                st["chunk"] += 1
            for n in range(4):
                for t in range(MT):
                    act.wait_ge(chunk_done, st["chunk"] + 1)
                    act.activation(mem_v[:, t, 256 * n:256 * n + 256], psum[st["chunk"] % 4][:, 0:256], ACT.Copy).then_inc(chunk_out, 1)
                    st["chunk"] += 1
            pre_norm()
            for c in range(KD):
                act.wait_ge(chunk_done, st["chunk"] + 1)
                act.activation(mem_q[:, c, :], psum[st["chunk"] % 4][:, :], ACT.Copy).then_inc(chunk_out, 1)
                st["chunk"] += 1
            pv0 = st["chunk"]
            for n in range(len(mem_units) + 4):
                if n < len(mem_units):
                    act.wait_ge(ms_max, n + 1)
                    if n >= 4:
                        act.wait_ge(mpT_done, n - 3)
                    act.activation(mem_prob[:, n % 4, :], psum[4 + n % 2][:, 0:MEM], ACT.Exp, bias=mem_max(n), scale=HD ** -0.5,
                                   accum_out=mem_sum(n)).then_inc(mp_exp, 1)
                m = n - 2
                if 0 <= m < len(mem_units):
                    h, qi = mem_units[m]
                    act.wait_ge(mpT_done, m + 1)
                    if h >= 2:
                        act.wait_ge(chunk_done, pv0 + 2 * (h - 1))
                    act.activation(mem_probT[:, 2 * (h % 2):2 * (h % 2) + 2, qi * P:(qi + 1) * P],
                                   psum[6 + m % 2][:, 0:MEM].rearrange("p (t i) -> p t i", t=MT), ACT.Copy).then_inc(mpT_out, 1)
                m = n - 4
                if m >= 0 and m % 4 == 3:
                    for c in range(2):
                        act.wait_ge(chunk_done, st["chunk"] + 1)
                        act.activation(mem_out[:, 2 * (m // 4) + c, :], psum[st["chunk"] % 4][:, :], ACT.Copy).then_inc(chunk_out, 1)
                        st["chunk"] += 1
            post_norm()
            pre_norm()

            def pair_act(jj):
                for n in range(4):
                    act.wait_ge(chunk_done, FF0 + 4 * jj + n + 1)
                    if n == 0:
                        act.wait_ge(ff_conv, 4 * jj + 1)
                    act.activation(ff_raw[:, n, :], psum[n][:, :], ACT.Copy).then_inc(chunk_out, 1)
                    if n >= 2:
                        act.wait_ge(ff_conv, 4 * jj + n)
                        act.activation(ff_gate[:, n - 2, :], ff_gate[:, n - 2, :], ACT.Gelu_apprx_tanh).then_inc(ff_gelu, 1)

            for i in passes(act, FK // 2):
                pair_act(i)
            st["chunk"] += 2 * FK
            post_norm(ff_y)
            act.wait_ge(chunk_done, FF0 + 52)
            for t in range(NT):
                act.wait_ge(final_done, 2 * t + 1)
                act.activation(out_rows_sb[:, t, 0:512], psum[2 * t][:, :], ACT.Copy).then_inc(final_act, 1)

        @block.vector
        def _(dve):
            own = Tally(dve, dve_step)
            st = {"pre": 0, "post": 0}

            def pre_norm():
                n = st["pre"] + st["post"]
                dve.wait_ge(rms_ready, n + 1)
                for k in range(KD):
                    dve.scalar_tensor_tensor(out=hT[:, k, :], in0=xT[:, k, :], scalar=PRE[st["pre"]](k), in1=rs[:, :],
                                             op0=ALU.mult, op1=ALU.mult).then_inc(h_ready, 1)
                st["pre"] += 1

            def post_norm(y_T=y_T):
                n = st["pre"] + st["post"]
                dve.wait_ge(rms_ready, n + 1)
                for k in range(KD):
                    own.did(dve.scalar_tensor_tensor(out=y_T[:, k, :], in0=y_T[:, k, :], scalar=POST[st["post"]](k),
                                                     in1=rs[:, :], op0=ALU.mult, op1=ALU.mult))
                own.settle()
                for k in range(KD):
                    dve.tensor_tensor(xT[:, k, :], xT[:, k, :], y_T[:, k, :], ALU.add).then_inc(x_ready, 1)
                st["post"] += 1

            def conv(dst, src, taps, weight, bias=None):
                w = weight(taps - 1)
                if bias is None:
                    own.did(dve.tensor_scalar(dst, src, w, None, ALU.mult))
                else:
                    own.did(dve.tensor_scalar(dst, src, w, bias, ALU.mult, ALU.add))
                for s in range(1, taps):
                    own.settle()
                    ins = dve.scalar_tensor_tensor(out=dst[:, s:S], in0=src[:, 0:S - s], scalar=weight(taps - 1 - s),
                                                   in1=dst[:, s:S], op0=ALU.mult, op1=ALU.add)
                    if s < taps - 1:
                        own.did(ins)
                return ins

            dve.memset(small[:, :], NEG).then_inc(eps_set, 1)
            dve.wait_ge(eps_set, 1)
            dve.memset(eps, EPS).then_inc(eps_set, 1)
            dve.wait_ge(turned_used, 13)
            pre_norm()
            dve.wait_ge(ba_done, 1)
            lg = psum[4][:, 0:128].rearrange("p (t c) -> p t c", t=NT)
            own.did(dve.tensor_copy(R4(tmpA), lg[:, :, 0:16]))
            own.did(dve.tensor_tensor(R4(g_log), lg[:, :, 16:32], alog[:, 1:2, :].to_broadcast([P, NT, VH]), ALU.add))
            own.settle()
            own.did(dve.tensor_scalar(tmpB, g_log, -1.0, None, ALU.mult))
            own.settle()
            dve.tensor_tensor(tmpB, tmpB, g_log, ALU.max).then_inc(tok_act, 1)
            dve.wait_ge(tok_exp, 1)
            own.did(dve.tensor_scalar(beta, beta, 1.0, None, ALU.add))
            own.settle()
            own.did(dve.reciprocal(beta, beta))
            own.did(dve.scalar_tensor_tensor(out=tmpA, in0=g_log, scalar=0.0, in1=tmpA, op0=ALU.max, op1=ALU.add))
            own.settle()
            own.did(dve.tensor_scalar(tmpA, tmpA, -1.0, None, ALU.mult))
            own.settle()
            dve.tensor_tensor(R4(g_log), R4(tmpA), alog[:, 0:1, :].to_broadcast([P, NT, VH]), ALU.mult).then_inc(tok_dve, 1)

            def token_columns():
                dve.wait_ge(cum_done, 1)
                own.did(dve.tensor_copy(G_cum, psum[5][:, 0:64]))
                own.did(dve.tensor_copy(G_end, psum[5][:, 64:128]))
                own.did(dve.tensor_copy(end0, psum[5][:, 128:192]))
                own.did(dve.tensor_copy(end1, psum[5][:, 192:256]))
                own.settle()
                own.did(dve.tensor_scalar(neg_G, G_cum, -1.0, None, ALU.mult))
                own.settle()
                dve.tensor_tensor(tmpB, G_end, G_cum, ALU.subtract).then_inc(tok_act, 1)

            def token_products():
                dve.wait_ge(tok_exp, 2)
                own.did(dve.tensor_tensor(neg_bG, beta, e_G, ALU.mult))
                own.settle()
                own.did(dve.tensor_scalar(neg_bG, neg_bG, -1.0, None, ALU.mult))
                own.settle()

            for g in range(GROUPS):
                dsts = [q_T[:, 0, :], q_T[:, 1, :], k_T[:, 0, :], k_T[:, 1, :]] + [v_T[:, h, :] for h in range(HG)]
                chans = [2 * g, 2 * g + 1, 8 + 2 * g, 9 + 2 * g] + [16 + 4 * g + h for h in range(HG)]
                if g:
                    dve.wait_ge(su_done, 32 * g)
                    dve.wait_ge(ot_done, 4 * g)
                for n in range(8):
                    dve.wait_ge(chunk_out, 12 * g + n + 1)
                    conv(dsts[n], raw[:, n % 3, :], TAPS, lambda tap: GCONV(tap, chans[n])).then_inc(conv_done, 1)
                    if g == 0 and n == 1:
                        token_columns()
                if g == 0:
                    token_products()
                own.did(dve.tensor_copy(grp[:, 0, :].rearrange("p (t h) -> p t h", t=NT), R4(g_log)[:, :, 4 * g:4 * g + 4]))
                own.settle()
                dve.tensor_copy(grp[:, 1, :].rearrange("p (t h) -> p t h", t=NT), R4(beta)[:, :, 4 * g:4 * g + 4]).then_inc(grp_ready, 1)
                sqs = [raw[:, 0, :], raw[:, 1, :], raw[:, 2, :], decay[:, 0, :]]
                dve.wait_ge(silu_done, 8 * g + 8)
                dve.wait_ge(conv_done, 8 * g + 8)
                for n in range(4):
                    dve.tensor_tensor(sqs[n], dsts[n], dsts[n], ALU.mult).then_inc(l2_sq, 1)
                for n in range(4):
                    dve.wait_ge(l2_rms, 5 * g + n + 1)
                    dve.scalar_tensor_tensor(out=dsts[n], in0=dsts[n], scalar=(float(P) ** -0.5 if n < 2 else 1.0),
                                             in1=sqs[n], op0=ALU.mult, op1=ALU.mult).then_inc(qk_ready, 1)
                for h in range(HG):
                    dve.wait_ge(vt_done, 4 * g + h + 1)
                    b = R4(beta)[:, :, 4 * g + h:4 * g + h + 1].to_broadcast([P, NT, P])
                    dve.tensor_tensor(R2(v_T[:, h, :]), R2(psum[4 + h][:, :]), b, ALU.mult).then_inc(vb_ready, 1)
                for h in range(HG):
                    dve.wait_ge(decay_ready, 4 * g + h + 1)
                    dve.wait_ge(kk_ready, 4 * g + 4)
                    own.did(dve.tensor_tensor(QK_T[:, h, :], kq[:, h // 2, :], decay[:, h % 2, :], ALU.mult))
                    dve.tensor_tensor(A_T[:, h, :], kk[:, h // 2, :], decay[:, h % 2, :], ALU.mult).then_inc(decay_used, 1)
                for h in range(HG):
                    dve.wait_ge(bb_done, 4 * g + h + 1)
                    dve.wait_ge(decay_used, 4 * g + h + 1)
                    own.did(dve.tensor_tensor(A_T[:, h, :], A_T[:, h, :], psum[4 + h][:, :], ALU.mult))
                    own.settle()
                    own.did(dve.tensor_tensor(R2(Y_T[:, h, :]), R2(A_T[:, h, :]), masks[:, 3:4, :].to_broadcast([P, NT, P]), ALU.mult))
                    own.settle()
                    dve.tensor_tensor(R2(Y_T[:, h, :]), R2(Y_T[:, h, :]), masks[:, 0:1, :].to_broadcast([P, NT, P]),
                                      ALU.add).then_inc(y_start, 1)
                for pair in range(2):
                    for lv in range(5):
                        n0 = 20 * g + 10 * pair + 2 * lv
                        for j in range(2):
                            h = 2 * pair + j
                            dve.wait_ge(py_done, n0 + j + 1)
                            dve.tensor_tensor(Y_T[:, h, :], Y_T[:, h, :], psum[4 + h][:, :], ALU.add).then_inc(y_ready, 1)
                for h in range(HG):
                    dve.memset(state[:, h, :], 0.0).then_inc(state_ready, 1)
                for c in range(8):
                    rows, t = halves(c)
                    n0 = 32 * g + 4 * c
                    end = (end0, end1)[c % 2]
                    written = []
                    for h in range(HG + 1):
                        if h < HG:
                            col = 16 * t + 4 * g + h
                            dve.wait_ge(ks_done, n0 + h + 1)
                            written.append(own.did(dve.scalar_tensor_tensor(
                                out=resid[rows, h, :], in0=psum[4 + h][rows, 0:P], scalar=neg_bG[rows, col:col + 1],
                                in1=v_T[rows, h, t * P:(t + 1) * P], op0=ALU.mult, op1=ALU.add)))
                        if h:
                            col = 16 * t + 4 * g + h - 1
                            dve.wait_ge(dve_step, written[h - 1])
                            dve.tensor_scalar(v_T[rows, h - 1, t * P:(t + 1) * P], psum[3 + h][rows, P:2 * P],
                                              e_G[rows, col:col + 1], None, ALU.mult).then_inc(resid_ready, 1)
                    for h in range(HG):
                        col = 16 * t + 4 * g + h
                        dve.wait_ge(su_done, n0 + h + 1)
                        dve.scalar_tensor_tensor(out=state[:, h, :], in0=state[:, h, :], scalar=end[:, col:col + 1],
                                                 in1=psum[4 + h][:, P:2 * P], op0=ALU.mult, op1=ALU.add).then_inc(state_ready, 1)
                        dve.wait_ge(resid_ready, n0 + h + 1)
                        dve.tensor_tensor(v_T[rows, h, t * P:(t + 1) * P], v_T[rows, h, t * P:(t + 1) * P],
                                          psum[4 + h][rows, 2 * P:3 * P], ALU.add).then_inc(scan_done, 1)
                dve.wait_ge(l2_rms, 5 * g + 5)
                for h in range(HG):
                    r = ssq[:, 1, 4 * h:4 * h + 4].unsqueeze(2).to_broadcast([P, NT, P])
                    dve.tensor_tensor(R2(v_T[:, h, :]), R2(v_T[:, h, :]), r, ALU.mult).then_inc(ssq_ready, 1)
                dve.wait_ge(chunk_out, 12 * g + 12)
                for h in range(HG):
                    dve.wait_ge(ot_done, 4 * g + h + 1)
                    dve.scalar_tensor_tensor(out=gate_out[:, 4 * g + h, :], in0=psum[4 + h][:, :], scalar=GNW,
                                             in1=z_T[:, h, :], op0=ALU.mult, op1=ALU.mult).then_inc(gate_ready, 1)
            post_norm()
            pre_norm()
            sc_base = 56
            dve.sem_inc(sc_used, 1)
            for i in passes(dve, SC // 256):
                own.enter(i, 12)
                for s in range(2):
                    u, b, c, z = [sc_in[:, 2 * m + s, :] for m in range(4)]
                    dve.wait_ge(chunk_out, sc_base + 8 * i + 5 + s)
                    own.did(dve.tensor_tensor(u, u, c, ALU.mult))
                    own.settle()
                    own.did(conv(sc_conv[:, s, :], u, 3, lambda tap: SCONV(tap, 2 * i + s)))
                    own.settle()
                    own.did(dve.tensor_tensor(sc_conv[:, s, :], sc_conv[:, s, :], b, ALU.mult))
                    own.settle()
                    dve.wait_ge(chunk_out, sc_base + 8 * i + 7 + s)
                    own.did(dve.tensor_tensor(sc_out[:, 2 * i + s, :], sc_conv[:, s, :], z, ALU.mult))
                    own.settle()
                    dve.sem_inc(sc_used, 1)
                own.leave(8)
            post_norm()
            pre_norm()
            m0 = 128
            dve.wait_ge(chunk_out, m0 + 10)
            dve.wait_ge(x_ready, 16)
            src, dst = pool_x, pool_b
            for shift, r0, c0 in ((1, 0, 0), (2, 64, 0), (4, 0, 1), (8, 64, 1)):
                parts = {(0, 0): [(0, P, 0, 2)], (64, 0): [(64, P, 0, 1), (0, P, 1, 2)], (0, 1): [(0, P, 1, 2)],
                         (64, 1): [(64, P, 1, 2)]}[(r0, c0)]
                for a, b, ca, cb in parts:
                    own.did(dve.tensor_copy(dst[a:b, ca:cb, 0:shift], src[a:b, ca:cb, 0:shift]))
                    own.did(dve.tensor_tensor(dst[a:b, ca:cb, shift:S], src[a:b, ca:cb, shift:S], src[a:b, ca:cb, 0:S - shift], ALU.add))
                own.settle()
                src, dst = dst, (pool_a if dst is pool_b else pool_b)
            dve.wait_ge(inv_in, 16)
            for g, (s_, win) in enumerate(((pool_b, 2), (pool_a, 4), (pool_b, 8), (pool_a, 16))):
                r, c = slice(64 * (g % 2), 64 * (g % 2) + 64), g // 2
                own.did(dve.tensor_tensor(pool_d[r, c, 0:16], s_[r, c, 0:16], inv_count[r, 16 * c:16 * c + 16], ALU.mult))
                own.did(dve.scalar_tensor_tensor(out=pool_d[r, c, 16:S], in0=s_[r, c, 16:S], scalar=1.0 / win, in1=pool_x[r, c, 16:S],
                                                 op0=ALU.mult, op1=ALU.subtract))
            own.settle()
            dve.tensor_tensor(pool_d[:, :, 0:16], pool_d[:, :, 0:16], pool_x[:, :, 0:16], ALU.subtract).then_inc(pool_ready, 1)
            dve.wait_ge(gate_exp, 1)
            own.did(dve.tensor_scalar(gate, gate, 1.0, None, ALU.add))
            own.settle()
            dve.reciprocal(gate, gate).then_inc(gates_ready, 1)
            dve.wait_ge(turn_done, 2)
            dve.tensor_tensor(spatial_T, psum[5][:, :].rearrange("p (h t) -> p h t", h=4),
                              masks[:, 13:14, :].to_broadcast([P, 4, P]), ALU.mult).then_inc(mask_done, 1)
            blk = blocks.rearrange("p (l c) -> p l c", c=NC)
            dve.wait_ge(turn_out, 1)
            for kind in range(2):
                if kind:
                    dve.wait_ge(hid_done, 1)
                s_ = cmp_kv[:, kind, :]
                over = bass.AP(tensor=s_.tensor, offset=s_.offset, ap=[list(s_.ap[0]), [1, 32], [16, NC]])
                dve.tensor_tensor(blk, over, pos_T[:, 32 * kind:32 * kind + 32].unsqueeze(2).to_broadcast([P, 32, NC]), ALU.add)\
                    .then_inc(blocks_ready, 1)
            dve.wait_ge(chunk_out, m0 + 20)
            dve.wait_ge(turn_out, 5)
            mean, var = small[:, 1:5], small[:, 5:9]
            bc = lambda v: v.unsqueeze(2).to_broadcast([P, NT, 256])
            own.did(dve.tensor_reduce(mean, sgu_v, AX.X, ALU.add))
            own.settle()
            own.did(dve.tensor_scalar(mean, mean, 1.0 / 256, None, ALU.mult))
            own.settle()
            own.did(dve.tensor_tensor(sgu_v, sgu_v, bc(mean), ALU.subtract))
            own.settle()
            own.did(dve.tensor_tensor(sgu_t, sgu_v, sgu_v, ALU.mult))
            own.settle()
            dve.tensor_reduce(var, sgu_t, AX.X, ALU.add).then_inc(var_ready, 1)
            dve.wait_ge(rstd_ready, 1)
            own.did(dve.tensor_tensor(sgu_v, sgu_v, bc(var), ALU.mult))
            own.settle()
            own.did(dve.tensor_tensor(sgu_v, sgu_v, sgu_gb[:, 0:1, :].to_broadcast([P, NT, 256]), ALU.mult))
            own.settle()
            dve.tensor_tensor(sgu_v, sgu_v, sgu_gb[:, 1:2, :].to_broadcast([P, NT, 256]), ALU.add).then_inc(sgu_norm, 1)
            dve.wait_ge(c2_done, 1)
            own.did(dve.tensor_scalar(cmp_k, psum[6][:, 0:NC], cols[:, 1, 53:54], None, ALU.add))
            dve.tensor_tensor(cmp_v[0:NC, :], psum[7][0:NC, 0:P], b_c2[0:NC].rearrange("p g d -> p (g d)"), ALU.add).then_inc(c2_ready, 1)
            dve.wait_ge(spatial_done, 1)
            for pair in range(2):
                tmp = sgu_t.rearrange("p (a n) t -> p a (n t)", a=2)[:, pair, :].rearrange("p (n t) -> p n t", n=NT)
                own.did(dve.tensor_tensor(tmp, psum[4 + pair][:, :].rearrange("p (n t) -> p n t", n=NT),
                                          sgu_bias[:, pair:pair + 1, :].to_broadcast([P, NT, P]), ALU.add))
                own.settle()
                dve.tensor_tensor(mix_T[:, 6 + pair, :].rearrange("p (n t) -> p n t", n=NT), tmp,
                                  sgu_u[:, pair, :].rearrange("p (n t) -> p n t", n=NT), ALU.mult).then_inc(sgu_done, 1)
            dve.wait_ge(sgu_done, 2)
            dve.wait_ge(bias_in, 32)
            dve.wait_ge(c2_ready, 1)

            def read_scores(n):
                qi, kind, h = units[n]
                dve.wait_ge(score_done, n + 1)
                if kind == 0:
                    if qi:
                        dve.wait_ge(probT_done, n - 16)
                    cb = bias_cmp[:, qi, :].rearrange("p (h c) -> p h c", h=ATT_H)
                    for g in range(2):
                        own.did(dve.tensor_tensor(cmp_prob[:, 4 * g:4 * g + 4, :],
                                                  psum[g][:, 0:P].rearrange("p (h c) -> p h c", h=4)[:, :, 0:NC],
                                                  cb[:, 4 * g:4 * g + 4, :], ALU.add))
                    own.settle()
                    own.did(dve.tensor_reduce(cmp_max, cmp_prob, AX.X, ALU.max))
                    own.settle()
                    own.did(dve.tensor_scalar(cmp_max, cmp_max, NEG / 10, None, ALU.max))
                    own.settle()
                    dve.tensor_tensor(cmp_prob, cmp_prob, cmp_max.unsqueeze(2).to_broadcast([P, ATT_H, NC]), ALU.subtract)\
                        .then_inc(score_read, 1)
                    return
                if n >= 4:
                    dve.wait_ge(probT_done, n - 3)
                w = P * (qi + 1)
                own.did(dve.tensor_tensor_reduce(prob[:, n % 4, 0:w], psum[n % 2][:, 0:w], bias_row[:, h, S - w:S], 1.0, -3.0e38,
                                                 ALU.add, ALU.max, neg_max(n)))
                own.settle()
                dve.tensor_scalar(neg_max(n), neg_max(n), -1.0, None, ALU.mult).then_inc(score_read, 1)

            def copy_probs(n):
                qi, kind, h = units[n]
                dve.wait_ge(probT_done, n + 1)
                need = n if is_cmp(n) or is_cmp(n - 1) else n - 1
                if need > 0:
                    dve.wait_ge(pv_done, need)
                if kind == 0:
                    s_ = sums(qi, 0)
                    if n >= 34:
                        dve.wait_ge(combined, qi - 1)
                    own.did(dve.tensor_reduce(s_, cmp_prob, AX.X, ALU.add))
                    own.did(dve.tensor_copy(prob_T[0:NC, 0, :], psum[2][0:NC, :]))
                    dve.tensor_copy(prob_T[0:NC, 1, :], psum[3][0:NC, :]).then_inc(probT_out, 1)
                    own.settle()
                    own.did(dve.tensor_scalar(s_, s_, 1.0, None, ALU.max))
                else:
                    dve.tensor_copy(prob_T[:, n % 2, 0:P * (qi + 1)], psum[2 + n % 2][:, 0:P * (qi + 1)]).then_inc(probT_out, 1)

            def combine(qi):
                last = 17 * qi + 16
                dve.wait_ge(prob_ready, last + 1)
                dve.wait_ge(gates_ready, 1)
                own.settle()
                for kind in range(3):
                    own.did(dve.reciprocal(sums(qi, kind), sums(qi, kind)))
                own.settle()
                g3 = gate[:, qi, :].rearrange("p (h x) -> p x h", x=3)
                for kind in range(3):
                    own.did(dve.tensor_tensor(g3[:, kind, :], g3[:, kind, :], sums(qi, kind), ALU.mult))
                own.settle()
                dve.wait_ge(pv_done, last + 1)
                if qi:
                    dve.wait_ge(attT_done, qi)
                for kind in range(3):
                    own.did(dve.tensor_tensor(att_o[:, kind, :].rearrange("p (h d) -> p h d", h=ATT_H),
                                              psum[4 + kind][:, :].rearrange("p (h d) -> p h d", h=ATT_H),
                                              g3[:, kind, :].unsqueeze(2).to_broadcast([P, ATT_H, DH]), ALU.mult))
                own.settle()
                own.did(dve.tensor_tensor(att_o[:, 0, :], att_o[:, 0, :], att_o[:, 1, :], ALU.add))
                own.settle()
                dve.tensor_tensor(att_o[:, 0, :], att_o[:, 0, :], att_o[:, 2, :], ALU.add).then_inc(combined, 1)

            for n in range(len(units) + 4):
                if n < len(units):
                    read_scores(n)
                if 0 <= n - 2 < len(units):
                    copy_probs(n - 2)
                if n >= 19 and (n - 19) % 17 == 0:
                    combine((n - 19) // 17)
            post_norm()
            dve.wait_ge(mem_rstd, 1)
            own.did(dve.tensor_scalar(mem_rows[:, 0, :], mem_rows[:, 0, :], small[:, 1:2], None, ALU.mult))
            dve.tensor_scalar(mem_rows[:, 1, :], mem_rows[:, 1, :], small[:, 2:3], None, ALU.mult).then_inc(mem_scaled, 1)
            pre_norm()
            for n in range(len(mem_units) + 1):
                if n < len(mem_units):
                    dve.wait_ge(ms_done, n + 1)
                    own.did(dve.tensor_reduce(mem_max(n), psum[4 + n % 2][:, 0:MEM], AX.X, ALU.max))
                    own.settle()
                    dve.tensor_scalar(mem_max(n), mem_max(n), -(HD ** -0.5), None, ALU.mult).then_inc(ms_max, 1)
                m = n - 1
                if m >= 0:
                    dve.wait_ge(mp_exp, m + 1)
                    own.did(dve.reciprocal(mem_sum(m), mem_sum(m)))
                    own.settle()
                    dve.tensor_scalar(mem_prob[:, m % 4, :], mem_prob[:, m % 4, :], mem_sum(m), None, ALU.mult).then_inc(mp_ready, 1)
            post_norm()
            pre_norm()
            dve.wait_ge(x_ready, 32)
            dve.sem_inc(ff_conv, 1)
            for jj in passes(dve, FK // 2):
                own.enter(jj, 8)
                for v in range(2):
                    for s in range(2):
                        c = 2 * jj + s + FK * v
                        dve.wait_ge(chunk_out, FF0 + 4 * jj + 2 * v + s + 1)
                        conv((ff_gate, ff_val)[v][:, s, :], ff_raw[:, 2 * v + s, :], 3, lambda tap: FCONV(tap, c), FBIAS(c))\
                            .then_inc(ff_conv, 1)
                for s in range(2):
                    dve.wait_ge(ff_gelu, 2 * jj + s + 1)
                    dve.wait_ge(ff_conv, 4 * jj + 4 + s)
                    dve.tensor_tensor(ff_hid[:, 2 * jj + s, :], ff_gate[:, s, :], ff_val[:, s, :], ALU.mult).then_inc(ff_ready, 1)
                dve.wait_ge(ff_ready, 2 * jj + 2)
                own.leave(FK // 2)
            post_norm(ff_y)
            dve.wait_ge(chunk_done, FF0 + 52)
            for t in range(NT):
                dve.wait_ge(final_done, 2 * t + 2)
                dve.tensor_copy(out_rows_sb[:, t, 512:1024], psum[2 * t + 1][:, :]).then_inc(final_dve, 1)

        @block.gpsimd
        def _(pool):
            for g in range(GROUPS):
                for pair in range(2):
                    for lv in range(5):
                        n0 = 20 * g + 10 * pair + 2 * lv
                        for j in range(2):
                            h = 2 * pair + j
                            pool.wait_ge(y_start, 4 * g + h + 1)
                            pool.wait_ge(decay_used, 4 * g + 4)
                            if lv or pair:
                                pool.wait_ge(p_done, n0 + j - 1)
                            pool.tensor_tensor(R2(decay[:, j, :]), R2(A_T[:, h, :]),
                                               masks[:, 4 + lv:5 + lv, :].to_broadcast([P, NT, P]), ALU.mult)\
                                .then_inc(level_ready, 1)






_INS = ["x", "pre_norm_w", "post_norm_w", "gdn_w_in", "gdn_conv_w", "gdn_A_log", "gdn_dt_bias", "gdn_norm_w", "gdn_w_out",
        "sc_w_in", "sc_conv_w", "sc_w_out", "mem_2", "rel_bias_2", "mix_norm_pre_2", "mix_norm_post_2", "w_in_2",
        "cmp_pos_2", "cmp_w1_2", "cmp_b1_2", "cmp_w2_2", "cmp_b2_2", "pool_w_2", "pool_scale_2", "sgu_norm_g_2",
        "sgu_norm_b_2", "sgu_w_2", "sgu_b_2", "w_out_2", "mem_norm_pre_2", "mem_norm_kv_2", "mem_norm_post_2", "w_mq_2",
        "w_mk_2", "w_mv_2", "w_mo_2", "ffn_norm_pre_2", "ffn_norm_post_2", "w_up_2", "conv_w_2", "conv_b_2", "w_down_2"]


def kernel(**inputs):
    import concourse.bacc as _bacc
    from concourse.bass_utils import run_bass_kernel_spmd as _run

    nc = _bacc.Bacc("TRN2", target_bir_lowering=False, num_devices=1)
    arrays = {name: np.ascontiguousarray(inputs[name]) for name in _INS}
    arrays["masks_d"], arrays["hot_d"], arrays["inv_d"] = shape_constants()
    args = {name: nc.dram_tensor(f"in_{name}", a.shape, mybir.dt.from_np(a.dtype), kind="ExternalInput").ap()
            for name, a in arrays.items()}
    out = nc.dram_tensor("out_x", (1, S, D), mybir.dt.float32, kind="ExternalOutput").ap()
    build(nc, out=out, **args)
    r = _run(nc, [{f"in_{name}": a for name, a in arrays.items()}], core_ids=[0])
    return r.results[0]["out_x"]
```

```python
import numpy as np
import concourse.bass as bass
from concourse import mybir
from contextlib import ExitStack

S = 512
D = 1024
P = 128
KD = D // P
NT = S // P
EPS = 1e-6
NEG = -1.0e30
KH, VH = 8, 16
QK_W, V_W = KH * P, VH * P
CONV_W = 2 * QK_W + V_W
TAPS = 4
CH = 64
GROUPS = 4
HG = VH // GROUPS
SC = 2048
ATT_H, DH = 8, 64
REL = 32
NC = S // 16 - 1
W2 = 2072
MEM, MH = 256, 4
FF = 2816
FK = FF // P
SLOT = 2048


def shape_constants():
    i = np.arange(P)
    row, col = i[:, None], i[None, :]
    same = row // CH == col // CH
    parts = [np.eye(P), same & (row <= col), np.where(same & (row <= col), 0.0, NEG)]
    for s in (1, 2, 4, 8, 16, 32):
        pair = (row // (2 * s) == col // (2 * s)) & (col // s % 2 == 1) & (row // s % 2 == 0)
        parts.append(-1.0 * pair)
    parts += [same, (row < CH) & (col >= 0), (row >= CH) & (col >= 0), np.ones((P, P)), row <= col]
    masks = np.concatenate([np.asarray(m, np.float32) for m in parts], 1)
    dist = np.arange(S)
    n = np.maximum(dist, 1).astype(np.float32)
    far = 16 + (np.log(n / np.float32(16)) / np.float32(np.log(64.0)) * np.float32(16)).astype(np.int32)
    bucket = np.where(dist < 16, dist, np.minimum(far, REL - 1))
    hot = np.zeros((REL + 1, 1023), np.float32)
    y = np.arange(1023)
    hot[np.where(y < 511, REL, bucket[np.maximum(y - 511, 0)]), y] = 1
    hot = np.concatenate([hot, np.zeros((REL + 1, 1), np.float32)], 1)
    hot[REL, 1023] = 1
    hot = np.concatenate([hot, hot[:, 1022::-1], hot[:, 1023:]], 1)
    inv = np.zeros((P, 2, 16), np.float32)
    for g, win in enumerate((2, 4, 8, 16)):
        inv[64 * (g % 2):64 * (g % 2) + 64, g // 2] = 1.0 / np.minimum(np.arange(16) + 1, win)
    return masks, hot, inv.reshape(P, 32)


class Tally:

    def __init__(self, eng, sem):
        self.eng, self.sem, self.base, self.n = eng, sem, 0, 0

    def did(self, ins):
        ins.then_inc(self.sem, 1)
        self.n += 1
        return self.now()

    def now(self):
        return self.base + self.n

    def settle(self):
        self.eng.wait_ge(self.sem, self.now())

    def enter(self, i, per):
        self.start, self.per = self.now(), per
        self.base, self.n = self.start + i * per, 0

    def leave(self, times):
        assert self.n == self.per, (self.sem, self.n)
        self.base, self.n = self.start + times * self.per, 0


def build(nc, x, pre_norm_w, post_norm_w, gdn_w_in, gdn_conv_w, gdn_A_log, gdn_dt_bias, gdn_norm_w, gdn_w_out,
          sc_w_in, sc_conv_w, sc_w_out, mem_2, rel_bias_2, mix_norm_pre_2, mix_norm_post_2, w_in_2, cmp_pos_2,
          cmp_w1_2, cmp_b1_2, cmp_w2_2, cmp_b2_2, pool_w_2, pool_scale_2, sgu_norm_g_2, sgu_norm_b_2, sgu_w_2,
          sgu_b_2, w_out_2, mem_norm_pre_2, mem_norm_kv_2, mem_norm_post_2, w_mq_2, w_mk_2, w_mv_2, w_mo_2,
          ffn_norm_pre_2, ffn_norm_post_2, w_up_2, conv_w_2, conv_b_2, w_down_2, masks_d, hot_d, inv_d, out):
    F32 = mybir.dt.float32
    ALU, ACT, AX = mybir.AluOpType, mybir.ActivationFunctionType, mybir.AxisListType
    ds = bass.ds
    ctx = ExitStack()
    with ctx:
        def sb(name, *shape):
            return ctx.enter_context(nc.sbuf_tensor(name, [shape[0], int(np.prod(shape[1:]))], F32))

        def sbr(name, n):
            return ctx.enter_context(nc.sbuf_tensor(name, [P, n], mybir.dt.float32r))[:, :]

        def sem(name):
            return ctx.enter_context(nc.semaphore(name))

        xT = sb("xT", P, KD, S)[:, :].rearrange("p (k s) -> p k s", k=KD)
        ring = sb("ring", P, 2, SLOT)[:, :].rearrange("p (r w) -> p r w", r=2)
        w_hi, w_lo = [sbr(n, 2 * SLOT).rearrange("p (r w) -> p r w", r=2) for n in ("w_hi", "w_lo")]
        h_hi, h_lo = [sbr(n, KD * S).rearrange("p (k s) -> p k s", k=KD) for n in ("h_hi", "h_lo")]
        ws_hi, ws_lo = [sbr(n, KD * 32).rearrange("p (k c) -> p k c", k=KD) for n in ("ws_hi", "ws_lo")]
        masks = sb("masks", P, 14, P)[:, :].rearrange("p (m c) -> p m c", m=14)
        cols = sb("cols", P, 5, P)[:, :].rearrange("p (m c) -> p m c", m=5)
        rs = sb("rs", P, S)
        sq = sb("sq", P, 2, S)[:, :].rearrange("p (r s) -> p r s", r=2)
        small = sb("small", P, 64)
        inv_count = sb("inv_count", P, 32)[:, :]
        eps = small[:, 0:1]
        ident, upper, negmask = masks[:, 0, :], masks[:, 1, :], masks[:, 2, :]
        neglevel = [masks[:, 3 + n, :] for n in range(6)]
        same, half0, half1, ones, causal = [masks[:, 9 + n, :] for n in range(5)]
        ARENA = 24056
        arena = sb("arena", P, ARENA)
        psum = [ctx.enter_context(nc.psum_tensor(f"bank{n}", [P, S], F32)) for n in range(8)]

        def cut(start, *shape):
            n = int(np.prod(shape))
            assert start + n <= ARENA, (start, shape)
            v = arena[:, start:start + n]
            if len(shape) == 2:
                v = v.rearrange("p (a b) -> p a b", a=shape[0])
            if len(shape) == 3:
                v = v.rearrange("p (a b c) -> p a b c", a=shape[0], b=shape[1])
            return v, start + n

        GCONV = lambda tap, c: cols[:, 0, tap * 32 + c:tap * 32 + c + 1] if isinstance(c, int) else cols[:, 0, ds(c + tap * 32, 1)]
        SCONV = lambda tap, c: cols[:, 1, ds(c + tap * 16, 1)]
        FCONV = lambda tap, c: (cols[:, 2 + tap // 2, ds(c + (tap % 2) * 44, 1)])
        FBIAS = lambda c: cols[:, 3, ds(c + 44, 1)]
        GNW = cols[:, 1, 50:51]
        PSC = lambda c: cols[:, 1, 48 + c:49 + c]
        PRE = [lambda k: cols[:, 4, k:k + 1], lambda k: cols[:, 4, 8 + k:9 + k],
               lambda k: cols[:, 4, 32 + k:33 + k], lambda k: cols[:, 4, 48 + k:49 + k], lambda k: cols[:, 4, 72 + k:73 + k]]
        POST = [lambda k: cols[:, 4, 16 + k:17 + k], lambda k: cols[:, 4, 24 + k:25 + k],
                lambda k: cols[:, 4, 40 + k:41 + k], lambda k: cols[:, 4, 64 + k:65 + k], lambda k: cols[:, 4, 80 + k:81 + k]]
        KVW = lambda k: cols[:, 4, 56 + k:57 + k]

        consts_in = sem("consts_in")
        rows_in = sem("rows_in")
        x_in = sem("x_in")
        slot_in = [sem(f"slot_in{n}") for n in range(2)]
        w_hi_ready = sem("w_hi_ready")
        split_ready = sem("split_ready")
        h32_ready = sem("h32_ready")
        h_hi_ready = sem("h_hi_ready")
        ws_ready, ws_hi_ready = sem("ws_ready"), sem("ws_hi_ready")
        chunk_done = sem("chunk_done")
        chunk_out = sem("chunk_out")
        square_ready = sem("square_ready")
        square_used = sem("square_used")
        rms_ready = sem("rms_ready")
        h_ready = sem("h_ready")
        x_ready = sem("x_ready")
        act_step = sem("act_step")
        dve_step = sem("dve_step")
        pool_step = sem("pool_step")
        eps_set = sem("eps_set")
        turned = sem("turned")
        turned_used = sem("turned_used")
        inv_in = sem("inv_in")
        stored = sem("stored")

        gate_out, at = cut(0, VH, S)
        x_kept = nc.dram_tensor("x_kept", [P, KD * S], F32, kind="Internal").ap()
        x_away, x_back = sem("x_away"), sem("x_back")
        z_T, at = cut(at, HG, S)
        raw, at = cut(at, 3, S)
        k_rows, at = cut(at, 2, S)
        kk, at = cut(at, 2, S)
        kq, at = cut(at, 2, S)
        decay, at = cut(at, 2, S)
        A_T, at = cut(at, HG, S)
        Y_T, at = cut(at, HG, S)
        QK_T, at = cut(at, HG, S)
        state, at = cut(at, HG, P)
        resid, v_new, v_dec = [A_T[:, n, :].rearrange("p (h c) -> p h c", h=HG) for n in range(3)]
        tok, at = cut(at, 12, 64)
        grp, at = cut(at, 2, 16)
        ssq, at = cut(at, 2, 16)
        alog, at = cut(at, 2, 16)
        wba, _ = cut(at, KD, 32)
        late, _ = cut(at, S)
        squares = [kk[:, 0, :], kk[:, 1, :], kq[:, 0, :], kq[:, 1, :]]
        q_of = [[xT[:, 0, :], xT[:, 1, :]], [sq[:, 0, :], sq[:, 1, :]]]
        k_of = [[xT[:, 2, :], xT[:, 3, :]], [rs[:, :], late]]
        v_of = [xT[:, 4:8, :], gate_out[:, 12:16, :]]
        beta, g_log, G_cum, G_end, e_G, neg_G, neg_bG, e_rest, end0, end1, tmpA, tmpB = [tok[:, n, :] for n in range(12)]
        x_rows = arena[:, 0:NT * D].rearrange("p (t c) -> p t c", t=NT)
        par_rows = arena[:, NT * D:NT * D + 5 * P].rearrange("p (m c) -> p m c", m=5)
        y_T, _ = cut(VH * S, KD, S)
        R2 = lambda v: v.rearrange("p (t c) -> p t c", t=NT)
        R4 = lambda v: v.rearrange("p (t h) -> p t h", t=NT)

        wba_in = sem("wba_in")
        ba_done = sem("ba_done")
        tok_act, tok_dve, tok_exp = sem("tok_act"), sem("tok_dve"), sem("tok_exp")
        cum_done = sem("cum_done")
        tok_ready = sem("tok_ready")
        conv_done = sem("conv_done")
        silu_done = sem("silu_done")
        l2_sq = sem("l2_sq")
        l2_sum = sem("l2_sum")
        l2_rms = sem("l2_rms")
        qk_ready = sem("qk_ready")
        grp_ready = sem("grp_ready")
        kk_done, kk_ready = sem("kk_done"), sem("kk_ready")
        kr_done, kr_ready = sem("kr_done"), sem("kr_ready")
        vt_done, vb_ready = sem("vt_done"), sem("vb_ready")
        gb_done, decay_ready = sem("gb_done"), sem("decay_ready")
        decay_used = sem("decay_used")
        bb_done, y_start = sem("bb_done"), sem("y_start")
        level_ready, level_used = sem("level_ready"), sem("level_used")
        xt_done, xt_ready = sem("xt_done"), sem("xt_ready")
        p_done, p_ready = sem("p_done"), sem("p_ready")
        py_done, y_ready = sem("py_done"), sem("y_ready")
        ks_done, resid_ready = sem("ks_done"), sem("resid_ready")
        vn_done, vn_ready = sem("vn_done"), sem("vn_ready")
        su_done, state_ready = sem("su_done"), sem("state_ready")
        scan_done = sem("scan_done")
        ssq_ready, ot_done, gate_ready = sem("ssq_ready"), sem("ot_done"), sem("gate_ready")

        plan = []

        def slab_of(kind, chunks, dmas=1, n=1):
            for _ in range(n):
                prev = plan[-1] if plan else {"end": 0, "splits": 0}
                before = plan[-2]["arrived"] if len(plan) > 1 else 0
                plan.append({"kind": kind, "end": prev["end"] + chunks, "splits": prev["splits"] + (kind == "split"),
                             "arrived": before + 16 * dmas})

        for _ in range(GROUPS):
            slab_of("split", 2, n=4)
            slab_of("split", 6)
            slab_of("split", 2)
        slab_of("raw", 1, n=8)
        SC0 = len(plan)
        slab_of("split", 2, n=32)
        slab_of("raw", 1, n=8)
        MIX0 = len(plan)
        slab_of("split", 2, dmas=4, n=2)
        slab_of("split", 2)
        slab_of("split", 5, n=2)
        slab_of("split", 2, n=2)
        slab_of("split", 8)
        slab_of("cmp0", 0, dmas=2, n=2)
        slab_of("cmp1", 0, dmas=2, n=2)
        slab_of("raw", 2, n=4)
        MEM0 = len(plan)
        slab_of("raw", 2, n=8)
        slab_of("split", 2, n=4)
        MEM1 = len(plan)
        plan[-1]["end"] += KD
        slab_of("raw", 2, n=4)
        FF1 = len(plan)
        slab_of("split", 2, n=FK)
        for c in range(KD):
            slab_of("half", 0)
            plan[-1]["half"] = c + 1
            slab_of("raw", 1)

        sc_out, _ = cut(0, SC // P, S)
        sc_in, at = cut(12288, 8, S)
        sc_conv, at = cut(at, 2, S)
        sc_used = sem("sc_used")
        mix_T, at = cut(0, KD, S)
        att_q, at = cut(at, 4, S)
        cmp_kv, at = cut(at, 2, S)
        att_k, at = cut(at, 2, S)
        pool_x, at = cut(at, 2, S)
        sgu_u, at = cut(at, 2, S)
        att_v, at = cut(at, NT, 256)
        sgu_v, at = cut(at, NT, 256)
        gate_raw, at = cut(at, NT, 24)
        gate, at = cut(at, NT, 24)
        spatial_T, at = cut(at, 4, P)
        sgu_gb = mix_T[:, 5, :].rearrange("p (a c) -> p a c", a=2)
        w_gate = mix_T[:, 7, 0:KD * 24].rearrange("p (k c) -> p k c", k=KD)
        pos_rows = mix_T[:, 7, 256:256 + P]
        sgu_bias, at = cut(at, 2, P)
        w_pool, at = cut(at, 2, DH)
        w_c2, at = cut(at, 2, DH)
        b_c2 = mix_T[:, 7, 384:512].rearrange("p (g d) -> p g d", g=2)
        bias_row, at = cut(at, ATT_H, S)
        bias_cmp, at = cut(at, NT, ATT_H * NC)
        free = at
        hot, at = cut(free, 2, 1024)
        table, at = cut(at, 2, 1024)
        bias_cmp_T, _ = cut(free, ATT_H, S)
        prob, at = cut(free, 4, S)
        prob_T, at = cut(at, 2, S)
        pool_a, pool_b, pool_d = prob[:, 0:2, :], prob[:, 2:4, :], prob_T
        att_o, _ = cut(at, 2, S)
        sgu_t, at = cut(at, NT, 256)
        blocks, at = cut(at, 32 * NC)
        hidden, at = cut(at, 4, NC)
        cmp_k, at = cut(at, NC)
        cmp_v, at = cut(at, P)
        pos_T, at = cut(at, 64)
        spatial_rows = mix_T[:, 6, :].rearrange("p (h s) -> p h s", h=4)
        cmp_prob = blocks[:, 0:ATT_H * NC].rearrange("p (h c) -> p h c", h=ATT_H)
        rel = small[0:REL + 1, 1:9]
        neg_max = lambda n: small[:, 1 + n % 4:2 + n % 4]
        cmp_max = small[:, 5:13]
        sums = lambda qi, kind: small[:, 13 + 24 * (qi % 2) + 8 * kind:21 + 24 * (qi % 2) + 8 * kind]
        ROW_L, CMP_L = S + P, 2 * S - 32
        row_copies = nc.dram_tensor("row_copies", [ATT_H, P, ROW_L], F32, kind="Internal").ap()
        cmp_copies = nc.dram_tensor("cmp_copies", [ATT_H, NC, CMP_L], F32, kind="Internal").ap()
        hot_in, mixer_in = sem("hot_in"), sem("mixer_in")
        rel_in, w_gate_in = sem("rel_in"), sem("w_gate_in")
        table_done, table_out = sem("table_done"), sem("table_out")
        table_stored, bias_in = sem("table_stored"), sem("bias_in")
        turn_done, turn_out = sem("turn_done"), sem("turn_out")
        ct_done = sem("ct_done")
        mask_done = sem("mask_done")
        blocks_ready, hid_done, hid_ready = sem("blocks_ready"), sem("hid_done"), sem("hid_ready")
        c2_done, c2_ready = sem("c2_done"), sem("c2_ready")
        gate_exp, gates_ready = sem("gate_exp"), sem("gates_ready")
        var_ready, rstd_ready, sgu_norm = sem("var_ready"), sem("rstd_ready"), sem("sgu_norm")
        spatial_done, sgu_done = sem("spatial_done"), sem("sgu_done")
        pool_ready, pool_done, pool_out = sem("pool_ready"), sem("pool_done"), sem("pool_out")
        score_done, score_read, prob_ready = sem("score_done"), sem("score_read"), sem("prob_ready")
        probT_done, probT_out, pv_done = sem("probT_done"), sem("probT_out"), sem("pv_done")
        combined, attT_done, attT_out = sem("combined"), sem("attT_done"), sem("attT_out")
        units = [(qi, kind, h) for qi in range(NT) for kind, h in [(0, 0)] + [(k, h) for k in (1, 2) for h in range(ATT_H)]]
        is_cmp = lambda n: 0 <= n < len(units) and units[n][1] == 0
        MT, HD = MEM // P, D // MH
        mem_out, at = cut(0, KD, S)
        mem_q, at = cut(at, KD, S)
        mem_k, at = cut(12288, KD, MEM)
        mem_v, at = cut(at, MT, D)
        mem_rows, at = cut(at, MT, D)
        mem_T, at = cut(at, KD, MEM)
        mem_prob, at = cut(at, 4, MEM)
        mem_probT, at = cut(at, 4, S)
        mem_junk = mem_T.rearrange("p k m -> p (k m)")[:, 0:D]
        mem_sum = lambda n: small[:, 20 + n:21 + n]
        mem_max = lambda n: small[:, 36 + n:37 + n]
        mem_in = sem("mem_in")
        mem_rstd, mem_scaled = sem("mem_rstd"), sem("mem_scaled")
        mem_turned, mem_turned_out = sem("mem_turned"), sem("mem_turned_out")
        ms_done, ms_max, mp_exp, mp_ready = sem("ms_done"), sem("ms_max"), sem("mp_exp"), sem("mp_ready")
        mpT_done, mpT_out = sem("mpT_done"), sem("mpT_out")
        mem_units = [(h, qi) for h in range(MH) for qi in range(NT)]
        ff_hid, at = cut(0, FK, S)
        ff_y, at = cut(at, KD, S)
        ff_raw, at = cut(at, 4, S)
        ff_gate, at = cut(at, 2, S)
        ff_val, at = cut(at, 2, S)
        out_rows_sb, _ = cut(0, NT, D)
        ff_conv, ff_gelu, ff_ready = sem("ff_conv"), sem("ff_gelu"), sem("ff_ready")
        final_done, final_act, final_dve = sem("final_done"), sem("final_act"), sem("final_dve")
        half_used = sem("half_used")
        FF0 = plan[FF1 - 1]["end"]
        def passes(eng, n):
            with eng.Fori(0, n) as i:
                yield i

        def slab_rows(ring, pos, c, n):
            return lambda k: ring[:, pos, k * 256 + c:k * 256 + c + n]

        MIXER_IN = 16 * 16

        def halves(c):
            return slice(CH * (c % 2), CH * (c % 2) + CH), c // 2

        block = ctx.enter_context(nc.Block())

        @block.sync
        def _(sp):
            st = {"n": 0}

            def slot_free(n):
                if n < 2:
                    return
                last = plan[n - 2]
                if last["kind"] == "split":
                    sp.wait_ge(split_ready, last["splits"])
                elif last["kind"] == "raw":
                    sp.wait_ge(chunk_done, last["end"])
                elif last["kind"] == "half":
                    sp.wait_ge(half_used, last["half"])
                else:
                    sp.wait_ge(hid_done, 1 + (last["kind"] == "cmp1"))

            def load(src, view):
                slot_free(st["n"])
                sp.dma_start(view(ring[:, st["n"] % 2, :]), src).then_inc(slot_in[st["n"] % 2], 16)
                st["n"] += 1

            wide = lambda n: (lambda r: r[:, 0:n * KD].rearrange("p (k c) -> p k c", k=KD))
            sp.dma_start(masks[:, :, :].rearrange("p m c -> p (m c)"), masks_d).then_inc(consts_in, 16)
            sp.dma_start(x_rows, x[0].rearrange("(t p) c -> p t c", p=P)).then_inc(x_in, 16)
            par = [
                (0, 0, gdn_conv_w[0].rearrange("t (c p) -> (t c) p", p=P), 128),
                (1, 0, sc_conv_w[0].rearrange("t (c p) -> (t c) p", p=P), 48),
                (1, 48, pool_scale_2[0].rearrange("(c p) -> c p", p=P), 2),
                (1, 50, gdn_norm_w, 1),
                (1, 51, cmp_b1_2[0], 2),
                (2, 0, conv_w_2[0, 0:2].rearrange("t (c p) -> (t c) p", p=P), 88),
                (3, 0, conv_w_2[0, 2:3].rearrange("t (c p) -> (t c) p", p=P), 44),
                (3, 44, conv_b_2[0].rearrange("(c p) -> c p", p=P), 44),
                (4, 0, pre_norm_w.rearrange("l (c p) -> (l c) p", p=P), 16),
                (4, 16, post_norm_w.rearrange("l (c p) -> (l c) p", p=P), 16)]
            for n, w in enumerate((mix_norm_pre_2, mix_norm_post_2, mem_norm_pre_2, mem_norm_kv_2, mem_norm_post_2,
                                   ffn_norm_pre_2, ffn_norm_post_2)):
                par.append((4, 32 + 8 * n, w[0].rearrange("(c p) -> c p", p=P), 8))
            sp.dma_start(par_rows[53:54, 1, 0:DH], cmp_b2_2[0, 0:1]).then_inc(rows_in, 16)
            sp.dma_start(par_rows[53:54, 1, DH:P], cmp_b2_2[0, 0:1]).then_inc(rows_in, 16)
            for m, row, src, n in par:
                sp.dma_start(par_rows[row:row + n, m, :], src).then_inc(rows_in, 16)
            w_k = gdn_w_in[0].rearrange("(k p) c -> p k c", p=P)
            sp.dma_start(wba, w_k[:, :, 6144:6176]).then_inc(wba_in, 16)
            sp.dma_start(alog[:, 0, :], gdn_A_log.to_broadcast([P, VH])).then_inc(wba_in, 16)
            sp.dma_start(alog[:, 1, :], gdn_dt_bias.to_broadcast([P, VH])).then_inc(wba_in, 16)
            sp.wait_ge(turned_used, 13)
            sp.dma_start(x_kept, xT.rearrange("p k s -> p (k s)")).then_inc(x_away, 16)
            for g in range(GROUPS):
                for c0 in ((256 * g, QK_W + 256 * g, 2 * QK_W + 512 * g, 2 * QK_W + 512 * g + 256,
                           4096 + 512 * g, 4096 + 512 * g + 256)):
                    load(w_k[:, :, c0:c0 + 256], wide(256))
            sp.wait_ge(ot_done, 4 * GROUPS)
            sp.wait_ge(x_away, 16)
            sp.dma_start(xT.rearrange("p k s -> p (k s)"), x_kept).then_inc(x_back, 16)
            tall = lambda r: r[:, :].rearrange("p (k c) -> p k c", c=P)
            for n in range(KD):
                load(gdn_w_out[0].rearrange("(k p) c -> p k c", p=P)[:, :, P * n:P * n + P], tall)
            w_sc = sc_w_in[0].rearrange("(k p) c -> p k c", p=P)
            sp.wait_ge(chunk_done, plan[SC0 - 1]["end"])
            for i in passes(sp, SC // 256):
                for m in range(4):
                    sp.wait_ge(split_ready, plan[SC0]["splits"] + 4 * i + m - 2)
                    sp.dma_start(ring[:, m % 2, :].rearrange("p (k c) -> p k c", k=KD),
                                 w_sc[:, :, ds(256 * i + SC * m, 256)]).then_inc(slot_in[m % 2], 16)
            st["n"] += 32
            for n in range(KD):
                load(sc_w_out[0].rearrange("(k p) c -> p k c", p=P)[:, :, P * n:P * n + P], tall)
            sp.dma_start(small[0:REL, 1:9], rel_bias_2).then_inc(rel_in, 16)
            sp.dma_start(inv_count, inv_d).then_inc(inv_in, 16)
            w_in = w_in_2[0].rearrange("(k p) c -> p k c", p=P)
            for a in range(2):
                slot_free(st["n"])
                for f in range(2):
                    for c in range(2):
                        sp.dma_start(ring[:, a, :].rearrange("p (k c f d) -> p k c f d", k=KD, c=2, f=2)[:, :, c, f, :],
                                     w_in[:, :, 256 * f + 128 * a + 64 * c:256 * f + 128 * a + 64 * c + 64])\
                            .then_inc(slot_in[a], 16)
                st["n"] += 1
            sp.wait_ge(x_ready, 16)
            sp.dma_start(hot[0:REL + 1, :, :], hot_d.rearrange("b (a y) -> b a y", a=2)).then_inc(hot_in, 16)
            sp.dma_start(w_gate, w_in[:, :, 1280:1304]).then_inc(w_gate_in, 16)
            sp.dma_start(spatial_rows, sgu_w_2[0].rearrange("h t s -> t h s")).then_inc(mixer_in, 16)
            for n, v in enumerate((sgu_norm_g_2, sgu_norm_b_2)):
                sp.dma_start(sgu_gb[:, n, :], v.to_broadcast([P, 256])).then_inc(mixer_in, 16)
            for h in range(4):
                f = slice(64 * (h % 2), 64 * (h % 2) + 64)
                sp.dma_start(sgu_bias[f, h // 2, :], sgu_b_2[0, h:h + 1, :].to_broadcast([64, P])).then_inc(mixer_in, 16)
                sp.dma_start(w_pool[f, h // 2, :], pool_w_2[0, h]).then_inc(mixer_in, 16)
            sp.dma_start(w_c2, cmp_w2_2[0].rearrange("k h d -> h k d")).then_inc(mixer_in, 16)
            for g in range(2):
                sp.dma_start(b_c2[0:NC, g, :], cmp_b2_2[0, 1:2, :].to_broadcast([NC, DH])).then_inc(mixer_in, 16)
                sp.dma_start(pos_rows[0:64, 64 * g:64 * g + 64], cmp_pos_2[0].rearrange("k l d -> (k l) d")).then_inc(mixer_in, 16)
            load(w_in[:, :, 512:768], wide(256))
            load(w_in[:, :, 768:1024], wide(256))
            sp.wait_ge(table_out, 4)
            sp.dma_start(row_copies, table[0:ATT_H, 1:2, 0:ROW_L].to_broadcast([ATT_H, P, ROW_L])).then_inc(table_stored, 16)
            sp.dma_start(cmp_copies, table[0:ATT_H, 0:1, 0:CMP_L].to_broadcast([ATT_H, NC, CMP_L])).then_inc(table_stored, 16)
            sp.wait_ge(table_stored, 32)
            sp.dma_start(bias_row, bass.AP(tensor=row_copies.tensor, offset=P - 1, ap=[[ROW_L - 1, P], [P * ROW_L, ATT_H], [1, S]]))\
                .then_inc(bias_in, 16)
            sp.dma_start(bias_cmp_T[0:NC, :, :],
                         bass.AP(tensor=cmp_copies.tensor, offset=480, ap=[[CMP_L - 16, NC], [NC * CMP_L, ATT_H], [1, S]]))\
                .then_inc(bias_in, 16)
            load(w_in[:, :, 1024:1280], wide(256))
            load(w_in[:, :, 1304:1560], wide(256))
            load(w_in[:, :, 1560:1816], wide(256))
            load(w_in[:, :, 1816:2072], wide(256))
            for kind in range(2):
                slot_free(st["n"])
                slot_free(st["n"] + 1)
                for g in range(2):
                    for a in range(2):
                        sp.dma_start(ring[64 * g:64 * g + 64, a, :].rearrange("d (l h) -> d l h", h=P),
                                     cmp_w1_2[0, kind, 16 * a:16 * a + 16].rearrange("l d h -> d l h")).then_inc(slot_in[a], 16)
                st["n"] += 2
            for n in range(4):
                load(w_out_2[0].rearrange("(k p) c -> p k c", p=P)[:, :, 256 * n:256 * n + 256], wide(256))
            sp.wait_ge(attT_out, NT)
            sp.dma_start(mem_rows, mem_2[0].rearrange("(t p) c -> p t c", p=P)).then_inc(mem_in, 16)
            for w in (w_mk_2, w_mv_2, w_mq_2, w_mo_2):
                for n in range(4):
                    load(w[0].rearrange("(k p) c -> p k c", p=P)[:, :, 256 * n:256 * n + 256], wide(256))
            assert st["n"] == FF1
            w_u = w_up_2[0].rearrange("(k p) c -> p k c", p=P)
            sp.wait_ge(chunk_done, plan[FF1 - 1]["end"])
            for jj in passes(sp, FK // 2):
                for v in range(2):
                    sp.wait_ge(split_ready, plan[FF1 + v]["splits"] + 2 * jj - 2)
                    sp.dma_start(ring[:, v, :].rearrange("p (k c) -> p k c", k=KD),
                                 w_u[:, :, ds(256 * jj + FF * v, 256)]).then_inc(slot_in[v], 16)
            st["n"] += FK
            w_d = w_down_2[0].rearrange("(k p) c -> p k c", p=P)
            for c in range(KD):
                for a in range(2):
                    load(w_d[:, FK // 2 * a:FK // 2 * (a + 1), P * c:P * c + P],
                         lambda r: r[:, 0:FK // 2 * P].rearrange("p (k c) -> p k c", c=P))
            for t in range(NT):
                sp.wait_ge(final_act, t + 1)
                sp.wait_ge(final_dve, t + 1)
                sp.dma_start(out[0, t * P:(t + 1) * P, :], out_rows_sb[:, t, :]).then_inc(stored, 16)
            sp.wait_ge(stored, 16 * NT)

        @block.tensor
        def _(pe):
            st = {"chunk": 0, "norm": 0, "n": 0}

            def next_slab(dmas=None):
                n = st["n"]
                st["n"] += 1
                if plan[n]["kind"] == "split":
                    pe.wait_ge(split_ready, plan[n]["splits"])
                else:
                    pe.wait_ge(slot_in[n % 2], plan[n]["arrived"])
                return n % 2

            def take_bank(at):
                count, b = at if at else (st["chunk"], st["chunk"] % 4)
                if st["chunk"] >= 4:
                    pe.wait_ge(chunk_out, count - 3)
                if at is None:
                    st["chunk"] += 1
                return b

            def chunk(weights, kt, rhs, n_rhs, first=True, last=True):
                b = take_bank(None) if first else (st["chunk"] - 1) % 4
                for k in range(kt):
                    mm = pe.matmul(psum[b][:, 0:n_rhs], weights(k), rhs(k), start=(first and k == 0), stop=(last and k == kt - 1))
                if last:
                    mm.then_inc(chunk_done, 1)
                return mm

            def product3(o, a_hi, a_lo, b_hi, b_lo, tiles_ready=None):
                for k in range(KD):
                    if tiles_ready is not None:
                        pe.wait_ge(h_ready, tiles_ready + k + 1)
                    pe.matmul(o, a_hi(k), b_hi(k), start=(k == 0), stop=False)
                    pe.matmul(o, a_hi(k), b_lo(k), start=False, stop=False)
                    mm = pe.matmul(o, a_lo(k), b_hi(k), start=False, stop=(k == KD - 1))
                return mm

            def chunk3(slot, c, at=None, tiles_ready=None):
                b = take_bank(at)
                product3(psum[b][:, :], lambda k: w_hi[:, slot, k * 256 + c:k * 256 + c + P],
                         lambda k: w_lo[:, slot, k * 256 + c:k * 256 + c + P],
                         lambda k: h_hi[:, k, :], lambda k: h_lo[:, k, :], tiles_ready).then_inc(chunk_done, 1)

            def rows3(t, w, n, c=0):
                b = take_bank(None)
                tok_t = slice(t * P, (t + 1) * P)
                product3(psum[b][:, 0:n], lambda k: h_hi[:, k, tok_t], lambda k: h_lo[:, k, tok_t],
                         lambda k: w[0](k)[:, c:c + n], lambda k: w[1](k)[:, c:c + n]).then_inc(chunk_done, 1)

            def norm_sum():
                base = 8 * st["norm"]
                for k in range(KD):
                    norm_sum_tile(k)
                st["norm"] += 1

            def norm_sum_tile(k):
                base = 8 * st["norm"]
                pe.wait_ge(square_ready, base + k + 1)
                pe.matmul(psum[7][:, :], ones, sq[:, k % 2, :], start=(k == 0), stop=(k == KD - 1)).then_inc(square_used, 1)

            def post_norm_layer(out_chunk):
                for c in range(KD):
                    out_chunk(c)
                base = 8 * st["norm"]
                pe.wait_ge(square_used, base + KD - 1)
                pe.matmul(psum[7][:, :], ones, rs[:, :], start=True, stop=False)
                pe.wait_ge(square_ready, base + KD)
                pe.matmul(psum[7][:, :], ones, sq[:, (KD - 1) % 2, :], start=False, stop=True).then_inc(square_used, 1)
                st["norm"] += 1

            pe.wait_ge(consts_in, 16)
            pe.wait_ge(rows_in, 16 * 19)
            for m, n in enumerate((128, 54, 88, 88, 88)):
                mm = pe.transpose(psum[m % 4][:, 0:n], par_rows[0:n, m, :], ident[0:n, 0:n])
                mm.then_inc(turned, 1)
                if m == 3:
                    pe.wait_ge(turned_used, 1)
            pe.wait_ge(x_in, 16)
            for k in range(KD):
                pe.wait_ge(turned_used, k + 2)
                for t in range(NT):
                    mm = pe.transpose(psum[(k + 1) % 4][:, t * P:(t + 1) * P], x_rows[:, t, k * P:(k + 1) * P], ident)
                mm.then_inc(turned, 1)
            norm_sum()
            pe.wait_ge(h_ready, 8)
            pe.wait_ge(ws_ready, 1)
            for t in range(NT):
                tok_t = slice(t * P, (t + 1) * P)
                mm = product3(psum[4][:, 32 * t:32 * t + 32], lambda k: h_hi[:, k, tok_t], lambda k: h_lo[:, k, tok_t],
                              lambda k: ws_hi[:, k, :], lambda k: ws_lo[:, k, :])
            mm.then_inc(ba_done, 1)

            def token_sums():
                pe.wait_ge(tok_dve, 1)
                for n, m in enumerate((upper, same, half0, half1)):
                    mm = pe.matmul(psum[5][:, 64 * n:64 * n + 64], m, g_log, start=True, stop=True)
                mm.then_inc(cum_done, 1)

            def project(n, tiles):
                for k in tiles:
                    if k == 0:
                        if n % 2 == 0:
                            st["slot"] = next_slab()
                        st["bank"] = take_bank(None)
                    b, w = st["bank"], slice(k * 256 + P * (n % 2), k * 256 + P * (n % 2) + P)
                    pe.matmul(psum[b][:, :], w_hi[:, st["slot"], w], h_hi[:, k, :], start=(k == 0), stop=False)
                    pe.matmul(psum[b][:, :], w_hi[:, st["slot"], w], h_lo[:, k, :], start=False, stop=False)
                    mm = pe.matmul(psum[b][:, :], w_lo[:, st["slot"], w], h_hi[:, k, :], start=False, stop=(k == KD - 1))
                    if k == KD - 1:
                        mm.then_inc(chunk_done, 1)

            def head_sums(g):
                for n in range(4):
                    pe.wait_ge(l2_sq, 4 * g + n + 1)
                    b = take_bank(None)
                    pe.matmul(psum[b][:, :], ones, squares[n], start=True, stop=True).then_inc(chunk_done, 1)

            for n in range(8):
                project(n, range(KD))
                if n == 1:
                    token_sums()
            head_sums(0)
            project(8, range(KD))
            project(9, range(KD))
            for g in range(GROUPS):
                q_T, k_T, v_T = q_of[g % 2], k_of[g % 2], v_of[g % 2]
                ahead = g + 1 < GROUPS
                pe.wait_ge(qk_ready, 4 * g + 4)
                for j in range(2):
                    for n in range(2):
                        rhs = (k_T, q_T)[n]
                        if g:
                            pe.wait_ge(gate_ready, 4 * g - 3 + 2 * j + n)
                        for t in range(NT):
                            mm = pe.matmul(psum[4 + 2 * j + n][:, t * P:(t + 1) * P], k_T[j][:, t * P:(t + 1) * P],
                                           rhs[j][:, t * P:(t + 1) * P], start=True, stop=True)
                        mm.then_inc(kk_done, 1)
                for j in range(2):
                    pe.wait_ge(kk_ready, 4 * g + 2 * j + 1)
                    for t in range(NT):
                        mm = pe.transpose(psum[4 + 2 * j][:, t * P:(t + 1) * P], k_T[j][:, t * P:(t + 1) * P], ident)
                    mm.then_inc(kr_done, 1)
                for h in range(HG):
                    if h % 2 == 0:
                        pe.wait_ge(kr_ready, 2 * g + h // 2 + 1)
                    else:
                        pe.wait_ge(kk_ready, 4 * g + h + 1)
                    pe.wait_ge(silu_done, 8 * g + 8)
                    for t in range(NT):
                        mm = pe.transpose(psum[4 + h][:, t * P:(t + 1) * P], v_T[:, h, t * P:(t + 1) * P], ident)
                    mm.then_inc(vt_done, 1)
                pe.wait_ge(grp_ready, g + 1)
                for h in range(HG):
                    pe.wait_ge(vb_ready, 4 * g + h + 1)
                    for t in range(NT):
                        o = psum[4 + h][:, t * P:(t + 1) * P]
                        pe.matmul(o, grp[:, 0, 4 * t + h:4 * t + h + 1].to_broadcast([P, P]), upper, start=True, stop=False)
                        mm = pe.matmul(o, ident, negmask, start=False, stop=True)
                    mm.then_inc(gb_done, 1)
                for h in range(HG):
                    pe.wait_ge(decay_ready, 4 * g + h + 1)
                    for t in range(NT):
                        mm = pe.matmul(psum[4 + h][:, t * P:(t + 1) * P],
                                       grp[:, 1, 4 * t + h:4 * t + h + 1].to_broadcast([P, P]), ident, start=True, stop=True)
                    mm.then_inc(bb_done, 1)
                for pair in range(2):
                    for lv in range(5):
                        n0 = 20 * g + 10 * pair + 2 * lv
                        step = 2 * (5 * pair + lv)
                        if step < 2 * KD:
                            project(10 + step // KD, [step % KD])
                        for j in range(2):
                            h = 2 * pair + j
                            if lv == 0:
                                pe.wait_ge(y_start, 4 * g + h + 1)
                            else:
                                pe.wait_ge(y_ready, n0 + j - 1)
                            for t in range(NT):
                                mm = pe.transpose(psum[4 + h][:, t * P:(t + 1) * P], Y_T[:, h, t * P:(t + 1) * P], ident)
                            mm.then_inc(xt_done, 1)
                        if step < 2 * KD:
                            project(10 + step // KD, [step % KD + 1])
                        for j in range(2):
                            h = 2 * pair + j
                            pe.wait_ge(xt_ready, n0 + j + 1)
                            pe.wait_ge(level_ready, n0 + j + 1)
                            for t in range(NT):
                                mm = pe.matmul(psum[4 + h][:, t * P:(t + 1) * P], decay[:, j, t * P:(t + 1) * P],
                                               kk[:, j, t * P:(t + 1) * P], start=True, stop=True)
                            mm.then_inc(p_done, 1)
                        for j in range(2):
                            h = 2 * pair + j
                            pe.wait_ge(p_ready, n0 + j + 1)
                            for t in range(NT):
                                mm = pe.matmul(psum[4 + h][:, t * P:(t + 1) * P], kq[:, j, t * P:(t + 1) * P],
                                               Y_T[:, h, t * P:(t + 1) * P], start=True, stop=True)
                            mm.then_inc(py_done, 1)
                pe.wait_ge(y_ready, 20 * g + 20)
                for c in range(8):
                    rows, t = halves(c)
                    i = slice(CH * c, CH * c + CH)
                    n0 = 32 * g + 4 * c
                    if ahead:
                        project(c, [0, 1])
                    for h in range(HG):
                        pe.wait_ge(state_ready, 36 * g + 4 * c + h + 1)
                        if c >= 1:
                            pe.wait_ge(scan_done, n0 + h - 3)
                        pe.matmul(psum[4 + h][rows, 0:P], k_T[h // 2][:, i], state[:, h, :], start=True, stop=True)
                        pe.matmul(psum[4 + h][rows, P:2 * P], q_T[h // 2][:, i], state[:, h, :], start=True, stop=True)\
                            .then_inc(ks_done, 1)
                    if ahead:
                        project(c, [2, 3, 4])
                    for h in range(HG):
                        pe.wait_ge(resid_ready, n0 + h + 1)
                        pe.matmul(psum[4 + h][rows, 0:P], Y_T[rows, h, i], resid[rows, h, :], start=True, stop=True)\
                            .then_inc(vn_done, 1)
                    if ahead:
                        project(c, [5, 6, 7])
                    for h in range(HG):
                        pe.wait_ge(vn_ready, n0 + h + 1)
                        pe.matmul(psum[4 + h][:, P:2 * P], k_rows[rows, h // 2, t * P:(t + 1) * P], v_dec[rows, h, :],
                                  start=True, stop=True)
                        pe.matmul(psum[4 + h][rows, 2 * P:3 * P], QK_T[rows, h, i], v_new[rows, h, :],
                                  start=True, stop=True).then_inc(su_done, 1)
                if ahead:
                    head_sums(g + 1)
                    project(8, range(KD))
                    project(9, range(KD // 2))
                for h in range(HG):
                    pe.wait_ge(ssq_ready, 4 * g + h + 1)
                    for tt in range(NT):
                        mm = pe.transpose(psum[4 + h][:, tt * P:(tt + 1) * P], v_T[:, h, tt * P:(tt + 1) * P], ident)
                    mm.then_inc(ot_done, 1)
                if ahead:
                    project(9, range(KD // 2, KD))
            pe.wait_ge(gate_ready, 16)

            def gdn_out(c):
                pos = next_slab()
                chunk(lambda k: ring[:, pos, k * P:(k + 1) * P], VH, lambda k: gate_out[:, k, :], S)

            post_norm_layer(gdn_out)
            norm_sum()
            for i in passes(pe, SC // 256):
                for n in range(8):
                    if n % 2 == 0:
                        pe.wait_ge(split_ready, plan[SC0]["splits"] + 4 * i + n // 2)
                    chunk3(n // 2 % 2, P * (n % 2), at=(st["chunk"] + 8 * i + n, n % 4),
                           tiles_ready=8 if n == 0 else None)
            st["chunk"] += 64
            st["n"] += 32

            def sc_proj(c):
                if c == 0:
                    pe.wait_ge(sc_used, SC // P + 1)
                pos = next_slab()
                chunk(lambda k: ring[:, pos, k * P:(k + 1) * P], SC // P, lambda k: sc_out[:, k, :], S)

            post_norm_layer(sc_proj)
            pe.wait_ge(hot_in, 16)
            pe.wait_ge(rel_in, 16)
            pe.wait_ge(chunk_out, st["chunk"])
            for n in range(4):
                pe.matmul(psum[3 + n][0:ATT_H, :], rel, hot[0:REL + 1, n // 2, 512 * (n % 2):512 * (n % 2) + 512],
                          start=True, stop=True).then_inc(table_done, 1)
            pe.wait_ge(table_out, 4)
            norm_sum()
            slab = lambda pos, c: (lambda k: ring[:, pos, k * 256 + c:k * 256 + c + P])
            wide3 = lambda pos: [lambda k, w=w: w[:, pos, k * 256:k * 256 + 256] for w in (w_hi, w_lo)]
            for kind in "qqcvvpuv":
                pos = next_slab()
                first = {"tiles_ready": 16} if st["n"] == MIX0 + 1 else {}
                if st["n"] < MIX0 + 8:
                    chunk3(pos, 0, **first)
                if st["n"] in (MIX0 + 4, MIX0 + 5):
                    for t in range(NT):
                        rows3(t, wide3(pos), P, P)
                elif st["n"] < MIX0 + 8:
                    chunk3(pos, P)
                else:
                    for t in range(NT):
                        rows3(t, wide3(pos), 256)
            pe.wait_ge(ws_ready, 2)
            for t in range(NT):
                rows3(t, [lambda k: ws_hi[:, k, 0:24], lambda k: ws_lo[:, k, 0:24]], 24)
            pe.wait_ge(mixer_in, MIXER_IN)
            pe.transpose(psum[4][:, 0:64], pos_rows[0:64, :], ident[0:64, 0:64]).then_inc(turn_done, 1)
            for h in range(4):
                mm = pe.transpose(psum[5][:, h * P:(h + 1) * P], spatial_rows[:, h, :], ident)
            mm.then_inc(turn_done, 1)
            pe.wait_ge(bias_in, 32)
            for qi in range(NT):
                pe.wait_ge(turn_out, 1)
                for h in range(ATT_H):
                    mm = pe.transpose(psum[(6, 7, 4, 6)[qi]][:, NC * h:NC * h + NC], bias_cmp_T[0:NC, h, qi * P:(qi + 1) * P], ident[0:NC, 0:NC])
                mm.then_inc(turn_done, 1)
                if qi == 2:
                    pe.wait_ge(turn_out, 2)
            w_c1 = ring[:, :, :].rearrange("p r (x h) -> p (r x) h", h=P)
            blk = blocks.rearrange("p (l c) -> p l c", c=NC)
            for kind in range(2):
                next_slab()
                next_slab()
                pe.wait_ge(blocks_ready, kind + 1)
                pe.wait_ge(turn_out, 4)
                pe.wait_ge(mask_done, 1)
                for g in range(2):
                    f = slice(64 * g, 64 * g + 64)
                    for l in range(32):
                        mm = pe.matmul(psum[4 + g][:, 32 * kind:32 * kind + NC], w_c1[f, l, :], blk[f, l, :],
                                       start=(l == 0), stop=(l == 31))
                mm.then_inc(hid_done, 1)
            pe.wait_ge(hid_ready, 1)
            pe.wait_ge(turn_out, 5)
            for g in range(2):
                pe.matmul(psum[6][64 * g:64 * g + 64, 0:NC], w_c2[:, 0, :], hidden[:, g, :], start=True, stop=True)
            for g in range(2):
                mm = pe.matmul(psum[7][0:NC, 64 * g:64 * g + 64], hidden[:, 2 + g, :], w_c2[:, 1, :], start=True, stop=True)
            mm.then_inc(c2_done, 1)
            pe.wait_ge(sgu_norm, 1)
            for pair in range(2):
                for n in range(NT):
                    for f in range(2):
                        h = 2 * pair + f
                        mm = pe.matmul(psum[4 + pair][64 * f:64 * f + 64, n * P:(n + 1) * P], sgu_v[:, n, 64 * h:64 * h + 64],
                                       spatial_T[:, h, :], start=True, stop=True)
            mm.then_inc(spatial_done, 1)
            pe.wait_ge(pool_ready, 1)
            pe.wait_ge(c2_ready, 1)
            for c in range(2):
                if c:
                    pe.wait_ge(pool_out, 1)
                for f in range(2):
                    r = slice(64 * f, 64 * f + 64)
                    mm = pe.matmul(psum[6 + f][r, :], w_pool[r, c, :], pool_d[r, c, :], start=True, stop=True)
                mm.then_inc(pool_done, 1)
            pe.wait_ge(chunk_out, st["chunk"])
            pe.wait_ge(sgu_done, 2)
            pe.wait_ge(pool_out, 2)

            def scores(n):
                qi, kind, h = units[n]
                need = n if is_cmp(n) or is_cmp(n - 1) else n - 1
                if need > 0:
                    pe.wait_ge(score_read, need)
                tok_q = slice(qi * P, (qi + 1) * P)
                if kind == 0:
                    for hh in range(ATT_H):
                        f = slice(64 * (hh // 4), 64 * (hh // 4) + 64)
                        mm = pe.matmul(psum[hh // 4][:, 32 * (hh % 4):32 * (hh % 4) + NC], att_q[f, hh % 4, tok_q], cmp_k[f, :],
                                       start=True, stop=True)
                else:
                    f = slice(64 * (h // 4), 64 * (h // 4) + 64)
                    mm = pe.matmul(psum[n % 2][:, 0:P * (qi + 1)], att_q[f, h % 4, tok_q], att_k[f, kind - 1, 0:P * (qi + 1)],
                                   start=True, stop=True)
                mm.then_inc(score_done, 1)

            def turn_probs(n):
                qi, kind, h = units[n]
                pe.wait_ge(prob_ready, n + 1)
                need = n if is_cmp(n) or is_cmp(n - 1) else n - 1
                if need > 0:
                    pe.wait_ge(probT_out, need)
                if kind == 0:
                    for hh in range(ATT_H):
                        mm = pe.transpose(psum[2 + hh // 4][0:NC, P * (hh % 4):P * (hh % 4) + P], cmp_prob[:, hh, :], ident)
                else:
                    for j in range(qi + 1):
                        mm = pe.transpose(psum[2 + n % 2][:, P * j:P * j + P], prob[:, n % 4, P * j:P * j + P], ident)
                mm.then_inc(probT_done, 1)

            def values(n):
                qi, kind, h = units[n]
                pe.wait_ge(probT_out, n + 1)
                if qi and h == 0:
                    pe.wait_ge(combined, qi)
                if kind == 0:
                    pt = prob_T.rearrange("p a (h i) -> p (a h) i", i=P)
                    for hh in range(ATT_H):
                        mm = pe.matmul(psum[4][:, DH * hh:DH * hh + DH], pt[0:NC, hh, :], cmp_v[0:NC, 64 * (hh // 4):64 * (hh // 4) + 64],
                                       start=True, stop=True)
                else:
                    v0 = 128 * (kind - 1) + 64 * (h // 4)
                    for j in range(qi + 1):
                        mm = pe.matmul(psum[4 + kind][:, DH * h:DH * h + DH], prob_T[:, n % 2, P * j:P * j + P], att_v[:, j, v0:v0 + 64],
                                       start=(j == 0), stop=(j == qi))
                mm.then_inc(pv_done, 1)

            def turn_out_rows(qi):
                pe.wait_ge(combined, qi + 1)
                if qi:
                    pe.wait_ge(attT_out, qi)
                for c in range(4):
                    mm = pe.transpose(psum[7][:, c * P:(c + 1) * P], att_o[:, 0, c * P:(c + 1) * P], ident)
                mm.then_inc(attT_done, 1)

            for n in range(len(units) + 3):
                if n < len(units):
                    scores(n)
                if 0 <= n - 2 < len(units):
                    turn_probs(n - 2)
                if n >= 3:
                    values(n - 3)
                if n >= 22 and (n - 5) % 17 == 0:
                    turn_out_rows((n - 5) // 17 - 1)
            turn_out_rows(NT - 1)
            pe.wait_ge(attT_out, NT)

            def mix_proj(c):
                if c % 2 == 0:
                    st["slot"] = next_slab()
                chunk(slab(st["slot"], 128 * (c % 2)), KD, lambda k: mix_T[:, k, :], S)

            post_norm_layer(mix_proj)
            pe.wait_ge(mem_scaled, 1)
            for k in range(KD):
                if k >= 2:
                    pe.wait_ge(mem_turned_out, k - 1)
                for t in range(MT):
                    mm = pe.transpose(psum[4 + k % 2][:, t * P:(t + 1) * P], mem_rows[:, t, k * P:(k + 1) * P], ident)
                mm.then_inc(mem_turned, 1)
            pe.wait_ge(mem_turned_out, KD)
            for n in range(4):
                pos = next_slab()
                for side in range(2):
                    chunk(slab(pos, 128 * side), KD, lambda k: mem_T[:, k, :], MEM)
            for n in range(4):
                pos = next_slab()
                for t in range(MT):
                    chunk(lambda k: mem_T[:, k, t * P:(t + 1) * P], KD, lambda k: ring[:, pos, k * 256:k * 256 + 256], 256)
            norm_sum()
            for n in range(4):
                pos = next_slab()
                chunk3(pos, 0, tiles_ready=24 if n == 0 else None)
                chunk3(pos, P)
            pe.wait_ge(chunk_out, st["chunk"])
            for n in range(len(mem_units) + 3):
                if n < len(mem_units):
                    h, qi = mem_units[n]
                    if n >= 2:
                        pe.wait_ge(mp_exp, n - 1)
                    for c in range(2):
                        mm = pe.matmul(psum[4 + n % 2][:, 0:MEM], mem_q[:, 2 * h + c, qi * P:(qi + 1) * P], mem_k[:, 2 * h + c, :],
                                       start=(c == 0), stop=(c == 1))
                    mm.then_inc(ms_done, 1)
                m = n - 2
                if 0 <= m < len(mem_units):
                    pe.wait_ge(mp_ready, m + 1)
                    if m >= 2:
                        pe.wait_ge(mpT_out, m - 1)
                    for t in range(MT):
                        mm = pe.transpose(psum[6 + m % 2][:, t * P:(t + 1) * P], mem_prob[:, m % 4, t * P:(t + 1) * P], ident)
                    mm.then_inc(mpT_done, 1)
                m = n - 3
                if m >= 0 and m % 4 == 3:
                    h = m // 4
                    pe.wait_ge(mpT_out, m + 1)
                    for c in range(2):
                        chunk(lambda t: mem_v[:, t, HD * h + P * c:HD * h + P * c + P], MT, lambda t: mem_probT[:, 2 * (h % 2) + t, :], S)
            pe.wait_ge(chunk_out, st["chunk"])

            def mem_proj(c):
                if c % 2 == 0:
                    st["slot"] = next_slab()
                chunk(slab(st["slot"], 128 * (c % 2)), KD, lambda k: mem_out[:, k, :], S)

            post_norm_layer(mem_proj)
            norm_sum()
            assert st["chunk"] == FF0 and st["n"] == FF1
            for jj in passes(pe, FK // 2):
                for v in range(2):
                    pe.wait_ge(split_ready, plan[FF1 + v]["splits"] + 2 * jj)
                    for s in range(2):
                        chunk3(v, P * s, at=(FF0 + 4 * jj + 2 * v + s, 2 * v + s),
                               tiles_ready=32 if v + s == 0 else None)
            st["chunk"] += 2 * FK
            st["n"] += FK

            def down(c):
                for a in range(2):
                    pos = next_slab()
                    if c == 0:
                        pe.wait_ge(ff_ready, 12 if a == 0 else FK)
                    mm = chunk(lambda k: ring[:, pos, k * P:(k + 1) * P], FK // 2, lambda k: ff_hid[:, FK // 2 * a + k, :], S,
                               first=(a == 0), last=(a == 1))
                    if a == 0:
                        mm.then_inc(half_used, 1)

            post_norm_layer(down)
            pe.wait_ge(x_ready, 40)
            for t in range(NT):
                for a in range(2):
                    for k in range(4):
                        mm = pe.transpose(psum[2 * t + a][:, k * P:(k + 1) * P], xT[:, 4 * a + k, t * P:(t + 1) * P], ident)
                    mm.then_inc(final_done, 1)

        @block.scalar
        def _(act):
            own = Tally(act, act_step)
            st = {"chunk": 0, "norm": 0, "pre": 0}

            def split_hi(n, arrived=None, used=None, split=None):
                if arrived is None:
                    arrived = plan[n]["arrived"]
                    old = [p for p in plan[:n] if p["kind"] == "split"][-2:]
                    used = old[0]["end"] if len(old) == 2 else None
                act.wait_ge(slot_in[n % 2], arrived)
                if used is not None:
                    act.wait_ge(chunk_done, used)
                act.activation(w_hi[:, n % 2, :], ring[:, n % 2, :], ACT.Copy).then_inc(w_hi_ready, 1)

            def split_input():
                for k in range(KD):
                    n = 8 * st["pre"] + k
                    act.wait_ge(h32_ready, n + 1)
                    act.activation(h_hi[:, k, :], y_T[:, k, :], ACT.Copy).then_inc(h_hi_ready, 1)
                st["pre"] += 1

            def inverse_rms(bank, out_, scale, done, tmp=None):
                own.did(act.activation(out_, bank, ACT.Ln, bias=eps, scale=scale))
                own.settle()
                act.activation(out_, out_, ACT.Exp, scale=-0.5).then_inc(done, 1)

            def square_tile(k, src):
                n = 8 * st["norm"] + k
                if n >= 2:
                    act.wait_ge(square_used, n - 1)
                act.activation(sq[:, k % 2, :], src, ACT.Square).then_inc(square_ready, 1)

            def norm_rms():
                act.wait_ge(square_used, 8 * st["norm"] + 8)
                if st["norm"] >= 1:
                    pre, post = (st["norm"] + 1) // 2, st["norm"] // 2
                    act.wait_ge(h_ready, 8 * pre)
                    if post:
                        act.wait_ge(x_ready, 8 * post)
                inverse_rms(psum[7][:, :], rs[:, :], 1.0 / D, rms_ready)
                st["norm"] += 1

            def pre_norm():
                act.wait_ge(x_ready, 8 * (st["norm"] // 2))
                for k in range(KD):
                    square_tile(k, xT[:, k, :])
                norm_rms()
                split_input()

            def post_norm(y_T=y_T):
                for k in range(KD):
                    n = st["chunk"]
                    act.wait_ge(chunk_done, n + 1)
                    square_tile(k, psum[n % 4][:, :])
                    act.activation(y_T[:, k, :], psum[n % 4][:, :], ACT.Copy).then_inc(chunk_out, 1)
                    st["chunk"] += 1
                norm_rms()

            for m, n in enumerate((128, 54, 88, 88, 88)):
                act.wait_ge(turned, m + 1)
                act.activation(cols[:, m, 0:n], psum[m % 4][:, 0:n], ACT.Copy).then_inc(turned_used, 1)
            for k in range(KD):
                act.wait_ge(turned, 6 + k)
                act.activation(xT[:, k, :], psum[(k + 1) % 4][:, :], ACT.Copy).then_inc(turned_used, 1)
            act.wait_ge(turned_used, 13)
            act.wait_ge(eps_set, 2)
            for k in range(KD):
                square_tile(k, xT[:, k, :])
            norm_rms()
            act.wait_ge(wba_in, 48)
            act.activation(ws_hi[:, :, :], wba, ACT.Copy).then_inc(ws_hi_ready, 1)
            split_hi(0)
            split_input()
            split_hi(1)
            act.wait_ge(tok_act, 1)
            own.did(act.activation(beta, tmpA, ACT.Exp, scale=-1.0))
            own.settle()
            own.did(act.activation(tmpA, tmpB, ACT.Exp, scale=-1.0))
            own.settle()
            own.did(act.activation(tmpA, tmpA, ACT.Ln, bias=1.0))
            act.activation(alog[:, 0, :], alog[:, 0, :], ACT.Exp).then_inc(tok_exp, 1)

            def token_exps():
                act.wait_ge(tok_act, 2)
                own.did(act.activation(e_G, G_cum, ACT.Exp))
                own.did(act.activation(e_rest, tmpB, ACT.Exp))
                own.did(act.activation(end0, end0, ACT.Exp))
                act.activation(end1, end1, ACT.Exp).then_inc(tok_exp, 1)

            def silu(g, n):
                dst = (q_of[g % 2] + k_of[g % 2])[n] if n < 4 else v_of[g % 2][:, n - 4, :]
                act.wait_ge(conv_done, 8 * g + n + 1)
                act.activation(dst, dst, ACT.Silu).then_inc(silu_done, 1)

            def projected(g, n):
                c = st["chunk"]
                act.wait_ge(chunk_done, c + 1)
                if n < 8:
                    if 8 * g + n >= 3:
                        act.wait_ge(conv_done, 8 * g + n - 2)
                    if n == 0 and g:
                        act.wait_ge(qk_ready, 4 * g)
                    act.activation(raw[:, n % 3, :], psum[c % 4][:, :], ACT.Copy).then_inc(chunk_out, 1)
                else:
                    if g and n == 8:
                        act.wait_ge(gate_ready, 4 * g)
                    act.activation(z_T[:, n - 8, :], psum[c % 4][:, :], ACT.Silu).then_inc(chunk_out, 1)
                st["chunk"] += 1
                if n % 2 == 1 and 6 * g + n // 2 + 2 < 24:
                    split_hi(6 * g + n // 2 + 2)

            for n in range(8):
                projected(0, n)
                if n == 3:
                    token_exps()
                if n:
                    silu(0, n - 1)
            silu(0, 7)

            def head_logs(g):
                for n in range(4):
                    c = st["chunk"]
                    act.wait_ge(chunk_done, c + 1)
                    act.activation(squares[n], psum[c % 4][:, :], ACT.Ln, bias=eps).then_inc(chunk_out, 1)
                    st["chunk"] += 1

            def head_norms():
                for n in range(4):
                    act.wait_ge(chunk_out, st["chunk"] - 3 + n)
                    act.activation(squares[n], squares[n], ACT.Exp, scale=-0.5).then_inc(l2_rms, 1)

            head_logs(0)
            head_norms()
            for g in range(GROUPS):
                ahead = g + 1 < GROUPS
                v_T = v_of[g % 2]
                for n in range(4):
                    act.wait_ge(kk_done, 4 * g + n + 1)
                    dst = (kk, kq)[n % 2][:, n // 2, :]
                    act.activation(dst, psum[4 + n][:, :], ACT.Copy).then_inc(kk_ready, 1)
                for j in range(2):
                    act.wait_ge(kr_done, 2 * g + j + 1)
                    act.activation(k_rows[:, j, :], psum[4 + 2 * j][:, :], ACT.Copy).then_inc(kr_ready, 1)
                projected(g, 8)
                projected(g, 9)
                for h in range(HG):
                    act.wait_ge(gb_done, 4 * g + h + 1)
                    act.wait_ge(grp_ready, g + 1)
                    if h >= 2:
                        act.wait_ge(decay_used, 4 * g + h - 1)
                    for t in range(NT):
                        col = neg_G[:, 16 * t + 4 * g + h:16 * t + 4 * g + h + 1]
                        ins = act.activation(decay[:, h % 2, t * P:(t + 1) * P], psum[4 + h][:, t * P:(t + 1) * P],
                                             ACT.Exp, bias=col)
                    ins.then_inc(decay_ready, 1)
                for pair in range(2):
                    for lv in range(5):
                        n0 = 20 * g + 10 * pair + 2 * lv
                        for j in range(2):
                            act.wait_ge(xt_done, n0 + j + 1)
                            if lv or pair:
                                act.wait_ge(p_done, n0 + j - 1)
                            act.activation(kk[:, j, :], psum[4 + 2 * pair + j][:, :], ACT.Copy).then_inc(xt_ready, 1)
                        for j in range(2):
                            act.wait_ge(p_done, n0 + j + 1)
                            act.wait_ge(py_done, n0 + j - 1) if (lv or pair) else None
                            act.activation(kq[:, j, :], psum[4 + 2 * pair + j][:, :], ACT.Copy).then_inc(p_ready, 1)
                        if 5 * pair + lv in (5, 8):
                            projected(g, 10 if 5 * pair + lv == 5 else 11)
                for c in range(8):
                    rows, t = halves(c)
                    n0 = 32 * g + 4 * c
                    if ahead and c:
                        projected(g + 1, c - 1)
                    if ahead and c >= 2:
                        silu(g + 1, c - 2)
                    for h in range(HG):
                        col = 16 * t + 4 * g + h
                        act.wait_ge(vn_done, n0 + h + 1)
                        if c:
                            act.wait_ge(su_done, n0 + h - 3)
                        act.activation(v_new[rows, h, :], psum[4 + h][rows, 0:P], ACT.Copy)
                        act.activation(v_dec[rows, h, :], psum[4 + h][rows, 0:P], ACT.Copy,
                                       scale=e_rest[rows, col:col + 1]).then_inc(vn_ready, 1)
                if ahead:
                    projected(g + 1, 7)
                    silu(g + 1, 6)
                    silu(g + 1, 7)
                    head_logs(g + 1)
                for h in range(HG):
                    act.wait_ge(scan_done, 32 * g + 32)
                    act.wait_ge(vn_ready, 32 * g + 32)
                    for t in range(NT):
                        own.did(act.activation(A_T[:, h, t * P:(t + 1) * P], v_T[:, h, t * P:(t + 1) * P], ACT.Square,
                                               accum_out=ssq[:, 0, 4 * h + t:4 * h + t + 1]))
                own.settle()
                own.did(act.activation(ssq[:, 1, :], ssq[:, 0, :], ACT.Ln, bias=eps, scale=1.0 / P))
                own.settle()
                act.activation(ssq[:, 1, :], ssq[:, 1, :], ACT.Exp, scale=-0.5).then_inc(l2_rms, 1)
                if ahead:
                    head_norms()
            post_norm()
            split_hi(SC0)
            split_hi(SC0 + 1)
            pre_norm()

            def sc_pass(i, last):
                for n in range(8):
                    act.wait_ge(chunk_done, st["chunk"] + 8 * i + n + 1)
                    if n == 0:
                        act.wait_ge(sc_used, 2 * i + 1)
                    act.activation(sc_in[:, n, :], psum[n % 4][:, :], ACT.Silu if n >= 6 else ACT.Copy).then_inc(chunk_out, 1)
                    if n % 2 == 1 and not (last and n >= 4):
                        m = n // 2 + 2
                        split_hi(SC0 + m, plan[SC0 + m]["arrived"] + 32 * i, plan[SC0 + m - 2]["end"] + 8 * i)

            for i in passes(act, SC // 256 - 1):
                sc_pass(i, False)
            sc_pass(SC // 256 - 1, True)
            st["chunk"] += 64
            post_norm()
            for n in range(4):
                act.wait_ge(table_done, n + 1)
                act.activation(table[0:ATT_H, n // 2, 512 * (n % 2):512 * (n % 2) + 512], psum[3 + n][0:ATT_H, :], ACT.Copy)\
                    .then_inc(table_out, 1)
            split_hi(MIX0)
            split_hi(MIX0 + 1)
            pre_norm()
            m0 = st["chunk"]
            act.wait_ge(w_gate_in, 16)
            act.wait_ge(ba_done, 1)
            act.activation(ws_hi[:, :, 0:24], w_gate, ACT.Copy).then_inc(ws_hi_ready, 1)

            def out_of_bank(dst, w, func=ACT.Copy, scale=1.0):
                c = st["chunk"]
                act.wait_ge(chunk_done, c + 1)
                act.activation(dst, psum[c % 4][:, 0:w], func, scale=scale).then_inc(chunk_out, 1)
                st["chunk"] += 1

            GELU = ACT.Gelu_apprx_tanh
            for a in range(2):
                for c in range(2):
                    out_of_bank(att_q[:, 2 * a + c, :], S, scale=DH ** -0.5)
                split_hi(MIX0 + 2 + a)
            for c in range(2):
                out_of_bank(cmp_kv[:, c, :], S)
            split_hi(MIX0 + 4)
            for a in range(2):
                out_of_bank(att_k[:, a, :], S)
                for t in range(NT):
                    out_of_bank(att_v[:, t, 128 * a:128 * a + 128], P)
                split_hi(MIX0 + 5 + a)
            for c in range(2):
                out_of_bank(pool_x[:, c, :], S)
            split_hi(MIX0 + 7)
            for c in range(2):
                out_of_bank(sgu_u[:, c, :], S, GELU)
            for t in range(NT):
                out_of_bank(sgu_v[:, t, :], 256, GELU)
            for t in range(NT):
                out_of_bank(gate_raw[:, t, :], 24)
            act.wait_ge(chunk_out, m0 + 28)
            act.activation(gate, gate_raw, ACT.Exp, scale=-1.0).then_inc(gate_exp, 1)
            act.wait_ge(turn_done, 1)
            act.activation(pos_T, psum[4][:, 0:64], ACT.Copy).then_inc(turn_out, 1)
            for qi in range(NT):
                act.wait_ge(turn_done, 3 + qi)
                act.activation(bias_cmp[:, qi, :], psum[(6, 7, 4, 6)[qi]][:, 0:ATT_H * NC], ACT.Copy).then_inc(turn_out, 1)
            for kind in range(2):
                act.wait_ge(hid_done, kind + 1)
            for kind in range(2):
                for g in range(2):
                    ins = act.activation(hidden[:, 2 * kind + g, :], psum[4 + g][:, 32 * kind:32 * kind + NC], ACT.Gelu_apprx_tanh,
                                         bias=cols[:, 1, 51 + kind:52 + kind])
            ins.then_inc(hid_ready, 1)
            act.wait_ge(var_ready, 1)
            own.did(act.activation(small[:, 5:9], small[:, 5:9], ACT.Ln, bias=eps, scale=1.0 / 256))
            own.settle()
            act.activation(small[:, 5:9], small[:, 5:9], ACT.Exp, scale=-0.5).then_inc(rstd_ready, 1)
            for c in range(2):
                act.wait_ge(pool_done, c + 1)
                for f in range(2):
                    r = slice(64 * f, 64 * f + 64)
                    ins = act.activation(mix_T[r, 4 + c, :], psum[6 + f][r, :], ACT.Copy, scale=PSC(c)[r])
                ins.then_inc(pool_out, 1)

            def out_rows(qi):
                act.wait_ge(attT_done, qi + 1)
                act.activation(mix_T[:, 0:4, qi * P:(qi + 1) * P], psum[7][:, :].rearrange("p (c i) -> p c i", c=4), ACT.Copy)\
                    .then_inc(attT_out, 1)

            for n in range(len(units)):
                qi, kind, h = units[n]
                act.wait_ge(score_read, n + 1)
                if kind == 0:
                    act.activation(cmp_prob, cmp_prob, ACT.Exp).then_inc(prob_ready, 1)
                else:
                    if qi >= 2:
                        act.wait_ge(combined, qi - 1)
                    p = prob[:, n % 4, 0:P * (qi + 1)]
                    act.activation(p, p, ACT.Exp, bias=neg_max(n), accum_out=sums(qi, kind)[:, h:h + 1]).then_inc(prob_ready, 1)
                if n >= 22 and (n - 5) % 17 == 0:
                    out_rows((n - 5) // 17 - 1)
            out_rows(NT - 1)
            post_norm()
            act.wait_ge(mem_in, 16)
            for t in range(MT):
                own.did(act.activation(mem_junk, mem_rows[:, t, :], ACT.Square, accum_out=small[:, 1 + t:2 + t]))
                own.settle()
            own.did(act.activation(small[:, 1:3], small[:, 1:3], ACT.Ln, bias=eps, scale=1.0 / D))
            own.settle()
            act.activation(small[:, 1:3], small[:, 1:3], ACT.Exp, scale=-0.5).then_inc(mem_rstd, 1)
            for k in range(KD):
                act.wait_ge(mem_turned, k + 1)
                act.activation(mem_T[:, k, :], psum[4 + k % 2][:, 0:MEM], ACT.Copy, scale=KVW(k)).then_inc(mem_turned_out, 1)
            for c in range(KD):
                act.wait_ge(chunk_done, st["chunk"] + 1)
                act.activation(mem_k[:, c, :], psum[st["chunk"] % 4][:, 0:MEM], ACT.Copy).then_inc(chunk_out, 1)
                st["chunk"] += 1
            for n in range(4):
                for t in range(MT):
                    act.wait_ge(chunk_done, st["chunk"] + 1)
                    act.activation(mem_v[:, t, 256 * n:256 * n + 256], psum[st["chunk"] % 4][:, 0:256], ACT.Copy).then_inc(chunk_out, 1)
                    st["chunk"] += 1
            split_hi(MEM0 + 8)
            split_hi(MEM0 + 9)
            pre_norm()
            for c in range(KD):
                act.wait_ge(chunk_done, st["chunk"] + 1)
                act.activation(mem_q[:, c, :], psum[st["chunk"] % 4][:, :], ACT.Copy).then_inc(chunk_out, 1)
                st["chunk"] += 1
                if c in (1, 3):
                    split_hi(MEM0 + 10 + c // 2)
            pv0 = st["chunk"]
            for n in range(len(mem_units) + 4):
                if n < len(mem_units):
                    act.wait_ge(ms_max, n + 1)
                    if n >= 4:
                        act.wait_ge(mpT_done, n - 3)
                    act.activation(mem_prob[:, n % 4, :], psum[4 + n % 2][:, 0:MEM], ACT.Exp, bias=mem_max(n), scale=HD ** -0.5,
                                   accum_out=mem_sum(n)).then_inc(mp_exp, 1)
                m = n - 2
                if 0 <= m < len(mem_units):
                    h, qi = mem_units[m]
                    act.wait_ge(mpT_done, m + 1)
                    if h >= 2:
                        act.wait_ge(chunk_done, pv0 + 2 * (h - 1))
                    act.activation(mem_probT[:, 2 * (h % 2):2 * (h % 2) + 2, qi * P:(qi + 1) * P],
                                   psum[6 + m % 2][:, 0:MEM].rearrange("p (t i) -> p t i", t=MT), ACT.Copy).then_inc(mpT_out, 1)
                m = n - 4
                if m >= 0 and m % 4 == 3:
                    for c in range(2):
                        act.wait_ge(chunk_done, st["chunk"] + 1)
                        act.activation(mem_out[:, 2 * (m // 4) + c, :], psum[st["chunk"] % 4][:, :], ACT.Copy).then_inc(chunk_out, 1)
                        st["chunk"] += 1
            post_norm()
            split_hi(FF1)
            split_hi(FF1 + 1)
            pre_norm()

            def pair_act(jj, last=False):
                for n in range(4):
                    act.wait_ge(chunk_done, FF0 + 4 * jj + n + 1)
                    if n == 0:
                        act.wait_ge(ff_conv, 4 * jj + 1)
                    act.activation(ff_raw[:, n, :], psum[n][:, :], ACT.Copy).then_inc(chunk_out, 1)
                    if n >= 2:
                        act.wait_ge(ff_conv, 4 * jj + n)
                        act.activation(ff_gate[:, n - 2, :], ff_gate[:, n - 2, :], ACT.Gelu_apprx_tanh).then_inc(ff_gelu, 1)
                    if n % 2 == 1 and not last:
                        v = n // 2
                        split_hi(FF1 + v, plan[FF1 + 2 + v]["arrived"] + 16 * jj, plan[FF1 + v]["end"] + 4 * jj)

            for i in passes(act, FK // 2 - 1):
                pair_act(i)
            pair_act(FK // 2 - 1, True)
            st["chunk"] += 2 * FK
            post_norm(ff_y)
            act.wait_ge(chunk_done, FF0 + 52)
            for t in range(NT):
                act.wait_ge(final_done, 2 * t + 1)
                act.activation(out_rows_sb[:, t, 0:512], psum[2 * t][:, :], ACT.Copy).then_inc(final_act, 1)

        @block.vector
        def _(dve):
            own = Tally(dve, dve_step)
            st = {"pre": 0, "post": 0}

            def split_lo(n, count=None):
                dve.wait_ge(w_hi_ready, plan[n]["splits"] if count is None else count)
                dve.tensor_tensor(w_lo[:, n % 2, :], ring[:, n % 2, :], w_hi[:, n % 2, :].bitcast(F32), ALU.subtract)\
                    .then_inc(split_ready, 1)

            def pre_norm():
                n = st["pre"] + st["post"]
                dve.wait_ge(rms_ready, n + 1)
                for k in range(KD + 2):
                    if k < KD:
                        dve.scalar_tensor_tensor(out=y_T[:, k, :], in0=xT[:, k, :], scalar=PRE[st["pre"]](k), in1=rs[:, :],
                                                 op0=ALU.mult, op1=ALU.mult).then_inc(h32_ready, 1)
                    if k >= 2:
                        dve.wait_ge(h_hi_ready, 8 * st["pre"] + k - 1)
                        dve.tensor_tensor(h_lo[:, k - 2, :], y_T[:, k - 2, :], h_hi[:, k - 2, :].bitcast(F32), ALU.subtract)\
                            .then_inc(h_ready, 1)
                st["pre"] += 1

            def post_norm(y_T=y_T):
                n = st["pre"] + st["post"]
                dve.wait_ge(h_ready, 8 * st["pre"])
                for k in range(KD - 1):
                    dve.wait_ge(square_ready, 8 * n + k + 1)
                    if k == 0:
                        dve.tensor_copy(rs[:, :], sq[:, 0, :]).then_inc(square_used, 1)
                    else:
                        dve.wait_ge(square_used, 8 * n + k)
                        dve.tensor_tensor(rs[:, :], rs[:, :], sq[:, k % 2, :], ALU.add).then_inc(square_used, 1)
                dve.wait_ge(rms_ready, n + 1)
                for k in range(KD):
                    own.did(dve.scalar_tensor_tensor(out=y_T[:, k, :], in0=y_T[:, k, :], scalar=POST[st["post"]](k),
                                                     in1=rs[:, :], op0=ALU.mult, op1=ALU.mult))
                own.settle()
                if st["post"] == 0:
                    dve.wait_ge(x_back, 16)
                for k in range(KD):
                    dve.tensor_tensor(xT[:, k, :], xT[:, k, :], y_T[:, k, :], ALU.add).then_inc(x_ready, 1)
                st["post"] += 1

            def conv(dst, src, taps, weight, bias=None):
                w = weight(taps - 1)
                if bias is None:
                    own.did(dve.tensor_scalar(dst, src, w, None, ALU.mult))
                else:
                    own.did(dve.tensor_scalar(dst, src, w, bias, ALU.mult, ALU.add))
                for s in range(1, taps):
                    own.settle()
                    ins = dve.scalar_tensor_tensor(out=dst[:, s:S], in0=src[:, 0:S - s], scalar=weight(taps - 1 - s),
                                                   in1=dst[:, s:S], op0=ALU.mult, op1=ALU.add)
                    if s < taps - 1:
                        own.did(ins)
                return ins

            dve.memset(small[:, :], NEG).then_inc(eps_set, 1)
            dve.wait_ge(eps_set, 1)
            dve.memset(eps, EPS).then_inc(eps_set, 1)
            dve.wait_ge(turned_used, 13)
            dve.wait_ge(ws_hi_ready, 1)
            dve.tensor_tensor(ws_lo[:, :, :], wba, ws_hi[:, :, :].bitcast(F32), ALU.subtract).then_inc(ws_ready, 1)
            split_lo(0)
            pre_norm()
            split_lo(1)
            dve.wait_ge(x_away, 16)
            dve.wait_ge(ba_done, 1)
            lg = psum[4][:, 0:128].rearrange("p (t c) -> p t c", t=NT)
            own.did(dve.tensor_copy(R4(tmpA), lg[:, :, 0:16]))
            own.did(dve.tensor_tensor(R4(g_log), lg[:, :, 16:32], alog[:, 1:2, :].to_broadcast([P, NT, VH]), ALU.add))
            own.settle()
            own.did(dve.tensor_scalar(tmpB, g_log, -1.0, None, ALU.mult))
            own.settle()
            dve.tensor_tensor(tmpB, tmpB, g_log, ALU.max).then_inc(tok_act, 1)
            dve.wait_ge(tok_exp, 1)
            own.did(dve.tensor_scalar(beta, beta, 1.0, None, ALU.add))
            own.settle()
            own.did(dve.reciprocal(beta, beta))
            own.did(dve.scalar_tensor_tensor(out=tmpA, in0=g_log, scalar=0.0, in1=tmpA, op0=ALU.max, op1=ALU.add))
            own.settle()
            own.did(dve.tensor_scalar(tmpA, tmpA, -1.0, None, ALU.mult))
            own.settle()
            dve.tensor_tensor(R4(g_log), R4(tmpA), alog[:, 0:1, :].to_broadcast([P, NT, VH]), ALU.mult).then_inc(tok_dve, 1)

            def token_columns():
                dve.wait_ge(cum_done, 1)
                own.did(dve.tensor_copy(G_cum, psum[5][:, 0:64]))
                own.did(dve.tensor_copy(G_end, psum[5][:, 64:128]))
                own.did(dve.tensor_copy(end0, psum[5][:, 128:192]))
                own.did(dve.tensor_copy(end1, psum[5][:, 192:256]))
                own.settle()
                own.did(dve.tensor_scalar(neg_G, G_cum, -1.0, None, ALU.mult))
                own.settle()
                dve.tensor_tensor(tmpB, G_end, G_cum, ALU.subtract).then_inc(tok_act, 1)

            def token_products():
                dve.wait_ge(tok_exp, 2)
                own.did(dve.tensor_tensor(neg_bG, beta, e_G, ALU.mult))
                own.settle()
                own.did(dve.tensor_scalar(neg_bG, neg_bG, -1.0, None, ALU.mult))
                own.settle()


            def convolved(g, n):
                dst = (q_of[g % 2] + k_of[g % 2])[n] if n < 4 else v_of[g % 2][:, n - 4, :]
                channel_tile = 2 * g + n if n < 2 else 8 + 2 * g + n - 2 if n < 4 else 16 + 4 * g + n - 4
                if g >= 2 and n == 0:
                    dve.wait_ge(su_done, 32 * (g - 1))
                    dve.wait_ge(ot_done, 4 * (g - 1))
                dve.wait_ge(chunk_out, 16 * g + n + 1)
                conv(dst, raw[:, n % 3, :], TAPS, lambda tap: GCONV(tap, channel_tile)).then_inc(conv_done, 1)

            for n in range(8):
                convolved(0, n)
                if n % 2 == 1:
                    split_lo(n // 2 + 2)
                if n == 1:
                    token_columns()

            def head_squares(g, heads):
                for n in heads:
                    q_or_k = (q_of[g % 2] + k_of[g % 2])[n]
                    dve.wait_ge(silu_done, 8 * g + n + 1)
                    dve.tensor_tensor(squares[n], q_or_k, q_or_k, ALU.mult).then_inc(l2_sq, 1)

            def normalize_heads(g):
                for n in range(4):
                    q_or_k = (q_of[g % 2] + k_of[g % 2])[n]
                    dve.wait_ge(l2_rms, 5 * g + n + 1)
                    dve.scalar_tensor_tensor(out=q_or_k, in0=q_or_k, scalar=(float(P) ** -0.5 if n < 2 else 1.0),
                                             in1=squares[n], op0=ALU.mult, op1=ALU.mult).then_inc(qk_ready, 1)

            head_squares(0, range(4))
            normalize_heads(0)
            for g in range(GROUPS):
                ahead = g + 1 < GROUPS
                v_T = v_of[g % 2]
                if g == 0:
                    token_products()
                own.did(dve.tensor_copy(grp[:, 0, :].rearrange("p (t h) -> p t h", t=NT), R4(g_log)[:, :, 4 * g:4 * g + 4]))
                own.settle()
                dve.tensor_copy(grp[:, 1, :].rearrange("p (t h) -> p t h", t=NT), R4(beta)[:, :, 4 * g:4 * g + 4]).then_inc(grp_ready, 1)
                for h in range(HG):
                    dve.wait_ge(vt_done, 4 * g + h + 1)
                    b = R4(beta)[:, :, 4 * g + h:4 * g + h + 1].to_broadcast([P, NT, P])
                    dve.tensor_tensor(R2(v_T[:, h, :]), R2(psum[4 + h][:, :]), b, ALU.mult).then_inc(vb_ready, 1)
                for h in range(HG):
                    dve.wait_ge(decay_ready, 4 * g + h + 1)
                    dve.wait_ge(kk_ready, 4 * g + 4)
                    own.did(dve.tensor_tensor(QK_T[:, h, :], kq[:, h // 2, :], decay[:, h % 2, :], ALU.mult))
                    dve.tensor_tensor(A_T[:, h, :], kk[:, h // 2, :], decay[:, h % 2, :], ALU.mult).then_inc(decay_used, 1)
                for h in range(HG):
                    dve.wait_ge(bb_done, 4 * g + h + 1)
                    dve.wait_ge(decay_used, 4 * g + h + 1)
                    own.did(dve.tensor_tensor(A_T[:, h, :], A_T[:, h, :], psum[4 + h][:, :], ALU.mult))
                    own.settle()
                    own.did(dve.tensor_tensor(R2(Y_T[:, h, :]), R2(A_T[:, h, :]), masks[:, 3:4, :].to_broadcast([P, NT, P]), ALU.mult))
                    own.settle()
                    dve.tensor_tensor(R2(Y_T[:, h, :]), R2(Y_T[:, h, :]), masks[:, 0:1, :].to_broadcast([P, NT, P]),
                                      ALU.add).then_inc(y_start, 1)
                for pair in range(2):
                    for lv in range(5):
                        n0 = 20 * g + 10 * pair + 2 * lv
                        for j in range(2):
                            h = 2 * pair + j
                            dve.wait_ge(py_done, n0 + j + 1)
                            dve.tensor_tensor(Y_T[:, h, :], Y_T[:, h, :], psum[4 + h][:, :], ALU.add).then_inc(y_ready, 1)
                for h in range(HG):
                    dve.memset(state[:, h, :], 0.0).then_inc(state_ready, 1)
                if ahead:
                    dve.wait_ge(h_ready, 8)
                for c in range(8):
                    rows, t = halves(c)
                    n0 = 32 * g + 4 * c
                    end = (end0, end1)[c % 2]
                    written = []
                    for h in range(HG + 1):
                        if h < HG:
                            col = 16 * t + 4 * g + h
                            dve.wait_ge(ks_done, n0 + h + 1)
                            written.append(own.did(dve.scalar_tensor_tensor(
                                out=resid[rows, h, :], in0=psum[4 + h][rows, 0:P], scalar=neg_bG[rows, col:col + 1],
                                in1=v_T[rows, h, t * P:(t + 1) * P], op0=ALU.mult, op1=ALU.add)))
                        if h:
                            col = 16 * t + 4 * g + h - 1
                            dve.wait_ge(dve_step, written[h - 1])
                            dve.tensor_scalar(v_T[rows, h - 1, t * P:(t + 1) * P], psum[3 + h][rows, P:2 * P],
                                              e_G[rows, col:col + 1], None, ALU.mult).then_inc(resid_ready, 1)
                    for h in range(HG):
                        col = 16 * t + 4 * g + h
                        dve.wait_ge(su_done, n0 + h + 1)
                        dve.scalar_tensor_tensor(out=state[:, h, :], in0=state[:, h, :], scalar=end[:, col:col + 1],
                                                 in1=psum[4 + h][:, P:2 * P], op0=ALU.mult, op1=ALU.add).then_inc(state_ready, 1)
                        dve.wait_ge(resid_ready, n0 + h + 1)
                        dve.tensor_tensor(v_T[rows, h, t * P:(t + 1) * P], v_T[rows, h, t * P:(t + 1) * P],
                                          psum[4 + h][rows, 2 * P:3 * P], ALU.add).then_inc(scan_done, 1)
                    if ahead and c:
                        convolved(g + 1, c - 1)
                    if ahead and c >= 6:
                        head_squares(g + 1, (0, 1) if c == 6 else (2, 3))
                if ahead:
                    convolved(g + 1, 7)
                dve.wait_ge(l2_rms, 5 * g + 5)
                for h in range(HG):
                    r = ssq[:, 1, 4 * h:4 * h + 4].unsqueeze(2).to_broadcast([P, NT, P])
                    dve.tensor_tensor(R2(v_T[:, h, :]), R2(v_T[:, h, :]), r, ALU.mult).then_inc(ssq_ready, 1)
                if ahead:
                    normalize_heads(g + 1)
                dve.wait_ge(chunk_out, 16 * g + 16)
                for h in range(HG):
                    dve.wait_ge(ot_done, 4 * g + h + 1)
                    dve.scalar_tensor_tensor(out=gate_out[:, 4 * g + h, :], in0=psum[4 + h][:, :], scalar=GNW,
                                             in1=z_T[:, h, :], op0=ALU.mult, op1=ALU.mult).then_inc(gate_ready, 1)
            post_norm()
            dve.wait_ge(split_ready, plan[SC0 - 1]["splits"])
            split_lo(SC0)
            split_lo(SC0 + 1)
            pre_norm()
            sc_base = plan[SC0 - 1]["end"]
            dve.sem_inc(sc_used, 1)

            def sc_tiles(i, last):
                for m in (2, 3):
                    split_lo(SC0 + m, plan[SC0 + m]["splits"] + 4 * i)
                for s in range(2):
                    u, b, c, z = [sc_in[:, 2 * m + s, :] for m in range(4)]
                    dve.wait_ge(chunk_out, sc_base + 8 * i + 5 + s)
                    own.did(dve.tensor_tensor(u, u, c, ALU.mult))
                    own.settle()
                    own.did(conv(sc_conv[:, s, :], u, 3, lambda tap: SCONV(tap, 2 * i + s)))
                    own.settle()
                    own.did(dve.tensor_tensor(sc_conv[:, s, :], sc_conv[:, s, :], b, ALU.mult))
                    own.settle()
                if not last:
                    split_lo(SC0 + 4, plan[SC0 + 4]["splits"] + 4 * i)
                for s in range(2):
                    dve.wait_ge(chunk_out, sc_base + 8 * i + 7 + s)
                    own.did(dve.tensor_tensor(sc_out[:, 2 * i + s, :], sc_conv[:, s, :], sc_in[:, 6 + s, :], ALU.mult))
                    own.settle()
                    dve.sem_inc(sc_used, 1)
                if not last:
                    split_lo(SC0 + 5, plan[SC0 + 5]["splits"] + 4 * i)

            for i in passes(dve, SC // 256 - 1):
                own.enter(i, 12)
                sc_tiles(i, False)
                own.leave(SC // 256 - 1)
            sc_tiles(SC // 256 - 1, True)
            post_norm()
            split_lo(MIX0)
            split_lo(MIX0 + 1)
            pre_norm()
            m0 = plan[MIX0 - 1]["end"]
            dve.wait_ge(ws_hi_ready, 2)
            dve.tensor_tensor(ws_lo[:, :, 0:24], w_gate, ws_hi[:, :, 0:24].bitcast(F32), ALU.subtract).then_inc(ws_ready, 1)
            for n in range(2, 8):
                split_lo(MIX0 + n)
            dve.wait_ge(gate_exp, 1)
            own.did(dve.tensor_scalar(gate, gate, 1.0, None, ALU.add))
            own.settle()
            dve.reciprocal(gate, gate).then_inc(gates_ready, 1)
            dve.wait_ge(turn_done, 2)
            dve.tensor_tensor(spatial_T, psum[5][:, :].rearrange("p (h t) -> p h t", h=4),
                              masks[:, 13:14, :].to_broadcast([P, 4, P]), ALU.mult).then_inc(mask_done, 1)
            blk = blocks.rearrange("p (l c) -> p l c", c=NC)
            dve.wait_ge(turn_out, 1)
            for kind in range(2):
                if kind:
                    dve.wait_ge(hid_done, 1)
                s_ = cmp_kv[:, kind, :]
                over = bass.AP(tensor=s_.tensor, offset=s_.offset, ap=[list(s_.ap[0]), [1, 32], [16, NC]])
                dve.tensor_tensor(blk, over, pos_T[:, 32 * kind:32 * kind + 32].unsqueeze(2).to_broadcast([P, 32, NC]), ALU.add)\
                    .then_inc(blocks_ready, 1)
            dve.wait_ge(chunk_out, m0 + 28)
            dve.wait_ge(turn_out, 5)
            mean, var = small[:, 1:5], small[:, 5:9]
            bc = lambda v: v.unsqueeze(2).to_broadcast([P, NT, 256])
            own.did(dve.tensor_reduce(mean, sgu_v, AX.X, ALU.add))
            own.settle()
            own.did(dve.tensor_scalar(mean, mean, 1.0 / 256, None, ALU.mult))
            own.settle()
            own.did(dve.tensor_tensor(sgu_v, sgu_v, bc(mean), ALU.subtract))
            own.settle()
            own.did(dve.tensor_tensor(sgu_t, sgu_v, sgu_v, ALU.mult))
            own.settle()
            dve.tensor_reduce(var, sgu_t, AX.X, ALU.add).then_inc(var_ready, 1)
            dve.wait_ge(rstd_ready, 1)
            own.did(dve.tensor_tensor(sgu_v, sgu_v, bc(var), ALU.mult))
            own.settle()
            own.did(dve.tensor_tensor(sgu_v, sgu_v, sgu_gb[:, 0:1, :].to_broadcast([P, NT, 256]), ALU.mult))
            own.settle()
            dve.tensor_tensor(sgu_v, sgu_v, sgu_gb[:, 1:2, :].to_broadcast([P, NT, 256]), ALU.add).then_inc(sgu_norm, 1)
            dve.wait_ge(turn_out, 5)
            src, dst = pool_x, pool_b
            for shift, r0, c0 in ((1, 0, 0), (2, 64, 0), (4, 0, 1), (8, 64, 1)):
                parts = {(0, 0): [(0, P, 0, 2)], (64, 0): [(64, P, 0, 1), (0, P, 1, 2)], (0, 1): [(0, P, 1, 2)],
                         (64, 1): [(64, P, 1, 2)]}[(r0, c0)]
                for a, b, ca, cb in parts:
                    own.did(dve.tensor_copy(dst[a:b, ca:cb, 0:shift], src[a:b, ca:cb, 0:shift]))
                    own.did(dve.tensor_tensor(dst[a:b, ca:cb, shift:S], src[a:b, ca:cb, shift:S], src[a:b, ca:cb, 0:S - shift], ALU.add))
                own.settle()
                src, dst = dst, (pool_a if dst is pool_b else pool_b)
            dve.wait_ge(inv_in, 16)
            for g, (s_, win) in enumerate(((pool_b, 2), (pool_a, 4), (pool_b, 8), (pool_a, 16))):
                r, c = slice(64 * (g % 2), 64 * (g % 2) + 64), g // 2
                own.did(dve.tensor_tensor(pool_d[r, c, 0:16], s_[r, c, 0:16], inv_count[r, 16 * c:16 * c + 16], ALU.mult))
                own.did(dve.scalar_tensor_tensor(out=pool_d[r, c, 16:S], in0=s_[r, c, 16:S], scalar=1.0 / win, in1=pool_x[r, c, 16:S],
                                                 op0=ALU.mult, op1=ALU.subtract))
            own.settle()
            dve.tensor_tensor(pool_d[:, :, 0:16], pool_d[:, :, 0:16], pool_x[:, :, 0:16], ALU.subtract).then_inc(pool_ready, 1)
            dve.wait_ge(c2_done, 1)
            own.did(dve.tensor_scalar(cmp_k, psum[6][:, 0:NC], cols[:, 1, 53:54], None, ALU.add))
            dve.tensor_tensor(cmp_v[0:NC, :], psum[7][0:NC, 0:P], b_c2[0:NC].rearrange("p g d -> p (g d)"), ALU.add).then_inc(c2_ready, 1)
            dve.wait_ge(spatial_done, 1)
            dve.wait_ge(c2_ready, 1)
            for pair in range(2):
                tmp = sgu_t.rearrange("p (a n) t -> p a (n t)", a=2)[:, pair, :].rearrange("p (n t) -> p n t", n=NT)
                own.did(dve.tensor_tensor(tmp, psum[4 + pair][:, :].rearrange("p (n t) -> p n t", n=NT),
                                          sgu_bias[:, pair:pair + 1, :].to_broadcast([P, NT, P]), ALU.add))
                own.settle()
                dve.tensor_tensor(mix_T[:, 6 + pair, :].rearrange("p (n t) -> p n t", n=NT), tmp,
                                  sgu_u[:, pair, :].rearrange("p (n t) -> p n t", n=NT), ALU.mult).then_inc(sgu_done, 1)
            dve.wait_ge(sgu_done, 2)
            dve.wait_ge(bias_in, 32)
            dve.wait_ge(c2_ready, 1)

            def read_scores(n):
                qi, kind, h = units[n]
                dve.wait_ge(score_done, n + 1)
                if kind == 0:
                    if qi:
                        dve.wait_ge(probT_done, n - 16)
                    cb = bias_cmp[:, qi, :].rearrange("p (h c) -> p h c", h=ATT_H)
                    for g in range(2):
                        own.did(dve.tensor_tensor(cmp_prob[:, 4 * g:4 * g + 4, :],
                                                  psum[g][:, 0:P].rearrange("p (h c) -> p h c", h=4)[:, :, 0:NC],
                                                  cb[:, 4 * g:4 * g + 4, :], ALU.add))
                    own.settle()
                    own.did(dve.tensor_reduce(cmp_max, cmp_prob, AX.X, ALU.max))
                    own.settle()
                    own.did(dve.tensor_scalar(cmp_max, cmp_max, NEG / 10, None, ALU.max))
                    own.settle()
                    dve.tensor_tensor(cmp_prob, cmp_prob, cmp_max.unsqueeze(2).to_broadcast([P, ATT_H, NC]), ALU.subtract)\
                        .then_inc(score_read, 1)
                    return
                if n >= 4:
                    dve.wait_ge(probT_done, n - 3)
                w = P * (qi + 1)
                own.did(dve.tensor_tensor_reduce(prob[:, n % 4, 0:w], psum[n % 2][:, 0:w], bias_row[:, h, S - w:S], 1.0, -3.0e38,
                                                 ALU.add, ALU.max, neg_max(n)))
                own.settle()
                dve.tensor_scalar(neg_max(n), neg_max(n), -1.0, None, ALU.mult).then_inc(score_read, 1)

            def copy_probs(n):
                qi, kind, h = units[n]
                dve.wait_ge(probT_done, n + 1)
                need = n if is_cmp(n) or is_cmp(n - 1) else n - 1
                if need > 0:
                    dve.wait_ge(pv_done, need)
                if kind == 0:
                    s_ = sums(qi, 0)
                    if n >= 34:
                        dve.wait_ge(combined, qi - 1)
                    own.did(dve.tensor_reduce(s_, cmp_prob, AX.X, ALU.add))
                    own.did(dve.tensor_copy(prob_T[0:NC, 0, :], psum[2][0:NC, :]))
                    dve.tensor_copy(prob_T[0:NC, 1, :], psum[3][0:NC, :]).then_inc(probT_out, 1)
                    own.settle()
                    own.did(dve.tensor_scalar(s_, s_, 1.0, None, ALU.max))
                else:
                    dve.tensor_copy(prob_T[:, n % 2, 0:P * (qi + 1)], psum[2 + n % 2][:, 0:P * (qi + 1)]).then_inc(probT_out, 1)

            def combine(qi):
                last = 17 * qi + 16
                dve.wait_ge(prob_ready, last + 1)
                dve.wait_ge(gates_ready, 1)
                own.settle()
                for kind in range(3):
                    own.did(dve.reciprocal(sums(qi, kind), sums(qi, kind)))
                own.settle()
                g3 = gate[:, qi, :].rearrange("p (h x) -> p x h", x=3)
                for kind in range(3):
                    own.did(dve.tensor_tensor(g3[:, kind, :], g3[:, kind, :], sums(qi, kind), ALU.mult))
                own.settle()
                dve.wait_ge(pv_done, last + 1)
                if qi:
                    dve.wait_ge(attT_done, qi)
                for kind in range(3):
                    own.did(dve.tensor_tensor(att_o[:, min(kind, 1), :].rearrange("p (h d) -> p h d", h=ATT_H),
                                              psum[4 + kind][:, :].rearrange("p (h d) -> p h d", h=ATT_H),
                                              g3[:, kind, :].unsqueeze(2).to_broadcast([P, ATT_H, DH]), ALU.mult))
                    own.settle()
                    if kind == 1:
                        own.did(dve.tensor_tensor(att_o[:, 0, :], att_o[:, 0, :], att_o[:, 1, :], ALU.add))
                        own.settle()
                dve.tensor_tensor(att_o[:, 0, :], att_o[:, 0, :], att_o[:, 1, :], ALU.add).then_inc(combined, 1)

            for n in range(len(units) + 4):
                if n < len(units):
                    read_scores(n)
                if 0 <= n - 2 < len(units):
                    copy_probs(n - 2)
                if n >= 19 and (n - 19) % 17 == 0:
                    combine((n - 19) // 17)
            post_norm()
            dve.wait_ge(mem_rstd, 1)
            own.did(dve.tensor_scalar(mem_rows[:, 0, :], mem_rows[:, 0, :], small[:, 1:2], None, ALU.mult))
            dve.tensor_scalar(mem_rows[:, 1, :], mem_rows[:, 1, :], small[:, 2:3], None, ALU.mult).then_inc(mem_scaled, 1)
            split_lo(MEM0 + 8)
            split_lo(MEM0 + 9)
            pre_norm()
            split_lo(MEM0 + 10)
            split_lo(MEM0 + 11)
            for n in range(len(mem_units) + 1):
                if n < len(mem_units):
                    dve.wait_ge(ms_done, n + 1)
                    own.did(dve.tensor_reduce(mem_max(n), psum[4 + n % 2][:, 0:MEM], AX.X, ALU.max))
                    own.settle()
                    dve.tensor_scalar(mem_max(n), mem_max(n), -(HD ** -0.5), None, ALU.mult).then_inc(ms_max, 1)
                m = n - 1
                if m >= 0:
                    dve.wait_ge(mp_exp, m + 1)
                    own.did(dve.reciprocal(mem_sum(m), mem_sum(m)))
                    own.settle()
                    dve.tensor_scalar(mem_prob[:, m % 4, :], mem_prob[:, m % 4, :], mem_sum(m), None, ALU.mult).then_inc(mp_ready, 1)
            post_norm()
            split_lo(FF1)
            split_lo(FF1 + 1)
            pre_norm()
            dve.wait_ge(x_ready, 32)
            dve.sem_inc(ff_conv, 1)

            def pair_tiles(jj, last):
                for v in range(2):
                    for s in range(2):
                        c = 2 * jj + s + FK * v
                        dve.wait_ge(chunk_out, FF0 + 4 * jj + 2 * v + s + 1)
                        conv((ff_gate, ff_val)[v][:, s, :], ff_raw[:, 2 * v + s, :], 3, lambda tap: FCONV(tap, c), FBIAS(c))\
                            .then_inc(ff_conv, 1)
                    if not last:
                        split_lo(FF1 + v, plan[FF1 + 2 + v]["splits"] + 2 * jj)
                for s in range(2):
                    dve.wait_ge(ff_gelu, 2 * jj + s + 1)
                    dve.wait_ge(ff_conv, 4 * jj + 4 + s)
                    dve.tensor_tensor(ff_hid[:, 2 * jj + s, :], ff_gate[:, s, :], ff_val[:, s, :], ALU.mult).then_inc(ff_ready, 1)
                dve.wait_ge(ff_ready, 2 * jj + 2)

            for jj in passes(dve, FK // 2 - 1):
                own.enter(jj, 8)
                pair_tiles(jj, False)
                own.leave(FK // 2 - 1)
            pair_tiles(FK // 2 - 1, True)
            post_norm(ff_y)
            dve.wait_ge(chunk_done, FF0 + 52)
            for t in range(NT):
                dve.wait_ge(final_done, 2 * t + 2)
                dve.tensor_copy(out_rows_sb[:, t, 512:1024], psum[2 * t + 1][:, :]).then_inc(final_dve, 1)

        @block.gpsimd
        def _(pool):
            def split_lo(n):
                pool.wait_ge(w_hi_ready, plan[n]["splits"])
                pool.wait_ge(split_ready, plan[n]["splits"] - 1)
                pool.tensor_tensor(w_lo[:, n % 2, :], ring[:, n % 2, :], w_hi[:, n % 2, :].bitcast(F32), ALU.subtract)\
                    .then_inc(split_ready, 1)

            for g in range(GROUPS):
                for pair in range(2):
                    for lv in range(5):
                        n0 = 20 * g + 10 * pair + 2 * lv
                        for j in range(2):
                            h = 2 * pair + j
                            pool.wait_ge(y_start, 4 * g + h + 1)
                            pool.wait_ge(decay_used, 4 * g + 4)
                            if lv or pair:
                                pool.wait_ge(p_done, n0 + j - 1)
                            pool.tensor_tensor(R2(decay[:, j, :]), R2(A_T[:, h, :]),
                                               masks[:, 4 + lv:5 + lv, :].to_broadcast([P, NT, P]), ALU.mult)\
                                .then_inc(level_ready, 1)
                        if g + 1 < GROUPS and 5 * pair + lv == 1:
                            split_lo(6 * g + 6)
                if g + 1 < GROUPS:
                    for n in range(7, 12):
                        split_lo(6 * g + n)






_INS = ["x", "pre_norm_w", "post_norm_w", "gdn_w_in", "gdn_conv_w", "gdn_A_log", "gdn_dt_bias", "gdn_norm_w", "gdn_w_out",
        "sc_w_in", "sc_conv_w", "sc_w_out", "mem_2", "rel_bias_2", "mix_norm_pre_2", "mix_norm_post_2", "w_in_2",
        "cmp_pos_2", "cmp_w1_2", "cmp_b1_2", "cmp_w2_2", "cmp_b2_2", "pool_w_2", "pool_scale_2", "sgu_norm_g_2",
        "sgu_norm_b_2", "sgu_w_2", "sgu_b_2", "w_out_2", "mem_norm_pre_2", "mem_norm_kv_2", "mem_norm_post_2", "w_mq_2",
        "w_mk_2", "w_mv_2", "w_mo_2", "ffn_norm_pre_2", "ffn_norm_post_2", "w_up_2", "conv_w_2", "conv_b_2", "w_down_2"]


def kernel(**inputs):
    import concourse.bacc as _bacc
    from concourse.bass_utils import run_bass_kernel_spmd as _run

    nc = _bacc.Bacc("TRN2", target_bir_lowering=False, num_devices=1)
    arrays = {name: np.ascontiguousarray(inputs[name]) for name in _INS}
    arrays["masks_d"], arrays["hot_d"], arrays["inv_d"] = shape_constants()
    args = {name: nc.dram_tensor(f"in_{name}", a.shape, mybir.dt.from_np(a.dtype), kind="ExternalInput").ap()
            for name, a in arrays.items()}
    out = nc.dram_tensor("out_x", (1, S, D), mybir.dt.float32, kind="ExternalOutput").ap()
    build(nc, out=out, **args)
    r = _run(nc, [{f"in_{name}": a for name, a in arrays.items()}], core_ids=[0])
    return r.results[0]["out_x"]
```
